# Optimizing a Trainium2 kernel written in Bass

```python
import math
import jax, jax.numpy as jnp
from jax import lax
import numpy as np

D_MODEL = 1024
BATCH = 1
SEQ = 512
DEPTH = 2

GRID_W = 64
CTX_LEN = 256
HEAD_DIM = 64
N_HEADS_A = 8
N_KV_A = 2
N_HEADS_B = 8
N_HEADS_C = 8
N_KV_C = 2
MIX_WIDTH = HEAD_DIM * (N_HEADS_A + N_HEADS_B + N_HEADS_C)
Q_BLOCK = 128
NB_ROWS = 8
NB_COLS = 16
WINDOW = 128
ROPE_THETA = 10000.0
EPS = 1e-6
IN_SIZES = (
    N_HEADS_A * HEAD_DIM, N_KV_A * HEAD_DIM, N_KV_A * HEAD_DIM,
    N_HEADS_B * HEAD_DIM, N_HEADS_B * HEAD_DIM, N_HEADS_B * HEAD_DIM,
    N_HEADS_C * HEAD_DIM, N_KV_C * HEAD_DIM, N_KV_C * HEAD_DIM,
    MIX_WIDTH,
)
IN_WIDTH = sum(IN_SIZES)


def rmsnorm(x, w):
    xf = x.astype(jnp.float32)
    y = xf * lax.rsqrt(jnp.mean(xf * xf, axis=-1, keepdims=True) + EPS)
    return y.astype(x.dtype) * w

def softmax_f32(s, dtype):
    return jax.nn.softmax(s.astype(jnp.float32), axis=-1).astype(dtype)

def heads(z, h):
    return z.reshape(z.shape[:-1] + (h, HEAD_DIM))

def split_cols(z):
    outs, off = [], 0
    for sz in IN_SIZES:
        outs.append(z[..., off:off + sz])
        off += sz
    return outs

def axial_rope(n, dtype):
    t = jnp.arange(n, dtype=jnp.int32)
    rows = (t // GRID_W).astype(jnp.float32)
    cols = (t % GRID_W).astype(jnp.float32)
    n_freq = HEAD_DIM // 4
    freq = ROPE_THETA ** (-jnp.arange(n_freq, dtype=jnp.float32) / n_freq)
    ang = jnp.concatenate([rows[:, None] * freq, cols[:, None] * freq], axis=-1)
    return jnp.cos(ang).astype(dtype), jnp.sin(ang).astype(dtype)

def apply_rope(x, cos, sin):
    x1, x2 = jnp.split(x, 2, axis=-1)
    c = cos[None, :, None, :]
    s = sin[None, :, None, :]
    return jnp.concatenate([x1 * c - x2 * s, x1 * s + x2 * c], axis=-1)

def global_gqa(q, k, v, qc, kc, vc, cos, sin, qn, kn, need_ctx):
    B, N = q.shape[0], q.shape[1]
    C = qc.shape[1]
    G = N_HEADS_A // N_KV_A
    scale = HEAD_DIM ** -0.5
    q = apply_rope(rmsnorm(heads(q, N_HEADS_A), qn), cos, sin) * scale
    k = apply_rope(rmsnorm(heads(k, N_KV_A), kn), cos, sin)
    v = heads(v, N_KV_A)
    qc = rmsnorm(heads(qc, N_HEADS_A), qn) * scale
    kc = rmsnorm(heads(kc, N_KV_A), kn)
    vc = heads(vc, N_KV_A)
    k_all = jnp.concatenate([k, kc], axis=1)
    v_all = jnp.concatenate([v, vc], axis=1)
    nblk = N // Q_BLOCK
    qb = q.reshape(B, nblk, Q_BLOCK, N_KV_A, G, HEAD_DIM).transpose(1, 0, 2, 3, 4, 5)

    def block(qi):
        s = jnp.einsum('bqhgd,bkhd->bhgqk', qi, k_all)
        p = softmax_f32(s, v_all.dtype)
        return jnp.einsum('bhgqk,bkhd->bqhgd', p, v_all)

    y = lax.map(block, qb).transpose(1, 0, 2, 3, 4, 5).reshape(B, N, N_HEADS_A * HEAD_DIM)
    yc = None
    if need_ctx:
        qcg = qc.reshape(B, C, N_KV_A, G, HEAD_DIM)
        p = softmax_f32(jnp.einsum('bqhgd,bkhd->bhgqk', qcg, kc), vc.dtype)
        yc = jnp.einsum('bhgqk,bkhd->bqhgd', p, vc).reshape(B, C, N_HEADS_A * HEAD_DIM)
    return y, yc

def neighbourhood_attn(q, k, v, qc, kc, vc, rpb, need_ctx):
    B, N = q.shape[0], q.shape[1]
    C = qc.shape[1]
    H = N_HEADS_B
    scale = HEAD_DIM ** -0.5
    rows = N // GRID_W
    kh = min(NB_ROWS, rows)
    kw = NB_COLS
    t = jnp.arange(N, dtype=jnp.int32)
    r = t // GRID_W
    col = t % GRID_W
    rs = jnp.clip(r - kh // 2, 0, rows - kh)
    cs = jnp.clip(col - kw // 2, 0, GRID_W - kw)
    key_r = rs[:, None, None] + jnp.arange(kh, dtype=jnp.int32)[None, :, None]
    key_c = cs[:, None, None] + jnp.arange(kw, dtype=jnp.int32)[None, None, :]
    idx = (key_r * GRID_W + key_c).reshape(N, kh * kw)
    rel = ((key_r - r[:, None, None] + NB_ROWS - 1) * (2 * NB_COLS - 1)
           + (key_c - col[:, None, None] + NB_COLS - 1)).reshape(N, kh * kw)
    rpb_flat = rpb.reshape(H, -1)
    q = heads(q, H) * scale
    k = heads(k, H)
    v = heads(v, H)
    qc = heads(qc, H) * scale
    kc = heads(kc, H)
    vc = heads(vc, H)
    nblk = N // Q_BLOCK
    kn = kh * kw
    xs = (q.reshape(B, nblk, Q_BLOCK, H, HEAD_DIM).transpose(1, 0, 2, 3, 4),
          idx.reshape(nblk, Q_BLOCK, kn), rel.reshape(nblk, Q_BLOCK, kn))

    def block(args):
        qi, ii, ri = args
        kg = jnp.take(k, ii, axis=1)
        vg = jnp.take(v, ii, axis=1)
        s_nb = jnp.einsum('bqhd,bqkhd->bhqk', qi, kg) + jnp.take(rpb_flat, ri, axis=1)[None]
        s_ctx = jnp.einsum('bqhd,bchd->bhqc', qi, kc)
        p = softmax_f32(jnp.concatenate([s_nb, s_ctx], axis=-1), v.dtype)
        return (jnp.einsum('bhqk,bqkhd->bqhd', p[..., :kn], vg)
                + jnp.einsum('bhqc,bchd->bqhd', p[..., kn:], vc))

    y = lax.map(block, xs).transpose(1, 0, 2, 3, 4).reshape(B, N, H * HEAD_DIM)
    yc = None
    if need_ctx:
        p = softmax_f32(jnp.einsum('bqhd,bchd->bhqc', qc, kc), vc.dtype)
        yc = jnp.einsum('bhqc,bchd->bqhd', p, vc).reshape(B, C, H * HEAD_DIM)
    return y, yc

def window_gqa(q, k, v, qc, kc, vc, cos, sin, sink, need_ctx):
    B, N = q.shape[0], q.shape[1]
    C = qc.shape[1]
    G = N_HEADS_C // N_KV_C
    scale = HEAD_DIM ** -0.5
    q = (apply_rope(heads(q, N_HEADS_C), cos, sin) * scale).reshape(B, N, N_KV_C, G, HEAD_DIM)
    k = apply_rope(heads(k, N_KV_C), cos, sin)
    v = heads(v, N_KV_C)
    qc = (heads(qc, N_HEADS_C) * scale).reshape(B, C, N_KV_C, G, HEAD_DIM)
    kc = heads(kc, N_KV_C)
    vc = heads(vc, N_KV_C)
    pad = ((0, 0), (WINDOW, WINDOW), (0, 0), (0, 0))
    kp = jnp.pad(k, pad)
    vp = jnp.pad(v, pad)
    span = Q_BLOCK + 2 * WINDOW
    sink_l = sink.astype(jnp.float32).reshape(N_KV_C, G)
    neg = jnp.finfo(jnp.float32).min
    nblk = N // Q_BLOCK
    qs = q.reshape(B, nblk, Q_BLOCK, N_KV_C, G, HEAD_DIM).transpose(1, 0, 2, 3, 4, 5)

    def block(args):
        i, qi = args
        start = i * Q_BLOCK
        kb = lax.dynamic_slice_in_dim(kp, start, span, axis=1)
        vb = lax.dynamic_slice_in_dim(vp, start, span, axis=1)
        qpos = start + jnp.arange(Q_BLOCK, dtype=jnp.int32)
        kpos = start - WINDOW + jnp.arange(span, dtype=jnp.int32)
        valid = (jnp.abs(qpos[:, None] - kpos[None, :]) <= WINDOW) & (kpos >= 0)[None, :] & (kpos < N)[None, :]
        s = jnp.where(valid, jnp.einsum('bqhgd,bkhd->bhgqk', qi, kb).astype(jnp.float32), neg)
        s_ctx = jnp.einsum('bqhgd,bkhd->bhgqk', qi, kc).astype(jnp.float32)
        s_sink = jnp.broadcast_to(sink_l[None, :, :, None, None], s.shape[:-1] + (1,))
        p = softmax_f32(jnp.concatenate([s, s_ctx, s_sink], axis=-1), v.dtype)
        return (jnp.einsum('bhgqk,bkhd->bqhgd', p[..., :span], vb)
                + jnp.einsum('bhgqk,bkhd->bqhgd', p[..., span:span + C], vc))

    y = lax.map(block, (jnp.arange(nblk, dtype=jnp.int32), qs))
    y = y.transpose(1, 0, 2, 3, 4, 5).reshape(B, N, N_HEADS_C * HEAD_DIM)
    yc = None
    if need_ctx:
        s = jnp.einsum('bqhgd,bkhd->bhgqk', qc, kc).astype(jnp.float32)
        s_sink = jnp.broadcast_to(sink_l[None, :, :, None, None], s.shape[:-1] + (1,))
        p = softmax_f32(jnp.concatenate([s, s_sink], axis=-1), vc.dtype)
        yc = jnp.einsum('bhgqk,bkhd->bqhgd', p[..., :C], vc).reshape(B, C, N_HEADS_C * HEAD_DIM)
    return y, yc

def layer(x, cx, c_silu, cctx_silu, norm_w, ada_w, ada_b, w_in, w_out, qn, kn, rpb, sink, cos, sin, need_ctx):
    mod = c_silu @ ada_w + ada_b
    mod_c = cctx_silu @ ada_w + ada_b
    shift, scale, gate = jnp.split(mod, 3, axis=-1)
    shift_c, scale_c, gate_c = jnp.split(mod_c, 3, axis=-1)
    hx = rmsnorm(x, norm_w) * (1 + scale[:, None, :]) + shift[:, None, :]
    hc = rmsnorm(cx, norm_w) * (1 + scale_c) + shift_c
    px = split_cols(hx @ w_in)
    pc = split_cols(hc @ w_in)
    ya, yca = global_gqa(px[0], px[1], px[2], pc[0], pc[1], pc[2], cos, sin, qn, kn, need_ctx)
    yb, ycb = neighbourhood_attn(px[3], px[4], px[5], pc[3], pc[4], pc[5], rpb, need_ctx)
    yc_, ycc = window_gqa(px[6], px[7], px[8], pc[6], pc[7], pc[8], cos, sin, sink, need_ctx)
    ux = jnp.concatenate([ya, yb, yc_], axis=-1) * jax.nn.silu(px[9])
    x = x + gate[:, None, :] * (ux @ w_out)
    if need_ctx:
        uc = jnp.concatenate([yca, ycb, ycc], axis=-1) * jax.nn.silu(pc[9])
        cx = cx + gate_c * (uc @ w_out)
    return x, cx

def first_inputs(seed: int = 0) -> dict:
    key = jax.random.key(seed)
    ks = jax.random.split(key, 14)
    f32 = jnp.float32
    n_rel = (2 * NB_ROWS - 1, 2 * NB_COLS - 1)
    return {
        "x": jax.random.normal(ks[0], (BATCH, SEQ, D_MODEL), f32),
        "c": jax.random.normal(ks[1], (BATCH, D_MODEL), f32),
        "ctx": jax.random.normal(ks[2], (BATCH, CTX_LEN, D_MODEL), f32),
        "c_ctx": jax.random.normal(ks[3], (D_MODEL,), f32),
        "norm_w": 1.0 + 0.05 * jax.random.normal(ks[4], (DEPTH, D_MODEL), f32),
        "ada_w": jax.random.normal(ks[5], (DEPTH, D_MODEL, 3 * D_MODEL), f32) * D_MODEL ** -0.5,
        "ada_b": 0.02 * jax.random.normal(ks[6], (DEPTH, 3 * D_MODEL), f32),
        "w_in": jax.random.normal(ks[7], (DEPTH, D_MODEL, IN_WIDTH), f32) * D_MODEL ** -0.5,
        "w_out": jax.random.normal(ks[8], (DEPTH, MIX_WIDTH, D_MODEL), f32) * MIX_WIDTH ** -0.5,
        "q_norm_a": 1.0 + 0.05 * jax.random.normal(ks[9], (DEPTH, HEAD_DIM), f32),
        "k_norm_a": 1.0 + 0.05 * jax.random.normal(ks[10], (DEPTH, HEAD_DIM), f32),
        "rpb_b": 0.1 * jax.random.normal(ks[11], (DEPTH, N_HEADS_B) + n_rel, f32),
        "sink_c": 0.5 * jax.random.normal(ks[12], (DEPTH, N_HEADS_C), f32),
        "final_norm_w": 1.0 + 0.05 * jax.random.normal(ks[13], (D_MODEL,), f32),
    }

def first_block(x, c, ctx, c_ctx, norm_w, ada_w, ada_b, w_in, w_out, q_norm_a, k_norm_a, rpb_b, sink_c, final_norm_w):
    n_tok = x.shape[1]
    cos, sin = axial_rope(n_tok, x.dtype)
    c_silu = jax.nn.silu(c)
    cctx_silu = jax.nn.silu(c_ctx)
    cx = ctx
    for l in range(DEPTH):
        x, cx = layer(x, cx, c_silu, cctx_silu, norm_w[l], ada_w[l], ada_b[l], w_in[l], w_out[l],
                      q_norm_a[l], k_norm_a[l], rpb_b[l], sink_c[l], cos, sin, l < DEPTH - 1)
    return rmsnorm(x, final_norm_w)


N_MIXERS = 4
GROUP_WIDTH = D_MODEL // N_MIXERS
FOX_HEADS = GROUP_WIDTH // HEAD_DIM
RET_HEADS = GROUP_WIDTH // HEAD_DIM
POOL_WINDOWS = (2, 4, 8, 16)
POOL_GROUPS = len(POOL_WINDOWS)
POOL_GROUP_DIM = GROUP_WIDTH // POOL_GROUPS
CONV_WIDTH = 31
CONV_CH = GROUP_WIDTH
N_IN = 3 * GROUP_WIDTH + FOX_HEADS + GROUP_WIDTH + 4 * GROUP_WIDTH + 2 * CONV_CH
D_FF = ((8 * D_MODEL + 3 * 256 - 1) // (3 * 256)) * 256
RET_CHUNK = 128
ROPE_BASE = 10000.0


def rmsnorm_2(x, g):
    xf = x.astype(jnp.float32)
    y = xf * lax.rsqrt(jnp.mean(xf * xf, axis=-1, keepdims=True) + EPS)
    return (y * g.astype(jnp.float32)).astype(x.dtype)

def layernorm(x, g, b):
    xf = x.astype(jnp.float32)
    mu = jnp.mean(xf, axis=-1, keepdims=True)
    var = jnp.mean(jnp.square(xf - mu), axis=-1, keepdims=True)
    y = (xf - mu) * lax.rsqrt(var + EPS)
    return (y * g.astype(jnp.float32) + b.astype(jnp.float32)).astype(x.dtype)

def rope(x, positions):
    half = x.shape[-1] // 2
    inv = ROPE_BASE ** (-jnp.arange(half, dtype=jnp.float32) / half)
    ang = positions.astype(jnp.float32)[..., None] * inv
    cos = jnp.cos(ang)[:, :, None, :]
    sin = jnp.sin(ang)[:, :, None, :]
    x1, x2 = x[..., :half], x[..., half:]
    return jnp.concatenate([x1 * cos - x2 * sin, x1 * sin + x2 * cos], axis=-1).astype(x.dtype)

def fox_attention(q, k, v, f_logit, f_bias):
    B, S, H, Dh = q.shape
    log_f = jax.nn.log_sigmoid((f_logit + f_bias).astype(jnp.float32))
    cum = jnp.cumsum(log_f, axis=1).transpose(0, 2, 1)
    key_pos = jnp.arange(S)
    scale = Dh ** -0.5

    def block(i):
        start = i * Q_BLOCK
        qb = lax.dynamic_slice_in_dim(q, start, Q_BLOCK, axis=1)
        cq = lax.dynamic_slice_in_dim(cum, start, Q_BLOCK, axis=2)
        s = jnp.einsum('bqhd,bkhd->bhqk', qb, k).astype(jnp.float32) * scale
        s = s + cq[..., :, None] - cum[:, :, None, :]
        q_pos = start + jnp.arange(Q_BLOCK)
        causal = key_pos[None, :] <= q_pos[:, None]
        s = jnp.where(causal, s, -jnp.inf)
        p = jax.nn.softmax(s, axis=-1).astype(v.dtype)
        return jnp.einsum('bhqk,bkhd->bqhd', p, v)

    out = lax.map(block, jnp.arange(S // Q_BLOCK))
    return out.transpose(1, 0, 2, 3, 4).reshape(B, S, H * Dh)

def pool_mixer(u, pool_w, pool_scale):
    B, S, _ = u.shape
    ug = u.reshape(B, S, POOL_GROUPS, POOL_GROUP_DIM)
    cs = jnp.cumsum(ug.astype(jnp.float32), axis=1)
    pos = jnp.arange(S)
    means = []
    for gi, w in enumerate(POOL_WINDOWS):
        c_g = cs[:, :, gi]
        shifted = jnp.pad(c_g, ((0, 0), (w, 0), (0, 0)))[:, :S]
        count = jnp.minimum(pos + 1, w).astype(jnp.float32)[None, :, None]
        means.append((c_g - shifted) / count)
    pooled = jnp.stack(means, axis=2)
    delta = (pooled - ug.astype(jnp.float32)).astype(u.dtype)
    mixed = jnp.einsum('bsgc,gcd->bsgd', delta, pool_w).reshape(B, S, GROUP_WIDTH)
    return mixed * pool_scale

def retention(q, k, v, g, positions, gn_g):
    B, S, H, Dh = q.shape
    q = rope(q, positions)
    k = rope(k, positions) * (Dh ** -0.5)
    log_gamma = jnp.log(1.0 - 2.0 ** (-5.0 - jnp.arange(H, dtype=jnp.float32)))
    C = RET_CHUNK
    NC = S // C
    idx = jnp.arange(C, dtype=jnp.float32)
    diff = idx[:, None] - idx[None, :]
    dmask = jnp.where(diff >= 0, jnp.exp(log_gamma[:, None, None] * jnp.maximum(diff, 0.0)), 0.0)
    zeta = jnp.exp(log_gamma[:, None] * (C - 1 - idx))
    xi = jnp.exp(log_gamma[:, None] * (idx + 1))
    chunk_decay = jnp.exp(log_gamma * C)

    qc = q.reshape(B, NC, C, H, Dh)
    kc = k.reshape(B, NC, C, H, Dh)
    vc = v.reshape(B, NC, C, H, Dh)
    intra_s = jnp.einsum('bnqhd,bnkhd->bnhqk', qc, kc) * dmask
    intra = jnp.einsum('bnhqk,bnkhe->bnqhe', intra_s, vc)
    kv = jnp.einsum('bnkhd,hk,bnkhe->bnhde', kc, zeta, vc)

    def step(state, xs):
        q_n, kv_n = xs
        cross = jnp.einsum('bqhd,bhde->bqhe', q_n, state)
        new = (state * chunk_decay[None, :, None, None] + kv_n).astype(state.dtype)
        return new, cross

    state0 = jnp.zeros((B, H, Dh, Dh), dtype=kv.dtype)
    _, cross = lax.scan(step, state0, (qc.transpose(1, 0, 2, 3, 4), kv.transpose(1, 0, 2, 3, 4)))
    cross = cross.transpose(1, 0, 2, 3, 4) * xi.T[None, None, :, :, None]
    o = (intra + cross).reshape(B, S, H, Dh).astype(jnp.float32)
    mu = jnp.mean(o, axis=-1, keepdims=True)
    var = jnp.mean(jnp.square(o - mu), axis=-1, keepdims=True)
    o = (o - mu) * lax.rsqrt(var + EPS) * gn_g.reshape(H, Dh).astype(jnp.float32)
    o = o.reshape(B, S, H * Dh).astype(g.dtype)
    return jax.nn.silu(g) * o

def conformer_conv(u, conv_w, conv_b, ln_g, ln_b):
    a, gate = jnp.split(u, 2, axis=-1)
    h = a * jax.nn.sigmoid(gate)
    h = lax.conv_general_dilated(
        h, conv_w[:, None, :], window_strides=(1,), padding=[(CONV_WIDTH - 1, 0)],
        dimension_numbers=('NWC', 'WIO', 'NWC'), feature_group_count=CONV_CH) + conv_b
    return jax.nn.silu(layernorm(h, ln_g, ln_b))

def second_inputs(seed: int = 0) -> dict:
    key = jax.random.key(seed)
    ks = jax.random.split(key, 24)
    f32 = jnp.float32
    D, G = D_MODEL, GROUP_WIDTH
    nrm = lambda k, shape, s: jax.random.normal(k, shape, f32) * s
    return {
        "x": jax.random.normal(ks[0], (BATCH, SEQ, D), f32),
        "c": jax.random.normal(ks[1], (BATCH, D), f32),
        "positions": jnp.broadcast_to(jnp.arange(SEQ, dtype=jnp.int32)[None, :], (BATCH, SEQ)),
        "ada_w": nrm(ks[2], (DEPTH, D, 6 * D), 0.5 * D ** -0.5),
        "ada_b": nrm(ks[3], (DEPTH, 6 * D), 0.01),
        "norm_mix_g": 1.0 + nrm(ks[4], (DEPTH, D), 0.1),
        "norm_ffn_g": 1.0 + nrm(ks[5], (DEPTH, D), 0.1),
        "w_in": nrm(ks[6], (DEPTH, D, N_IN), D ** -0.5),
        "fox_fb": jax.random.uniform(ks[7], (DEPTH, FOX_HEADS), f32, 2.0, 5.0),
        "pool_w": nrm(ks[8], (DEPTH, POOL_GROUPS, POOL_GROUP_DIM, POOL_GROUP_DIM), POOL_GROUP_DIM ** -0.5),
        "pool_scale": 1.0 + nrm(ks[9], (DEPTH, G), 0.1),
        "ret_gn_g": 1.0 + nrm(ks[10], (DEPTH, G), 0.1),
        "conv_w": nrm(ks[11], (DEPTH, CONV_WIDTH, CONV_CH), CONV_WIDTH ** -0.5),
        "conv_b": nrm(ks[12], (DEPTH, CONV_CH), 0.01),
        "conv_ln_g": 1.0 + nrm(ks[13], (DEPTH, CONV_CH), 0.1),
        "conv_ln_b": nrm(ks[14], (DEPTH, CONV_CH), 0.01),
        "w_out": nrm(ks[15], (DEPTH, D, D), D ** -0.5),
        "ffn_w1": nrm(ks[16], (DEPTH, D, D_FF), D ** -0.5),
        "ffn_w3": nrm(ks[17], (DEPTH, D, D_FF), D ** -0.5),
        "ffn_w2": nrm(ks[18], (DEPTH, D_FF, D), D_FF ** -0.5),
        "final_g": 1.0 + nrm(ks[19], (D,), 0.1),
    }

def second_block(x, c, positions, ada_w, ada_b, norm_mix_g, norm_ffn_g, w_in, fox_fb,
              pool_w, pool_scale, ret_gn_g, conv_w, conv_b, conv_ln_g, conv_ln_b,
              w_out, ffn_w1, ffn_w3, ffn_w2, final_g):
    B, S, _ = x.shape
    G, H, Dh = GROUP_WIDTH, FOX_HEADS, HEAD_DIM
    bounds = [G, 2 * G, 3 * G, 3 * G + H,
              4 * G + H,
              5 * G + H, 6 * G + H, 7 * G + H, 8 * G + H]
    c_act = jax.nn.silu(c)
    for l in range(DEPTH):
        mod = (c_act @ ada_w[l] + ada_b[l])[:, None, :]
        sh1, sc1, g1, sh2, sc2, g2 = jnp.split(mod, 6, axis=-1)

        h = rmsnorm_2(x, norm_mix_g[l]) * (1.0 + sc1) + sh1
        u = h @ w_in[l]
        fq, fk, fv, ff, pu, rq, rk, rv, rg, cu = jnp.split(u, bounds, axis=-1)
        y_fox = fox_attention(fq.reshape(B, S, H, Dh), fk.reshape(B, S, H, Dh),
                              fv.reshape(B, S, H, Dh), ff, fox_fb[l])
        y_pool = pool_mixer(pu, pool_w[l], pool_scale[l])
        y_ret = retention(rq.reshape(B, S, RET_HEADS, Dh), rk.reshape(B, S, RET_HEADS, Dh),
                          rv.reshape(B, S, RET_HEADS, Dh), rg, positions, ret_gn_g[l])
        y_conv = conformer_conv(cu, conv_w[l], conv_b[l], conv_ln_g[l], conv_ln_b[l])
        mix = jnp.concatenate([y_fox, y_pool, y_ret, y_conv], axis=-1)
        x = x + g1 * (mix @ w_out[l])

        h = rmsnorm_2(x, norm_ffn_g[l]) * (1.0 + sc2) + sh2
        f = (jax.nn.silu(h @ ffn_w1[l]) * (h @ ffn_w3[l])) @ ffn_w2[l]
        x = x + g2 * f
    return rmsnorm_2(x, final_g)


def setup_inputs(seed=0):
    out = dict(first_inputs(seed))
    for name, value in second_inputs(seed + 1).items():
        if name != "x":
            out[name + "_2"] = value
    return out


def reference(
    x, c, ctx, c_ctx, norm_w, ada_w, ada_b, w_in, w_out, q_norm_a, k_norm_a, rpb_b, sink_c,
    final_norm_w, c_2, positions_2, ada_w_2, ada_b_2, norm_mix_g_2, norm_ffn_g_2, w_in_2,
    fox_fb_2, pool_w_2, pool_scale_2, ret_gn_g_2, conv_w_2, conv_b_2, conv_ln_g_2, conv_ln_b_2,
    w_out_2, ffn_w1_2, ffn_w3_2, ffn_w2_2, final_g_2,
):
    x = first_block(
        x, c, ctx, c_ctx, norm_w, ada_w, ada_b, w_in, w_out, q_norm_a, k_norm_a, rpb_b, sink_c,
        final_norm_w,
    )
    return second_block(
        x, c_2, positions_2, ada_w_2, ada_b_2, norm_mix_g_2, norm_ffn_g_2, w_in_2, fox_fb_2,
        pool_w_2, pool_scale_2, ret_gn_g_2, conv_w_2, conv_b_2, conv_ln_g_2, conv_ln_b_2,
        w_out_2, ffn_w1_2, ffn_w3_2, ffn_w2_2, final_g_2,
    )


_drawn_inputs = setup_inputs


def setup_inputs(seed=0):
    import zlib

    import numpy as np

    out = dict(_drawn_inputs(seed))
    spreads = {}
    factors = {'q_norm_a': 8.0,
     'k_norm_a': 8.0,
     'rpb_b': 8.0,
     'sink_c': 8.0,
     'ada_b_2': 3.603,
     'fox_fb_2': 27.584,
     'pool_scale_2': 3.277,
     'ret_gn_g_2': 3.839,
     'conv_b_2': 8.0,
     'conv_ln_g_2': 3.665,
     'conv_ln_b_2': 43.206}
    for name, (base, spread) in spreads.items():
        noise = np.random.default_rng([zlib.crc32(name.encode()), seed]).standard_normal(out[name].shape)
        drawn = base * np.exp(spread * noise) if base else spread * noise
        out[name] = __import__('jax').numpy.asarray(drawn.astype(out[name].dtype))
    for name, factor in factors.items():
        out[name] = (out[name] * factor).astype(out[name].dtype)
    return out
```

```python
from contextlib import ExitStack

import numpy as np

import concourse.bass as bass
from concourse import mybir

F32 = mybir.dt.float32
I32 = mybir.dt.int32
ACT = mybir.ActivationFunctionType
ALU = mybir.AluOpType
AX_X = mybir.AxisListType.X

P = 128
DM = 1024
KC = DM // P
SEQ, CTX = 512, 256
TOK = SEQ + CTX
DEPTH = 2
HD = 64
GRID = 64
ROWS = SEQ // GRID
NBC = 16
BAND_AT = (0, 8, 24, 32)
BAND = 32
NEG = -1.0e30
LOWEST = -3.0e38
EPS = 1e-6
QSCALE = HD ** -0.5
HEADS = 8

PAN = 256
W_IN = 4608
N_IN1 = W_IN // PAN
N_ADA1 = 3 * DM // PAN
N_ADA2 = 6 * DM // PAN
MIXC = 12
RING = 3
FF = 2816
FFC = FF // P
N_FF = FF // PAN
N_IN2 = 10
N_OUT2 = DM // PAN
W2_CUT = [(0, 8), (8, 15), (15, 22)]
PER2 = N_IN2 + N_OUT2 + 2 * N_FF + N_OUT2 * len(W2_CUT)
assert PER2 % RING == 0
CONV = 31
POOLPAD = 16
MAGIC = 1.5 * 2.0 ** 23

PRM = {}
_at = 0
for _name, _n in (("c", 2 * KC), ("c2", KC), ("ada_b", DEPTH * 24), ("norm_w", DEPTH * KC), ("final_w", KC),
                  ("qn", DEPTH), ("kn", DEPTH), ("final_g", KC), ("inv", 1), ("sign", 1)):
    PRM[_name] = (_at, _n)
    _at += _n
N_PRM = _at
LYR = {}
_at = 0
for _name, _n in (("ada_b", 48), ("nmix", KC), ("nffn", KC), ("pool_scale", 2), ("gn", 2), ("conv_b", 2),
                  ("ln_g", 2), ("ln_b", 2), ("conv_w", 2 * CONV), ("fox_b", 1)):
    LYR[_name] = (_at, _n)
    _at += _n
N_LYR = _at


def make_plan(groups, at):
    plan, waiting = [], None
    turned_for = {}

    def t_event(kind, **more):
        plan.append(dict(kind=kind, t=at["t"], **more))
        at["t"] += 1

    def behind(lo, hi):
        u = waiting
        for j in range(lo, hi):
            step = u["steps"][j]
            t_event("T", u=u["u"], unit=u, step=step, v=at["v"], first=j == 0, last=j == len(u["steps"]) - 1)
            at["v"] += 1
            u["t_last"], u["v_last"] = at["t"] - 1, at["v"] - 1

    def finish():
        plan.append(dict(kind="Y", u=waiting["u"], unit=waiting))

    v_end = []
    for g, (turns, units) in enumerate(groups):
        for src, dst in turns:
            t_event("V", src=src, dst=dst, need_group=g - 2, v_end=v_end)
        seen = at["t"]
        for u in units:
            u["u"], u["turned"] = at["u"], seen
            at["u"] += 1
            n = len(waiting["steps"]) if waiting else 0
            for qb in range(len(u["q"])):
                plan.append(dict(kind="S", s=at["s"], u=u["u"], unit=u, qb=qb))
                u["s_last"] = at["s"]
                at["s"] += 1
                if waiting:
                    k = len(u["q"])
                    behind(n * qb // k, n * (qb + 1) // k)
            if waiting:
                finish()
                if waiting.get("closes") is not None:
                    v_end.append(waiting["v_last"] + 1)
            waiting = u
        units[-1]["closes"] = g
    behind(0, len(waiting["steps"]))
    finish()
    return plan


def two_dit_blocks(nc, dram, out):
    with ExitStack() as ctx:
        def sb(name, shape, dt=F32, scope=ctx):
            return scope.enter_context(nc.sbuf_tensor(name, shape, dt))

        def sem(name):
            return ctx.enter_context(nc.semaphore(name))

        xl = sb("x_latent", [P, KC, SEQ])
        hl = sb("h_latent", [P, KC, SEQ])
        ring = sb("panel_ring", [P, RING, KC * PAN])
        prm = sb("vectors", [P, N_PRM])
        lyr = sb("layer_vectors", [P, DEPTH, N_LYR])
        mats = sb("matrices", [P, 5, P])
        ident, swap, turn, pairs, ones = (mats[:, i, :] for i in range(5))
        silu_c = sb("silu_c", [P, KC, 2])
        silu_c2 = sb("silu_c2", [P, KC])
        mod1 = sb("mod_first", [P, DEPTH, 24, 2])
        mod2 = sb("mod_second", [P, DEPTH, 48])
        gain1 = sb("gain_first", [P, 2, KC])
        rstd = sb("rstd", [P, TOK])
        probs = sb("probs", [P, 2, 2, TOK])
        squares, std = probs[:, 0, :, :], probs[:, 1, :, :]
        probs_t = sb("probs_turned", [P, 4, 256])
        rec = sb("reciprocals", [P, 2, 256])
        mx = sb("row_max", [P, 4])
        nmx = sb("neg_row_max", [P, 4])
        sinks = sb("sinks", [1, DEPTH * HEADS])
        sink_lhs = sb("sink_values", [1, 192])
        qn8 = sb("q_norm_scaled", [P, DEPTH])

        first, second = ExitStack(), ExitStack()
        with first:
            f = lambda *a: sb(*a, scope=first)
            xc = f("x_context", [P, KC, CTX])
            hc = f("h_context", [P, KC, CTX])
            y1 = f("mixed_first", [P, MIXC, TOK])
            slots = f("qkv", [P, 12, TOK])
            vband = f("values_band", [P, 2, 10, 192])
            bias = f("bias_rows", [P, 2, ROWS, 48])
            rope_c = f("rope_cos", [P, SEQ])
            rope_s = f("rope_sin", [P, SEQ])
            bmask = f("band_masks", [P, 3, SEQ])
            cmask = f("window_mask", [P, 641])
        vseq = slots[:, 9:12, :].rearrange("p a (b c) -> p (a b c)", c=192).rearrange(
            "p (t g c) -> p t g c", t=6, g=2)
        with second:
            f = lambda *a: sb(*a, scope=second)
            mix2 = f("mixed_second", [P, KC, SEQ])
            act2 = f("ffn_hidden", [P, FFC, SEQ])
            u2 = act2[:, 0:20, :]
            vret = f("values_retention", [P, 2, 4, 192])
            vfox = f("values_forgetting", [P, 2, 4, 192])
            ret_s = f("decayed_scores", [P, 4, SEQ])
            hpad = f("conv_in", [P, 2, CONV - 1 + SEQ])
            ppad = f("pool_in", [P, 2, POOLPAD + SEQ])
            psums = f("pool_sums", [P, 2, POOLPAD + SEQ])
            fmask = f("causal_mask", [P, P])[:, :]
            decay = f("decay", [P, 4, SEQ])
            counts = f("pool_counts", [P, 2, SEQ])
            rcos = f("ret_cos", [P, SEQ])
            rsin = f("ret_sin", [P, SEQ])
            poolw = f("pool_weights", [P, 2, P])
            ffw = f("forget_weights", [P, KC, 4])
            cur = f("this_layers_vectors", [P, N_LYR])
            mod = f("this_layers_mod", [P, 48])
            gain2 = f("gain_second", [P, 2, KC])
            augq = f("decay_of_queries", [P, SEQ])
            augk = f("decay_of_keys", [P, SEQ])
        conv = u2[:, 0:2, :]
        ret_o = u2[:, 4:6, :]
        pooled = u2[:, 12:14, :]
        angle = u2[:, 16:20, :]
        fz, ft = act2[0:4, 20, :], act2[0:4, 21, :]
        gate_buf = squares

        ps = ctx.enter_context(nc.psum_tensor("ps", [P, 4096], F32))
        bank = lambda b, a=0, e=512: ps[:, 512 * b + a:512 * b + e]

        vec_in, mats_in, x_in, tables_in, lyr_vec_in = (
            sem(n) for n in ("vec_in", "mats_in", "x_in", "tables_in", "lyr_vec_in"))
        panel_in = [sem(f"panel_in{i}") for i in range(RING)]
        silu_done = sem("silu_done")
        mod_ready, mod_taken = sem("mod_ready"), sem("mod_taken")
        x_ready = sem("x_ready")
        sq_ready, sq_summed, std_ready = sem("sq_ready"), sem("sq_summed"), sem("std_ready")
        hm_ready, h_ready = sem("hm_ready"), sem("h_ready")
        proj_ready, proj_taken = sem("proj_ready"), sem("proj_taken")
        qsq_ready, qsum_ready, qstd_ready, qn_done = (
            sem(n) for n in ("qsq_ready", "qsum_ready", "qstd_ready", "qn_done"))
        sw_ready, rope_done, kdup_done = sem("sw_ready"), sem("rope_done"), sem("kdup_done")
        vones = sem("vones")
        bias_in = [sem("bias_in0"), sem("bias_in1")]
        s_ready, max_ready, exp_done = sem("s_ready"), sem("max_ready"), sem("exp_done")
        pt_ready, pt_taken = sem("pt_ready"), [sem("pt_taken_dve"), sem("pt_taken_act")]
        pv_steps, y_done = sem("pv_steps"), sem("y_done")
        u_ready = sem("u_ready")
        out_ready = sem("out_ready")
        tables2_in, pos_in, pads_done = sem("tables2_in"), sem("pos_in"), sem("pads_done")
        angle_done, sines_done, ret_trig = sem("angle_done"), sem("sines_done"), sem("ret_trig")
        lyr_in, cur_done = sem("lyr_in"), sem("cur_done")
        conv_done, ln_sum, ln_dev, ln_sq, ln_var, ln_std, ln_norm, conv_mix = (
            sem(n) for n in ("conv_done", "ln_sum", "ln_dev", "ln_sq", "ln_var", "ln_std", "ln_norm", "conv_mix"))
        rv_ready, rv_taken = sem("rv_ready"), sem("rv_taken")
        rs_ready, rs_done, ro_steps, ro_taken = (sem(n) for n in ("rs_ready", "rs_done", "ro_steps", "ro_taken"))
        gn_sum, gn_dev, gn_sq, gn_var, gn_std, ret_mix = (
            sem(n) for n in ("gn_sum", "gn_dev", "gn_sq", "gn_var", "gn_std", "ret_mix"))
        pool_done, pool_proj, pool_mix = sem("pool_done"), sem("pool_proj"), sem("pool_mix")
        ff_ready, ff_log, ff_cum, aug_in = sem("ff_ready"), sem("ff_log"), sem("ff_cum"), sem("aug_in")
        h1_ready, h3_ready, silu_ready, f_ready = (
            sem(n) for n in ("h1_ready", "h3_ready", "silu_ready", "f_ready"))
        w2_used = sem("w2_used")
        result_ready, result_out = sem("result_ready"), sem("result_out")

        def vec(name, i=0, n=1):
            return prm[:, PRM[name][0] + i:PRM[name][0] + i + n]

        def lvec(name, i=0, n=1):
            return cur[:, LYR[name][0] + i:LYR[name][0] + i + n]

        MA, MB, MC = 0, 6, 18
        rows_of = lambda h: slice(HD * (h % 2), HD * (h % 2) + HD)

        def pv_value(tile, h):
            return tile[:, HD:HD + P] if h % 2 == 0 else tile[:, 0:P]

        def pv_pair(tile, h):
            return tile[:, 0:P] if h % 2 == 0 else tile[:, HD:HD + P]

        def sink_lhsT(h):
            return sink_lhs[:, HD:HD + P] if h % 2 == 0 else sink_lhs[:, 0:P]

        def seq_units(mixer, l):
            units = []
            for h in range(HEADS):
                kv, r = h // 4, rows_of(h)
                q, k = slots[r, h // 2, :], slots[r, 6 + kv, :]
                y = y1[r, (0 if mixer == "A" else 8) + h // 2, :]
                sink = [(sinks[:, l * HEADS + h:l * HEADS + h + 1])] if mixer == "C" else []
                for pair in range(2):
                    qbs = [2 * pair, 2 * pair + 1]
                    u = dict(h=h, q=[q[:, P * b:P * b + P] for b in qbs], seg=[], extra=[], w=[], mask=[], steps=[],
                             dst=[(0, 256, y[:, 256 * pair:256 * pair + 256])])
                    cols = []
                    for b in qbs:
                        if mixer == "A":
                            u["seg"].append([(0, k[:, 0:SEQ]), (SEQ, k[:, SEQ:TOK])])
                            u["w"].append(TOK)
                            u["mask"].append(None)
                            u["extra"].append([])
                            cols.append({t: P * t for t in range(6)})
                            continue
                        at, seg, col = 0, [], {}
                        if b > 0:
                            seg.append((0, k[:, P * (b - 1):P * b]))
                            col[b - 1] = 0
                            at = P
                        seg.append((at, k[:, SEQ:TOK]))
                        col[4], col[5] = at, at + P
                        at += CTX
                        for t in range(b, min(b + 2, 4)):
                            seg.append((at, k[:, P * t:P * t + P]))
                            col[t] = at
                            at += P
                        u["seg"].append(seg)
                        u["extra"].append([(at, ones[0:1, :], sink[0], True)])
                        col["sink"] = at
                        u["w"].append(at + 1)
                        first_col = 0 if b > 0 else P
                        u["mask"].append(cmask[:, first_col:first_col + at + 1])
                        cols.append(col)
                    for t in [4, 5, 0, 1, 2, 3] + (["sink"] if mixer == "C" else []):
                        has = [i for i in range(2) if t in cols[i]]
                        if not has:
                            continue
                        lhs = sink_lhsT(h) if t == "sink" else pv_value(vseq[:, t, kv, :], h)
                        u["steps"].append((lhs, 1 if t == "sink" else P, [(i, cols[i][t]) for i in has], P * has[0]))
                    units.append(u)
            return units

        def context_units(mixer, l):
            units = []
            for h in range(HEADS):
                r = rows_of(h)
                if mixer == "B":
                    q, k, y0 = slots[r, h // 2, :], slots[r, 4 + h // 2, :], 4
                else:
                    q, k, y0 = slots[r, h // 2, :], slots[r, 6 + h // 4, :], 0 if mixer == "A" else 8
                u = dict(h=h, q=[], seg=[], extra=[], w=[], mask=[], steps=[],
                         dst=[(0, 256, y1[r, y0 + h // 2, SEQ:TOK])])
                for b in range(2):
                    u["q"].append(q[:, SEQ + P * b:SEQ + P * b + P])
                    u["seg"].append([(0, k[:, SEQ:TOK])])
                    u["mask"].append(None)
                    u["extra"].append([(CTX, ones[0:1, :], sinks[:, l * HEADS + h:l * HEADS + h + 1], True)]
                                      if mixer == "C" else [])
                    u["w"].append(CTX + 1 if mixer == "C" else CTX)
                for t in range(2):
                    lhs = (pv_pair(vband[:, h // 2 % 2, t, :], h) if mixer == "B"
                           else pv_value(vseq[:, 4 + t, h // 4, :], h))
                    u["steps"].append((lhs, P, [(0, P * t), (1, P * t)], 0))
                if mixer == "C":
                    u["steps"].append((sink_lhsT(h), 1, [(0, CTX), (1, CTX)], 0))
                units.append(u)
            return units

        def grid(ap):
            return ap.rearrange("p (r c) -> p r c", c=GRID)

        def band_units(h, l):
            r = rows_of(h)
            q, k = slots[r, h // 2, :], slots[r, 4 + h // 2, :]
            y = grid(y1[r, 4 + h // 2, 0:SEQ])
            units = []
            for pair in range(2):
                u = dict(h=h, q=[], seg=[], extra=[], w=[], mask=[], steps=[], bias=(l * HEADS + h) if pair == 0 else None,
                         dst=[(0, 256, y[:, :, 32 * pair:32 * pair + 32].rearrange("p r c -> p c r"))])
                for i in range(2):
                    b = 2 * pair + i
                    k0 = BAND_AT[b]
                    off = NBC + BAND_AT[b] - NBC * b
                    u["q"].append(q[:, P * b:P * b + P])
                    u["seg"].append([(0, k[:, SEQ:TOK]), (CTX, k[:, ROWS * k0:ROWS * (k0 + BAND)])])
                    u["extra"].append([(CTX, turn, bias[:, h % 2, :, off:off + BAND].rearrange("p k j -> p j k"), False)])
                    u["w"].append(SEQ)
                    u["mask"].append(bmask[:, [0, 1, 1, 2][b], :])
                for t in range(2):
                    u["steps"].append((pv_pair(vband[:, h // 2 % 2, t, :], h), P, [(0, P * t), (1, P * t)], 0))
                for i in range(2):
                    for half in range(2):
                        tile = vband[:, h // 2 % 2, 2 + 2 * (2 * pair + i) + half, :]
                        u["steps"].append((pv_pair(tile, h), P, [(i, CTX + P * half)], P * i))
                units.append(u)
            units[-1]["bias_end"] = True
            return units

        def seq_turns():
            out = []
            for t in range(0, 6, 2):
                src = [slots[:, 5, P * (t + i):P * (t + i) + P] for i in range(2)]
                out.append((src, [vseq[:, t + i, :, HD:2 * HD] for i in range(2)]))
            return out

        def band_turns(p):
            v = slots[:, 8 + p, :]
            src = [v[:, SEQ + P * t:SEQ + P * t + P] for t in range(2)]
            for b in range(4):
                for half in range(2):
                    at0 = ROWS * BAND_AT[b] + P * half
                    src.append(v[:, at0:at0 + P])
            out = []
            for t in range(0, 10, 2):
                dst = [vband[:, p % 2, t + i, :].rearrange("p (g c) -> p g c", c=HD)[:, 0:3:2, :] for i in range(2)]
                out.append((src[t:t + 2], dst))
            return out

        at = dict(s=0, t=0, v=0, u=0)
        plans = {}
        for l in range(DEPTH):
            full = l < DEPTH - 1
            for m in "ABC":
                if m == "B":
                    groups = []
                    for p in range(4):
                        units = []
                        for h in (2 * p, 2 * p + 1):
                            units += band_units(h, l)
                        if full:
                            units += [u for u in context_units("B", l) if u["h"] // 2 == p]
                        groups.append((band_turns(p), units))
                else:
                    groups = [(seq_turns(), seq_units(m, l) + (context_units(m, l) if full else []))]
                plans[l, m] = (make_plan(groups, at), at["u"])
        start2 = dict(at)

        def fox_units():
            units = []
            for h in range(4):
                r = rows_of(h)
                q, k = u2[r, 14 + h // 2, :], u2[r, 16 + h // 2, :]
                for pair in range(2):
                    u = dict(h=h, q=[], seg=[], extra=[], w=[], mask=[], steps=[],
                             dst=[(0, 256, mix2[r, h // 2, 256 * pair:256 * pair + 256])])
                    for b in (2 * pair, 2 * pair + 1):
                        w = P * (b + 1)
                        u["q"].append(q[:, P * b:P * b + P])
                        u["seg"].append([(0, k[:, 0:w])])
                        u["extra"].append([(0, augq[32 * h:32 * h + 2, P * b:P * b + P], augk[32 * h:32 * h + 2, 0:w], False)])
                        u["w"].append(w)
                        u["mask"].append("last tile")
                    for t in range(2 * pair + 2):
                        has = [i for i in range(2) if t <= 2 * pair + i]
                        u["steps"].append((pv_pair(vfox[:, h // 2, t, :], h), P, [(i, P * t) for i in has], P * has[0]))
                    units.append(u)
            return units

        def fox_turns():
            out = []
            for p in range(2):
                for t in range(0, 4, 2):
                    src = [u2[:, 18 + p, P * (t + i):P * (t + i) + P] for i in range(2)]
                    dst = [vfox[:, p, t + i, :].rearrange("p (g c) -> p g c", c=HD)[:, 0:3:2, :] for i in range(2)]
                    out.append((src, dst))
            return out

        fox_plan = make_plan([(fox_turns(), fox_units())], at)
        per = {k: at[k] - start2[k] for k in at}
        assert per["s"] % 2 == 0 and per["t"] % 2 == 0 and per["v"] % 4 == 0 and per["u"] % 2 == 0

        class Off:
            def __init__(self, l):
                zero = l is None
                self.s = 0 if zero else l * per["s"]
                self.t = 0 if zero else l * per["t"]
                self.half = 0 if zero else l * (per["t"] // 2)
                self.v = 0 if zero else l * per["v"]
                self.u = 0 if zero else l * per["u"]

        def scores_at(s, n):
            return ps[:, 2048 + 1024 * (s % 2):2048 + 1024 * (s % 2) + n]

        def turned_at(t, k, n):
            return bank(2 + t % 2)[0:k, 0:n]

        def attention_pe(pe, plan, o):
            pend = None

            def multiply(ev):
                lhs, k, qbs, col = ev["step"]
                n = P * len(qbs)
                pe.wait_ge(pt_taken[ev["t"] % 2], ev["t"] // 2 + 1 + o.half)
                if ev["first"]:
                    seen = ev["unit"]["turned"]
                    if seen:
                        pe.wait_ge(pt_taken[0], (seen + 1) // 2 + o.half)
                        pe.wait_ge(pt_taken[1], seen // 2 + o.half)
                    if ev["u"] >= 2:
                        pe.wait_ge(y_done, ev["u"] - 1 + o.u)
                nc.tensor.matmul(bank(ev["u"] % 2, col, col + n), lhs, probs_t[0:k, ev["v"] % 4, 0:n],
                                 start=ev["first"], stop=ev["last"], skip_group_check=True).then_inc(pv_steps, 1)

            for ev in plan:
                u = ev.get("unit")
                if ev["kind"] == "S":
                    qb = ev["qb"]
                    if ev["s"] >= 2:
                        pe.wait_ge(exp_done, ev["s"] - 1 + o.s)
                    if qb == 0 and u.get("bias") is not None:
                        pe.wait_ge(bias_in[u["bias"] % 2], 16 * ROWS * (u["bias"] // 2 + 1))
                    S = scores_at(ev["s"], 1024)
                    for col, rhs in u["seg"][qb]:
                        n = rhs.free_size()
                        while n:
                            k = min(n, 512 - col % 512)
                            mm = nc.tensor.matmul(S[:, col:col + k], u["q"][qb], rhs, start=True, stop=True,
                                                  skip_group_check=True)
                            n -= k
                            assert n == 0
                    for col, lhs, rhs, alone in u["extra"][qb]:
                        n = rhs.free_size()
                        mm = nc.tensor.matmul(S[:, col:col + n], lhs, rhs, start=alone, stop=True, skip_group_check=True)
                    mm.then_inc(s_ready, 1)
                elif ev["kind"] in "TV":
                    if ev["kind"] == "T":
                        src = [probs[:, ev["u"] % 2, i, c:c + ev["step"][1]] for i, c in ev["step"][2]]
                        k = ev["step"][1]
                        if ev["first"]:
                            pe.wait_ge(exp_done, u["s_last"] + 1 + o.s)
                    else:
                        src, k = ev["src"], P
                    if ev["t"] >= 2:
                        pe.wait_ge(pt_taken[ev["t"] % 2], ev["t"] // 2 + o.half)
                    for i, x in enumerate(src):
                        mm = nc.tensor.transpose(turned_at(ev["t"], k, 256)[:, P * i:P * i + P], x, ident)
                    mm.then_inc(pt_ready, 1)
                    if pend:
                        multiply(pend)
                    pend = ev if ev["kind"] == "T" else None
                else:
                    if pend:
                        multiply(pend)
                    pend = None

        def copy_turned(eng, copy, ev, o):
            eng.wait_ge(pt_ready, ev["t"] + 1 + o.t)
            if ev["kind"] == "T":
                _, k, qbs, _ = ev["step"]
                n = P * len(qbs)
                if ev["v"] >= 4:
                    eng.wait_ge(pv_steps, ev["v"] - 3 + o.v)
                copy(probs_t[0:k, ev["v"] % 4, 0:n], turned_at(ev["t"], k, n)).then_inc(pt_taken[ev["t"] % 2], 1)
            else:
                if ev["need_group"] >= 0:
                    eng.wait_ge(pv_steps, ev["v_end"][ev["need_group"]] + o.v)
                for i, d in enumerate(ev["dst"]):
                    ins = copy(d, turned_at(ev["t"], P, 256)[:, P * i:P * i + P].rearrange("p (g c) -> p g c", c=HD))
                ins.then_inc(pt_taken[ev["t"] % 2], 1)

        def attention_dve(dve, plan, o):
            for ev in plan:
                u = ev.get("unit")
                if ev["kind"] == "S":
                    s, w, mask = ev["s"], u["w"][ev["qb"]], u["mask"][ev["qb"]]
                    dve.wait_ge(s_ready, s + 1 + o.s)
                    S = scores_at(s, w)
                    if mask == "last tile":
                        nc.vector.tensor_tensor(S[:, w - P:w], S[:, w - P:w], fmask, ALU.add)
                        dve.drain()
                        mask = None
                    if mask is None:
                        nc.vector.reduce_max(mx[:, s % 4:s % 4 + 1], S, AX_X)
                    else:
                        nc.vector.tensor_tensor_reduce(out=S, in0=S, in1=mask, scale=1.0, scalar=LOWEST, op0=ALU.add,
                                                       op1=ALU.max, accum_out=mx[:, s % 4:s % 4 + 1])
                    dve.drain()
                    nc.vector.tensor_scalar(nmx[:, s % 4:s % 4 + 1], mx[:, s % 4:s % 4 + 1], -1.0, None,
                                            ALU.mult).then_inc(max_ready, 1)
                elif ev["kind"] in "TV":
                    if ev["t"] % 2 == 0:
                        copy_turned(dve, nc.vector.tensor_copy, ev, o)
                else:
                    k = ev["u"]
                    r, sums = rows_of(u["h"]), rows_of(u["h"] + 1)
                    dve.wait_ge(pv_steps, u["v_last"] + 1 + o.v)
                    nc.vector.reciprocal(rec[r, k % 2, :], bank(k % 2, 0, 256)[sums])
                    dve.drain()
                    for c, n, d in u["dst"]:
                        a, b = bank(k % 2, c, c + n)[r], rec[r, k % 2, c:c + n]
                        if len(d.shape) == 3:
                            a, b = (z.rearrange("p (c r) -> p c r", r=ROWS) for z in (a, b))
                        ins = nc.vector.tensor_tensor(d, a, b, ALU.mult)
                    ins.then_inc(y_done, 1)

        def attention_act(act, plan, o):
            ends = {}
            for ev in plan:
                u = ev.get("unit")
                if ev["kind"] == "S":
                    s, w = ev["s"], u["w"][ev["qb"]]
                    act.wait_ge(max_ready, s + 1 + o.s)
                    if ev["qb"] == 0 and ev["u"] - 2 in ends:
                        act.wait_ge(pt_ready, ends[ev["u"] - 2] + 1 + o.t)
                    nc.scalar.activation(probs[:, ev["u"] % 2, ev["qb"], 0:w], scores_at(s, w), ACT.Exp,
                                         bias=nmx[:, s % 4:s % 4 + 1]).then_inc(exp_done, 1)
                elif ev["kind"] in "TV":
                    if ev["kind"] == "T":
                        ends[ev["u"]] = ev["t"]
                    if ev["t"] % 2 == 1:
                        copy_turned(act, nc.scalar.copy, ev, o)

        ADA1, ADA2, IN1, OUT1 = "ada1", "ada2", "in1", "out1"
        spare = {0: [(ADA1, 1, i) for i in range(N_ADA1)] + [(ADA2, 0, i) for i in range(N_ADA2)],
                 1: [(ADA2, 1, i) for i in range(N_ADA2)]}
        stream = [(ADA1, 0, i) for i in range(N_ADA1)]
        for l in range(DEPTH):
            for i in range(N_IN1):
                stream.append((IN1, l, i))
                stream += spare[l][2 * i:2 * i + 2]
            stream += [(OUT1, l, i) for i in range(KC)]
        number = {p: n for n, p in enumerate(stream)}
        N1 = len(stream)
        ada_seq = [p for p in stream if p[0] in (ADA1, ADA2)]
        ada_no = {p: n for n, p in enumerate(ada_seq)}
        n_mod1 = {l: max(ada_no[ADA1, l, i] for i in range(N_ADA1)) + 1 for l in range(DEPTH)}
        per2 = ([("in2", 0, i) for i in range(N_IN2)] + [("out2", 0, i) for i in range(N_OUT2)]
                + [(k, 0, i) for i in range(N_FF) for k in ("w1", "w3")]
                + [("w2", g, j) for g in range(N_OUT2) for j in range(len(W2_CUT))])
        assert len(per2) == PER2

        def slot(n, chunks=KC):
            return ring[:, n % RING, :].rearrange("p (c n) -> p c n", c=chunks)

        def panel_wait(eng, n, l=None):
            eng.wait_ge(panel_in[n % RING], 16 * (n // RING + 1) + (0 if l is None else l * (16 * PER2 // RING)))

        NSEQ = {}
        def blocks_of(l, m):
            lo, hi = {"A": (0, 6), "B": (6, 18), "C": (18, 24), "G": (24, 36)}[m]
            last = l == DEPTH - 1
            return [(b, SEQ if last and (m == "G" or b - lo < 4) else TOK) for b in range(lo, hi)]

        for l in range(DEPTH):
            for m in "ABCG":
                for b, _ in blocks_of(l, m):
                    NSEQ[l, b] = len(NSEQ)
        NPROJ1 = len(NSEQ)
        NX1 = DEPTH * KC + KC
        out_tokens = lambda l: TOK if l < DEPTH - 1 else SEQ
        slot_of = lambda b: b if b < 6 else b - 6 if b < 18 else b - 18

        def used(n):
            kind, l, i = stream[n]
            if kind in (ADA1, ADA2):
                return mod_ready, ada_no[stream[n]] + 1
            if kind == IN1:
                return proj_ready, NSEQ[l, 2 * i + 1] + 1
            return out_ready, l * KC + i + 1

        def used2(i, l):
            kind, g, j = per2[i]
            if kind == "in2":
                return proj_ready, NPROJ1 + 2 * j + 2 + l * 20
            if kind == "out2":
                return out_ready, DEPTH * KC + 2 * j + 2 + l * 2 * KC
            if kind == "w1":
                return h1_ready, 2 * j + 2 + l * FFC
            if kind == "w3":
                return h3_ready, 2 * j + 2 + l * FFC
            if j < len(W2_CUT) - 1:
                return w2_used, 2 * g + j + 1 + l * 2 * N_OUT2
            return out_ready, DEPTH * KC + KC + 2 * g + 2 + l * 2 * KC

        block = ctx.enter_context(nc.Block())

        @block.sync
        def _(sp):
            sp.dma_start(prm[:, :], dram["prm"]).then_inc(vec_in, 16)
            for n, (kind, l, i) in enumerate(stream):
                if n >= RING:
                    sp.wait_ge(*used(n - RING))
                src = dram[kind][l, i]
                sp.dma_start(ring[:, n % RING, 0:src.shape[-1]], src).then_inc(panel_in[n % RING], 16)
                if n == 0:
                    sp.dma_start(mats[:, :, :], dram["mats"]).then_inc(mats_in, 16)
                    sp.dma_start(xl[:, :, :], dram["x"]).then_inc(x_in, 16)
                    sp.dma_start(xc[:, :, :], dram["ctx"]).then_inc(x_in, 16)
                if n == 4:
                    sp.dma_start(rope_c[:, :], dram["rope"][:, 0, :]).then_inc(tables_in, 16)
                    sp.dma_start(rope_s[:, :], dram["rope"][:, 1, :]).then_inc(tables_in, 16)
                    sp.dma_start(bmask[:, :, :], dram["bmask"]).then_inc(tables_in, 16)
                    sp.dma_start(cmask[:, :], dram["cmask"]).then_inc(tables_in, 16)
                    sp.dma_start(sinks[:, :], dram["sinks"]).then_inc(tables_in, 16)
                    sp.dma_start(sink_lhs[:, :], dram["sink_lhs"]).then_inc(tables_in, 16)
                    sp.dma_start(lyr[:, :, :], dram["lyr"]).then_inc(lyr_vec_in, 16)
            sp.wait_ge(x_ready, NX1)
            sp.dma_start(angle[:, 0, :].bitcast(I32), dram["pos"].partition_broadcast(P)).then_inc(pos_in, 16)
            for tile, name in ((fmask, "fmask"), (decay[:, :, :], "decay"), (counts[:, :, :], "counts")):
                sp.dma_start(tile, dram[name]).then_inc(tables2_in, 16)
            with sp.Fori(0, DEPTH) as l:
                for i, (kind, g, j) in enumerate(per2):
                    n = N1 + i
                    if i < RING:
                        sp.wait_ge(out_ready, DEPTH * KC + l * 2 * KC)
                    else:
                        sp.wait_ge(*used2(i - RING, l))
                    if kind == "w2":
                        a, e = W2_CUT[j]
                        src = dram[kind][bass.ds(l, 1), g, :, PAN * a:PAN * e]
                    else:
                        src = dram[kind][bass.ds(l, 1), j, :, :]
                    src = src.rearrange("a p n -> (a p) n")
                    sp.dma_start(ring[:, n % RING, 0:src.shape[-1]], src).then_inc(panel_in[n % RING], 16)
                    if i == 0:
                        sp.dma_start(ffw[:, :, :].rearrange("p c n -> p (c n)"),
                                     dram["ffw"][bass.ds(l, 1), :, :].rearrange("a p n -> (a p) n")).then_inc(lyr_in, 16)
                        sp.dma_start(poolw[:, :, :].rearrange("p c n -> p (c n)"),
                                     dram["poolw"][bass.ds(l, 1), :, :].rearrange("a p n -> (a p) n")).then_inc(lyr_in, 16)
            sp.wait_ge(result_ready, KC)
            sp.dma_start(out, hl[:, :, :]).then_inc(result_out, 16)
            sp.wait_ge(result_out, 16)

        @block.gpsimd
        def _(pool):
            s_end = {}
            for l in range(DEPTH):
                for ev in plans[l, "B"][0]:
                    if ev["kind"] == "S" and ev["unit"].get("bias_end"):
                        s_end[l * HEADS + ev["unit"]["h"]] = ev["s"] + 1

            def bias_rows(n):
                if n >= 2:
                    pool.wait_ge(s_ready, s_end[n - 2])
                for r in range(ROWS):
                    src = bass.AP(dram["rpb"].tensor, n * 15 * 64 + 64 * r, [[1, NBC], [64, ROWS], [1, 48]])
                    pool.dma_start(bias[NBC * r:NBC * r + NBC, n % 2, :, :], src).then_inc(bias_in[n % 2], 16)

            pool.memset(vseq, 1.0).then_inc(vones, 1)
            pool.memset(vband[:, :, :, HD:2 * HD], 1.0).then_inc(vones, 1)
            for l in range(DEPTH):
                if l > 0:
                    pool.wait_ge(y_done, plans[l - 1, "C"][1])
                    pool.memset(vseq, 1.0).then_inc(vones, 1)
                for h in range(HEADS):
                    bias_rows(l * HEADS + h)
                pool.wait_ge(y_done, plans[l, "B"][1])
                pool.memset(vseq, 1.0).then_inc(vones, 1)
            pool.wait_ge(x_ready, NX1)
            pool.memset(hpad[:, :, 0:CONV - 1], 0.0).then_inc(pads_done, 1)
            pool.memset(ppad[:, :, 0:POOLPAD], 0.0).then_inc(pads_done, 1)
            pool.memset(vret[:, :, :, HD:2 * HD], 0.0).then_inc(pads_done, 1)
            pool.memset(vfox[:, :, :, HD:2 * HD], 1.0).then_inc(pads_done, 1)
            pool.memset(augq[:, :], 1.0).then_inc(pads_done, 1)
            pool.memset(augk[:, :], 1.0).then_inc(pads_done, 1)
            pool.wait_ge(pads_done, 6)
            pool.wait_ge(tables2_in, 48)
            with pool.Fori(0, DEPTH) as l:
                pool.wait_ge(proj_taken, NPROJ1 + 14 + l * 20)
                n = POOLPAD + SEQ
                A, B = psums[:, 0, :], psums[:, 1, :]
                halves = {1: (0, 0), 2: (1, 0), 4: (0, 1), 8: (1, 1)}
                for t in range(2):
                    src = ppad[:, t, :]
                    for k, dst in ((1, A), (2, B)) if t == 0 else ((1, A), (2, B), (4, A), (8, B)):
                        lo = 2 * k - 1
                        nc.gpsimd.tensor_tensor(dst[:, lo:n], src[:, lo:n], src[:, lo - k:n - k], ALU.add)
                        pool.drain()
                        half, tile = halves[k]
                        if tile == t:
                            r = slice(HD * half, HD * half + HD)
                            nc.gpsimd.tensor_tensor(pooled[r, t, :], dst[r, POOLPAD:n], counts[r, t, :], ALU.mult)
                        src = dst
                    pool.drain()
                nc.gpsimd.tensor_tensor(pooled, pooled, ppad[:, :, POOLPAD:n], ALU.subtract).then_inc(pool_done, 1)

        @block.scalar
        def _(act):
            A_ = nc.scalar.activation

            def take_mod(p):
                kind, l, i = p
                k = ada_no[p]
                act.wait_ge(mod_ready, k + 1)
                dst = mod1[:, l, 2 * i:2 * i + 2, :].rearrange("p a b -> p (a b)") if kind == ADA1 else mod2[:, l, 2 * i:2 * i + 2]
                n = 4 if kind == ADA1 else 2
                nc.scalar.copy(dst, bank(4 + k % 2, 0, n)).then_inc(mod_taken, 1)

            def norm(k, parts, x_count, kb=None, shift=None):
                for c in range(KC):
                    if x_count is None:
                        act.wait_ge(x_in, 32)
                    else:
                        act.wait_ge(x_ready, x_count + c + 1)
                    if isinstance(k, int) and 8 * k + c >= 2 or not isinstance(k, int):
                        act.wait_ge(sq_summed, 8 * k + c - 1)
                    for j, (x, _, lo, n) in enumerate(parts):
                        ins = A_(squares[:, c % 2, lo:lo + n], x[:, c, :], ACT.Square)
                    ins.then_inc(sq_ready, 1)
                act.wait_ge(sq_summed, 8 * k + KC)
                for j, (_, _, lo, n) in enumerate(parts):
                    ins = A_(std[:, 0, lo:lo + n], bank(6 + j, 0, n), ACT.Sqrt, bias=EPS, scale=1.0 / DM)
                ins.then_inc(std_ready, 1)
                if shift is None:
                    return
                for c in range(KC):
                    act.wait_ge(hm_ready, 8 * kb + c + 1)
                    for j, (_, h, lo, n) in enumerate(parts):
                        ins = A_(h[:, c, :], h[:, c, :], ACT.Identity, bias=shift(c, j))
                    ins.then_inc(h_ready, 1)

            both = [(xl, hl, 0, SEQ), (xc, hc, SEQ, CTX)]
            act.wait_ge(vec_in, 16)
            A_(silu_c[:, :, :].rearrange("p a b -> p (a b)"), vec("c", 0, 2 * KC), ACT.Silu).then_inc(silu_done, 1)
            A_(silu_c2[:, :], vec("c2", 0, KC), ACT.Silu).then_inc(silu_done, 1)
            for i in range(N_ADA1):
                take_mod((ADA1, 0, i))

            def projected(l, m):
                for b, n in blocks_of(l, m):
                    k = NSEQ[l, b]
                    act.wait_ge(proj_ready, k + 1)
                    if m == "G":
                        dst, f, scale = gate_buf[:, k % 2, :], ACT.Silu, 1.0
                        g = l * MIXC + b - 24
                        if g >= 2:
                            act.wait_ge(u_ready, g - 1)
                    else:
                        dst, f = slots[:, slot_of(b), :], ACT.Copy
                        scale = QSCALE if m in "BC" and b - {"B": 6, "C": 18}[m] < 4 else 1.0
                    to, src = dst[:, 0:SEQ], bank(k % 2)
                    if m == "B":
                        to, src = to.rearrange("p (c r) -> p r c", r=ROWS), src.rearrange("p (r c) -> p r c", c=GRID)
                    ins = A_(to, src, f, scale=scale)
                    if n == TOK:
                        ins = A_(dst[:, SEQ:TOK], bank(2 + k % 2, 0, CTX), f, scale=scale)
                    ins.then_inc(proj_taken, 1)
                    if b % 2 == 1:
                        for p in spare[l][b - 1:b + 1]:
                            take_mod(p)

            def qk_norm(l):
                width = lambda j: TOK if l < DEPTH - 1 or j == 4 else SEQ

                def square(j):
                    q = 5 * l + j
                    act.wait_ge(proj_taken, NSEQ[l, j] + 1)
                    if q >= 2:
                        act.wait_ge(qsum_ready, q - 1)
                    A_(squares[:, j % 2, 0:width(j)], slots[:, j, 0:width(j)], ACT.Square).then_inc(qsq_ready, 1)

                def root(j):
                    q = 5 * l + j
                    act.wait_ge(qsum_ready, q + 1)
                    if q >= 2:
                        act.wait_ge(qn_done, q - 1)
                    b = 4 + 2 * (j % 2)
                    ins = A_(std[:, j % 2, 0:SEQ], bank(b), ACT.Sqrt, bias=EPS, scale=1.0 / HD)
                    if width(j) == TOK:
                        ins = A_(std[:, j % 2, SEQ:TOK], bank(b + 1, 0, CTX), ACT.Sqrt, bias=EPS, scale=1.0 / HD)
                    ins.then_inc(qstd_ready, 1)

                square(0)
                for j in range(1, 5):
                    square(j)
                    root(j - 1)
                root(4)

            vones_by = {(0, "A"): 2, (0, "B"): 2, (0, "C"): 3, (1, "A"): 4, (1, "B"): 4, (1, "C"): 5}
            zero = Off(None)
            for l in range(DEPTH):
                norm(l, both, None if l == 0 else KC * (l - 1), l, lambda c, j: mod1[:, l, c, j:j + 1])
                for m in "ABC":
                    projected(l, m)
                    if m == "A":
                        qk_norm(l)
                    act.wait_ge(vones, vones_by[l, m])
                    attention_act(act, plans[l, m][0], zero)
                projected(l, "G")
            latent = [(xl, hl, 0, SEQ)]
            norm(2, latent, KC * (DEPTH - 1))

            act.wait_ge(angle_done, 1)
            A_(rsin[:, :], angle[:, 0, :], ACT.Sin).then_inc(sines_done, 1)
            A_(rcos[:, :], angle[:, 0, :], ACT.Sin, scale=0.5).then_inc(sines_done, 1)
            act.wait_ge(pads_done, 6)
            with act.Fori(0, DEPTH) as l:
                o = Off(l)
                norm(3 + l * 2, latent, NX1 - KC + l * 2 * KC, 2 + l * 2, lambda c, j: mod[:, c:c + 1])
                act.wait_ge(ff_ready, 1 + l)
                A_(fz, bank(3)[0:4], ACT.Identity, bias=lvec("fox_b")[0:4])
                act.drain()
                A_(ft, fz, ACT.Abs)
                act.drain()
                A_(ft, ft, ACT.Exp, scale=-1.0)
                act.drain()
                A_(ft, ft, ACT.Ln, bias=1.0).then_inc(ff_log, 1)
                for m in range(20):
                    act.wait_ge(proj_ready, NPROJ1 + m + 1 + l * 20)
                    src, dst, f, scale = bank(m % 2), u2[:, m, :], ACT.Copy, 1.0
                    if m in (2, 3):
                        f = ACT.Sigmoid
                    elif m in (6, 7, 14, 15):
                        scale = QSCALE
                    elif m in (10, 11):
                        f = ACT.Silu
                    elif m in (12, 13):
                        dst = ppad[:, m - 12, POOLPAD:]
                    A_(dst, src, f, scale=scale).then_inc(proj_taken, 1)
                act.wait_ge(ff_cum, 1 + l)
                for h in range(4):
                    act.dma_start(augq[32 * h:32 * h + 1, :], fz[h:h + 1, :]).then_inc(aug_in, 16)
                    act.dma_start(augk[32 * h + 1:32 * h + 2, :], ft[h:h + 1, :]).then_inc(aug_in, 16)
                for g in range(2):
                    act.wait_ge(rv_ready, g + 1 + l * 2)
                    for h in range(2):
                        ins = nc.scalar.copy(vret[:, g, :, P * h:P * h + HD],
                                             bank(2 + g).rearrange("p (t c) -> p t c", c=P)[:, :, HD * h:HD * h + HD])
                    ins.then_inc(rv_taken, 1)
                for g in range(2):
                    act.wait_ge(ro_steps, 8 * (g + 1) + l * 16)
                    nc.scalar.copy(ret_o[:, g, :], bank(g)).then_inc(ro_taken, 1)
                act.wait_ge(ln_dev, 2 + l * 2)
                for t in range(2):
                    A_(squares[:, t, 0:SEQ], conv[:, t, :], ACT.Square).then_inc(ln_sq, 1)
                act.wait_ge(ln_var, 1 + l)
                A_(std[:, 0, 0:SEQ], bank(7), ACT.Sqrt, bias=EPS, scale=1.0 / 256).then_inc(ln_std, 1)
                for t in range(2):
                    act.wait_ge(ln_norm, t + 1 + l * 2)
                    A_(mix2[:, 6 + t, :], conv[:, t, :], ACT.Silu, bias=lvec("ln_b", t), scale=lvec("ln_g", t)).then_inc(conv_mix, 1)
                for g in range(2):
                    act.wait_ge(gn_dev, g + 1 + l * 2)
                    A_(squares[:, g, 0:SEQ], ret_o[:, g, :], ACT.Square).then_inc(gn_sq, 1)
                for g in range(2):
                    act.wait_ge(gn_var, g + 1 + l * 2)
                    A_(std[:, g, 0:SEQ], bank(2 + g), ACT.Sqrt, bias=EPS, scale=1.0 / HD).then_inc(gn_std, 1)
                for t in range(2):
                    act.wait_ge(pool_proj, t + 1 + l * 2)
                    A_(mix2[:, 2 + t, :], bank(4 + t), ACT.Identity, scale=lvec("pool_scale", t)).then_inc(pool_mix, 1)
                attention_act(act, fox_plan, o)
                norm(4 + l * 2, latent, NX1 + l * 2 * KC, 3 + l * 2, lambda c, j: mod[:, 24 + c:25 + c])
                for b in range(FFC):
                    act.wait_ge(h1_ready, b + 1 + l * FFC)
                    if b >= 2:
                        act.wait_ge(f_ready, b - 1 + l * FFC)
                    A_(squares[:, b % 2, 0:SEQ], bank(4 * (b // 2 % 2) + b % 2), ACT.Silu).then_inc(silu_ready, 1)
            norm(3 + 2 * DEPTH, latent, NX1 + 2 * KC * DEPTH - KC)

        @block.vector
        def _(dve):
            V = nc.vector

            def norm(k, parts, gain, place=None, signal=None):
                dve.drain()
                dve.wait_ge(std_ready, k + 1)
                n = sum(p[3] for p in parts)
                V.reciprocal(rstd[:, 0:n], std[:, 0, 0:n])
                dve.drain()
                for c in range(KC):
                    for j, (x, h, lo, n) in enumerate(parts):
                        ins = V.scalar_tensor_tensor(out=(place or h)[:, c, :], in0=x[:, c, :], scalar=gain(c, j),
                                                     in1=rstd[:, lo:lo + n], op0=ALU.mult, op1=ALU.mult)
                    ins.then_inc(signal or hm_ready, 1)

            both = [(xl, hl, 0, SEQ), (xc, hc, SEQ, CTX)]
            latent = both[:1]
            dve.wait_ge(vec_in, 16)
            V.tensor_scalar(qn8[:, :], vec("qn", 0, DEPTH), QSCALE, None, ALU.mult)
            swaps = 0

            def rope(slot_ap, r, cos, sin):
                tmp = probs_t[:, 0:2, :].rearrange("p a b -> p (a b)")
                dve.drain()
                dve.wait_ge(sw_ready, r + 1)
                V.tensor_tensor(tmp, bank(r_bank), sin, ALU.mult)
                V.tensor_tensor(slot_ap, slot_ap, cos, ALU.mult)
                dve.drain()
                V.tensor_tensor(slot_ap, slot_ap, tmp, ALU.add).then_inc(rope_done, 1)

            def qk_norm(l, j):
                q = 5 * l + j
                n = TOK if l < DEPTH - 1 or j == 4 else SEQ
                dve.drain()
                dve.wait_ge(qstd_ready, q + 1)
                V.reciprocal(rstd[:, 0:n], std[:, j % 2, 0:n])
                dve.drain()
                w = vec("kn", l) if j == 4 else qn8[:, l:l + 1]
                V.scalar_tensor_tensor(out=slots[:, j, 0:n], in0=slots[:, j, 0:n], scalar=w, in1=rstd[:, 0:n],
                                       op0=ALU.mult, op1=ALU.mult).then_inc(qn_done, 1)

            def double_keys():
                dve.drain()
                for kv in range(2):
                    for half in range(2):
                        ins = V.tensor_copy(slots[HD * half:HD * half + HD, 6 + kv, :], slots[HD * kv:HD * kv + HD, 4, :])
                ins.then_inc(kdup_done, 1)

            vones_by = {(0, "A"): 2, (0, "B"): 2, (0, "C"): 3, (1, "A"): 4, (1, "B"): 4, (1, "C"): 5}
            zero = Off(None)
            for l in range(DEPTH):
                dve.wait_ge(mod_taken, n_mod1[l])
                for i in range(2):
                    V.tensor_tensor(mod1[:, l, :, i], mod1[:, l, :, i], vec("ada_b", 24 * l, 24), ALU.add)
                dve.drain()
                for i in range(2):
                    V.scalar_tensor_tensor(out=gain1[:, i, :], in0=mod1[:, l, KC:2 * KC, i], scalar=1.0,
                                           in1=vec("norm_w", KC * l, KC), op0=ALU.add, op1=ALU.mult)
                dve.drain()
                norm(l, both, lambda c, j: gain1[:, j, c:c + 1])
                for m in "ABC":
                    if l == 0 and m == "A":
                        dve.wait_ge(tables_in, 96)
                    if m == "A":
                        qk_norm(l, 0)
                        for j in range(5):
                            if j < 4:
                                qk_norm(l, j + 1)
                            r_bank = j % 2
                            dve.drain()
                            rope(slots[:, j, 0:SEQ], 10 * l + j, rope_c[:, :], rope_s[:, :])
                        double_keys()
                    elif m == "C":
                        for j in range(5):
                            r_bank = j % 2
                            rope(slots[:, j, 0:SEQ], 10 * l + 5 + j, rope_c[:, :], rope_s[:, :])
                        double_keys()
                    dve.wait_ge(vones, vones_by[l, m])
                    attention_dve(dve, plans[l, m][0], zero)
                for b, n in blocks_of(l, "G"):
                    k = NSEQ[l, b]
                    dve.wait_ge(proj_taken, k + 1)
                    V.tensor_tensor(y1[:, b - 24, 0:n], y1[:, b - 24, 0:n], gate_buf[:, k % 2, 0:n], ALU.mult).then_inc(u_ready, 1)
                for o in range(KC):
                    dve.wait_ge(out_ready, KC * l + o + 1)
                    for j, (x, _, lo, n) in enumerate(both if l < DEPTH - 1 else latent):
                        ins = V.scalar_tensor_tensor(out=x[:, o, :], in0=bank(4 - 2 * j + o % 2, 0, n),
                                                     scalar=mod1[:, l, 2 * KC + o, j:j + 1], in1=x[:, o, :],
                                                     op0=ALU.mult, op1=ALU.add)
                    ins.then_inc(x_ready, 1)
            dve.drain()
            norm(2, latent, lambda c, j: vec("final_w", c), place=xl, signal=x_ready)

            dve.wait_ge(pos_in, 16)
            V.tensor_copy(angle[:, 1, :], angle[:, 0, :].bitcast(I32))
            dve.drain()
            V.tensor_scalar(angle[:, 1, :], angle[:, 1, :], vec("inv"), None, ALU.mult)
            dve.drain()
            V.tensor_scalar(angle[:, 2, :], angle[:, 1, :], 1.0 / (2 * np.pi), MAGIC, ALU.mult, ALU.add)
            dve.drain()
            V.tensor_scalar(angle[:, 2, :], angle[:, 2, :], MAGIC, None, ALU.subtract)
            dve.drain()
            for part in TWO_PI:
                V.scalar_tensor_tensor(out=angle[:, 1, :], in0=angle[:, 2, :], scalar=-part, in1=angle[:, 1, :],
                                       op0=ALU.mult, op1=ALU.add)
                dve.drain()
            V.tensor_scalar(angle[:, 0, :], angle[:, 1, :], 3.1415925, -3.1415925, ALU.min, ALU.max).then_inc(angle_done, 1)
            dve.wait_ge(sines_done, 2)
            V.tensor_scalar(rsin[:, :], rsin[:, :], vec("sign"), None, ALU.mult)
            V.tensor_tensor(rcos[:, :], rcos[:, :], rcos[:, :], ALU.mult)
            dve.drain()
            V.tensor_scalar(rcos[:, :], rcos[:, :], -2.0, 1.0, ALU.mult, ALU.add)
            dve.wait_ge(lyr_vec_in, 16)
            dve.wait_ge(pads_done, 6)
            dve.wait_ge(tables2_in, 48)
            dve.wait_ge(mod_taken, len(ada_seq))
            with dve.Fori(0, DEPTH) as l:
                o = Off(l)
                dve.drain()
                V.tensor_copy(cur[:, :], lyr[:, bass.ds(l, 1), :].rearrange("p a b -> p (a b)"))
                dve.drain()
                V.tensor_tensor(mod[:, :], mod2[:, bass.ds(l, 1), :].rearrange("p a b -> p (a b)"), lvec("ada_b", 0, 48), ALU.add)
                dve.drain()
                for i, name in enumerate(("nmix", "nffn")):
                    V.scalar_tensor_tensor(out=gain2[:, i, :], in0=mod[:, 24 * i + KC:24 * i + 2 * KC], scalar=1.0,
                                           in1=lvec(name, 0, KC), op0=ALU.add, op1=ALU.mult)
                dve.drain()
                norm(3 + l * 2, latent, lambda c, j: gain2[:, 0, c:c + 1])
                dve.wait_ge(ff_log, 1 + l)
                V.scalar_tensor_tensor(out=ft, in0=fz, scalar=0.0, in1=ft, op0=ALU.min, op1=ALU.subtract)
                dve.drain()
                V.tensor_tensor_scan(fz, ft, ft, 0.0, ALU.add, ALU.bypass)
                dve.drain()
                V.tensor_scalar(ft, fz, -1.0, None, ALU.mult).then_inc(ff_cum, 1)
                dve.wait_ge(proj_taken, NPROJ1 + 4 + l * 20)
                for t in range(2):
                    V.tensor_tensor(hpad[:, t, CONV - 1:], u2[:, t, :], u2[:, 2 + t, :], ALU.mult)
                dve.drain()
                for j in range(CONV):
                    for t in range(2):
                        w, src = lvec("conv_w", CONV * t + j), hpad[:, t, j:j + SEQ]
                        if j == 0:
                            ins = V.tensor_scalar(conv[:, t, :], src, w, lvec("conv_b", t), ALU.mult, ALU.add)
                        else:
                            ins = V.scalar_tensor_tensor(out=conv[:, t, :], in0=src, scalar=w, in1=conv[:, t, :],
                                                         op0=ALU.mult, op1=ALU.add)
                    if j < CONV - 1:
                        dve.drain()
                ins.then_inc(conv_done, 1)
                for j in range(4):
                    r_bank = j % 2
                    rope(u2[:, 4 + j, :], 10 * DEPTH + j + l * 4, rcos[:, :], rsin[:, :])
                for i in range(16):
                    n = SEQ - P * (i % 4)
                    dve.wait_ge(rs_ready, i + 1 + l * 16)
                    if i >= 4:
                        dve.wait_ge(ro_steps, i - 3 + l * 16)
                    V.tensor_tensor(ret_s[:, i % 4, 0:n], bank(4 + i % 4, 0, n), decay[:, i // 4, 0:n], ALU.mult).then_inc(rs_done, 1)
                dve.wait_ge(ln_sum, 1 + l)
                for t in range(2):
                    V.scalar_tensor_tensor(out=conv[:, t, :], in0=bank(6), scalar=-1.0 / 256, in1=conv[:, t, :],
                                           op0=ALU.mult, op1=ALU.add).then_inc(ln_dev, 1)
                for g in range(2):
                    dve.wait_ge(gn_sum, g + 1 + l * 2)
                    V.scalar_tensor_tensor(out=ret_o[:, g, :], in0=bank(2 + g), scalar=-1.0 / HD, in1=ret_o[:, g, :],
                                           op0=ALU.mult, op1=ALU.add).then_inc(gn_dev, 1)
                dve.wait_ge(ln_std, 1 + l)
                V.reciprocal(rstd[:, 0:SEQ], std[:, 0, 0:SEQ])
                dve.drain()
                for t in range(2):
                    V.tensor_tensor(conv[:, t, :], conv[:, t, :], rstd[:, 0:SEQ], ALU.mult).then_inc(ln_norm, 1)
                for g in range(2):
                    dve.wait_ge(gn_std, g + 1 + l * 2)
                    V.reciprocal(rstd[:, 0:SEQ], std[:, g, 0:SEQ])
                    dve.drain()
                    V.scalar_tensor_tensor(out=ret_o[:, g, :], in0=ret_o[:, g, :], scalar=lvec("gn", g), in1=rstd[:, 0:SEQ],
                                           op0=ALU.mult, op1=ALU.mult)
                    dve.drain()
                    V.tensor_tensor(mix2[:, 4 + g, :], ret_o[:, g, :], u2[:, 10 + g, :], ALU.mult).then_inc(ret_mix, 1)
                attention_dve(dve, fox_plan, o)
                for i in range(KC):
                    dve.wait_ge(out_ready, DEPTH * KC + i + 1 + l * 2 * KC)
                    V.scalar_tensor_tensor(out=xl[:, i, :], in0=bank(i % 2), scalar=mod[:, 16 + i:17 + i], in1=xl[:, i, :],
                                           op0=ALU.mult, op1=ALU.add).then_inc(x_ready, 1)
                dve.drain()
                norm(4 + l * 2, latent, lambda c, j: gain2[:, 1, c:c + 1])
                for b in range(FFC):
                    dve.wait_ge(silu_ready, b + 1 + l * FFC)
                    dve.wait_ge(h3_ready, b + 1 + l * FFC)
                    V.tensor_tensor(act2[:, b, :], squares[:, b % 2, 0:SEQ], bank(4 * (b // 2 % 2) + 2 + b % 2), ALU.mult).then_inc(f_ready, 1)
                for i in range(KC):
                    dve.wait_ge(out_ready, DEPTH * KC + KC + i + 1 + l * 2 * KC)
                    V.scalar_tensor_tensor(out=xl[:, i, :], in0=bank(i % 4), scalar=mod[:, 40 + i:41 + i], in1=xl[:, i, :],
                                           op0=ALU.mult, op1=ALU.add).then_inc(x_ready, 1)
            dve.drain()
            norm(3 + 2 * DEPTH, latent, lambda c, j: vec("final_g", c), signal=result_ready)

        @block.tensor
        def _(pe):
            mm = nc.tensor.matmul

            def make_mod(p):
                n, k = number[p], ada_no[p]
                panel_wait(pe, n)
                if k >= 2:
                    pe.wait_ge(mod_taken, k - 1)
                nv = 2 if p[0] == ADA1 else 1
                for b in range(2):
                    for c in range(KC):
                        rhs = silu_c[:, c, :] if nv == 2 else silu_c2[:, c:c + 1]
                        ins = mm(bank(4 + k % 2, nv * b, nv * b + nv), slot(n)[:, c, P * b:P * b + P], rhs, start=c == 0, stop=c == KC - 1)
                ins.then_inc(mod_ready, 1)

            def norm(k, parts):
                for c in range(KC):
                    pe.wait_ge(sq_ready, 8 * k + c + 1)
                    for j, (_, _, lo, n) in enumerate(parts):
                        ins = mm(bank(6 + j, 0, n), ones, squares[:, c % 2, lo:lo + n], start=c == 0, stop=c == KC - 1)
                    ins.then_inc(sq_summed, 1)

            both = [(xl, hl, 0, SEQ), (xc, hc, SEQ, CTX)]
            latent = both[:1]
            pe.wait_ge(silu_done, 2)
            for i in range(N_ADA1):
                make_mod((ADA1, 0, i))
            pe.wait_ge(mats_in, 16)

            def project(l, m):
                for b, n in blocks_of(l, m):
                    k, pn = NSEQ[l, b], number[IN1, l, b // 2]
                    if b % 2 == 0:
                        panel_wait(pe, pn)
                    if k >= 2:
                        pe.wait_ge(proj_taken, k - 1)
                    for c in range(KC):
                        if b == 0:
                            pe.wait_ge(h_ready, KC * l + c + 1)
                        w = slot(pn)[:, c, P * (b % 2):P * (b % 2) + P]
                        ins = mm(bank(k % 2), w, hl[:, c, :], start=c == 0, stop=c == KC - 1)
                    if n == TOK:
                        for c in range(KC):
                            w = slot(pn)[:, c, P * (b % 2):P * (b % 2) + P]
                            ins = mm(bank(2 + k % 2, 0, CTX), w, hc[:, c, :], start=c == 0, stop=c == KC - 1)
                    ins.then_inc(proj_ready, 1)
                    if b % 2 == 1:
                        for p in spare[l][b - 1:b + 1]:
                            make_mod(p)
                pe.wait_ge(proj_taken, k + 1)
                pe.wait_ge(mod_taken, N_ADA1 + sum(len(spare[i][:W_IN // P]) for i in range(l)) + len(spare[l][:b + 1]))

            def head_sums(l, j):
                q = 5 * l + j
                pe.wait_ge(qsq_ready, q + 1)
                if q >= 2:
                    pe.wait_ge(qstd_ready, q - 1)
                b = 4 + 2 * (j % 2)
                ins = mm(bank(b), pairs, squares[:, j % 2, 0:SEQ], start=True, stop=True)
                if l < DEPTH - 1 or j == 4:
                    ins = mm(bank(b + 1, 0, CTX), pairs, squares[:, j % 2, SEQ:TOK], start=True, stop=True)
                ins.then_inc(qsum_ready, 1)

            def swap_halves(src, r, j):
                if not isinstance(r, int) or r >= 2:
                    pe.wait_ge(rope_done, r - 1)
                mm(bank(j % 2), swap, src, start=True, stop=True).then_inc(sw_ready, 1)

            zero = Off(None)
            for l in range(DEPTH):
                norm(l, both)
                for m in "ABC":
                    project(l, m)
                    if m == "A":
                        head_sums(l, 0)
                        for j in range(5):
                            if j < 4:
                                head_sums(l, j + 1)
                            pe.wait_ge(qn_done, 5 * l + j + 1)
                            swap_halves(slots[:, j, 0:SEQ], 10 * l + j, j)
                    elif m == "C":
                        for j in range(5):
                            swap_halves(slots[:, j, 0:SEQ], 10 * l + 5 + j, j)
                    if m != "B":
                        pe.wait_ge(kdup_done, 2 * l + (1 if m == "A" else 2))
                    attention_pe(pe, plans[l, m][0], zero)
                    pe.wait_ge(y_done, plans[l, m][1])
                project(l, "G")
                for o in range(KC):
                    pn = number[OUT1, l, o]
                    panel_wait(pe, pn)
                    k = KC * l + o
                    if o >= 2:
                        pe.wait_ge(x_ready, k - 1)
                    for j, (_, _, lo, n) in enumerate(both if l < DEPTH - 1 else latent):
                        for c in range(MIXC):
                            if o == 0:
                                pe.wait_ge(u_ready, MIXC * l + c + 1)
                            ins = mm(bank(4 - 2 * j + o % 2, 0, n), slot(pn, 16)[:, c, :], y1[:, c, lo:lo + n],
                                     start=c == 0, stop=c == MIXC - 1)
                    ins.then_inc(out_ready, 1)
            norm(2, latent)

            pe.wait_ge(tables2_in, 48)
            pe.wait_ge(pads_done, 6)
            with pe.Fori(0, DEPTH) as l:
                o = Off(l)
                hbase = DEPTH * KC + l * 2 * KC
                norm(3 + l * 2, latent)
                pe.wait_ge(lyr_in, 32 + l * 32)
                for c in range(KC):
                    pe.wait_ge(h_ready, hbase + c + 1)
                    ins = mm(bank(3)[0:4], ffw[:, c, :], hl[:, c, :], start=c == 0, stop=c == KC - 1)
                ins.then_inc(ff_ready, 1)
                for m in range(20):
                    n = N1 + m // 2
                    if m % 2 == 0:
                        panel_wait(pe, n, l)
                    pe.wait_ge(proj_taken, NPROJ1 + m - 1 + l * 20)
                    for c in range(KC):
                        ins = mm(bank(m % 2), slot(n)[:, c, P * (m % 2):P * (m % 2) + P], hl[:, c, :], start=c == 0, stop=c == KC - 1)
                    ins.then_inc(proj_ready, 1)
                pe.wait_ge(proj_taken, NPROJ1 + 20 + l * 20)
                for j in range(4):
                    swap_halves(u2[:, 4 + j, :], 10 * DEPTH + j + l * 4, j)
                pe.wait_ge(ff_log, 1 + l)
                for g in range(2):
                    for t in range(4):
                        ins = nc.tensor.transpose(bank(2 + g, P * t, P * t + P), u2[:, 8 + g, P * t:P * t + P], ident)
                    ins.then_inc(rv_ready, 1)
                pe.wait_ge(rope_done, 10 * DEPTH + 4 + l * 4)
                pe.wait_ge(rv_taken, 2 + l * 2)

                def decayed(i):
                    g, h, t = i // 8, i // 4, i % 4
                    n = SEQ - P * t
                    pe.wait_ge(rs_done, i + 1 + l * 16)
                    mm(bank(g, P * t, 512), pv_pair(vret[:, g, t, :], h), ret_s[:, i % 4, 0:n], start=i % 8 == 0, stop=i % 8 == 7,
                       skip_group_check=True).then_inc(ro_steps, 1)

                for i in range(16):
                    g, h, t = i // 8, i // 4, i % 4
                    r, n = rows_of(h), SEQ - P * t
                    if i >= 4:
                        pe.wait_ge(rs_done, i - 3 + l * 16)
                    mm(bank(4 + i % 4, 0, n), u2[r, 6 + g, P * t:P * t + P], u2[r, 4 + g, P * t:SEQ], start=True, stop=True).then_inc(rs_ready, 1)
                    if i >= 2:
                        decayed(i - 2)
                decayed(14)
                decayed(15)
                pe.wait_ge(conv_done, 1 + l)
                for t in range(2):
                    ins = mm(bank(6), ones, conv[:, t, :], start=t == 0, stop=t == 1)
                ins.then_inc(ln_sum, 1)
                for g in range(2):
                    pe.wait_ge(ro_taken, g + 1 + l * 2)
                    mm(bank(2 + g), pairs, ret_o[:, g, :], start=True, stop=True).then_inc(gn_sum, 1)
                for t in range(2):
                    pe.wait_ge(ln_sq, t + 1 + l * 2)
                    ins = mm(bank(7), ones, squares[:, t, 0:SEQ], start=t == 0, stop=t == 1)
                ins.then_inc(ln_var, 1)
                for g in range(2):
                    pe.wait_ge(gn_sq, g + 1 + l * 2)
                    mm(bank(2 + g), pairs, squares[:, g, 0:SEQ], start=True, stop=True).then_inc(gn_var, 1)
                pe.wait_ge(pool_done, 1 + l)
                for t in range(2):
                    mm(bank(4 + t), poolw[:, t, :], pooled[:, t, :], start=True, stop=True).then_inc(pool_proj, 1)
                pe.wait_ge(pool_mix, 2 + l * 2)
                pe.wait_ge(ret_mix, 2 + l * 2)
                pe.wait_ge(conv_mix, 2 + l * 2)
                pe.wait_ge(aug_in, 128 + l * 128)
                attention_pe(pe, fox_plan, o)
                pe.wait_ge(y_done, at["u"] + o.u)
                for i in range(KC):
                    n = N1 + N_IN2 + i // 2
                    if i % 2 == 0:
                        panel_wait(pe, n, l)
                    if i >= 2:
                        pe.wait_ge(x_ready, NX1 + i - 1 + l * 2 * KC)
                    for c in range(KC):
                        ins = mm(bank(i % 2), slot(n)[:, c, P * (i % 2):P * (i % 2) + P], mix2[:, c, :], start=c == 0, stop=c == KC - 1)
                    ins.then_inc(out_ready, 1)
                norm(4 + l * 2, latent)
                for i in range(N_FF):
                    for w, ready in ((0, h1_ready), (1, h3_ready)):
                        n = N1 + N_IN2 + N_OUT2 + 2 * i + w
                        panel_wait(pe, n, l)
                        if i >= 2 and w == 0:
                            pe.wait_ge(f_ready, 2 * i - 2 + l * FFC)
                        for b in range(2):
                            for c in range(KC):
                                if i == 0 and w == 0 and b == 0:
                                    pe.wait_ge(h_ready, hbase + KC + c + 1)
                                ins = mm(bank(4 * (i % 2) + 2 * w + b), slot(n)[:, c, P * b:P * b + P], hl[:, c, :],
                                         start=c == 0, stop=c == KC - 1)
                            ins.then_inc(ready, 1)
                pe.wait_ge(f_ready, FFC + l * FFC)
                for g in range(N_OUT2):
                    if g >= 2:
                        pe.wait_ge(x_ready, NX1 + KC + 2 * g - 2 + l * 2 * KC)
                    for j, (a, e) in enumerate(W2_CUT):
                        n = N1 + N_IN2 + N_OUT2 + 2 * N_FF + len(W2_CUT) * g + j
                        panel_wait(pe, n, l)
                        for b in range(2):
                            for c in range(a, e):
                                ins = mm(bank(2 * (g % 2) + b), slot(n)[:, c - a, P * b:P * b + P], act2[:, c, :],
                                         start=c == 0, stop=c == FFC - 1)
                            if j == len(W2_CUT) - 1:
                                ins.then_inc(out_ready, 1)
                        if j < len(W2_CUT) - 1:
                            ins.then_inc(w2_used, 1)
            norm(3 + 2 * DEPTH, latent)


_hi = float(np.float32(np.round(2 * np.pi * 128) / 128))
_mid = float(np.float32(np.round((2 * np.pi - _hi) * 2.0 ** 19) / 2.0 ** 19))
TWO_PI = (_hi, _mid, float(np.float32(2 * np.pi - _hi - _mid)))


def _tables():
    t = np.arange(SEQ)
    d = np.arange(P) % HD
    freq = 10000.0 ** (-np.arange(16) / 16.0)
    ang = np.concatenate([(t // GRID)[:, None] * freq, (t % GRID)[:, None] * freq], axis=1).T
    rope = np.stack([np.cos(ang)[d % 32], np.where(d < 32, -1.0, 1.0)[:, None] * np.sin(ang)[d % 32]], axis=1)
    i = np.arange(P)
    mats = np.stack([np.eye(P), i[:, None] == (i ^ 32)[None, :], i[:, None] == (ROWS - 1 - i % ROWS)[None, :] * NBC + (NBC - 1 - i // ROWS)[None, :],
                     i[:, None] // HD == i[None, :] // HD, np.ones((P, P))], axis=1)
    bmask = np.zeros((P, 3, SEQ))
    cl, j = np.arange(P) // ROWS, np.arange(BAND)
    for v, lo in enumerate((np.maximum(cl - 8, 0), cl, np.minimum(cl + 8, 16))):
        seen = (j[None, :] >= lo[:, None]) & (j[None, :] < lo[:, None] + NBC)
        bmask[:, v, CTX:] = np.repeat(np.where(seen, 0.0, NEG), ROWS, axis=1)
    cmask = np.zeros((P, 641))
    cmask[:, 0:P] = np.where(i[None, :] >= i[:, None], 0.0, NEG)
    cmask[:, 512:640] = np.where(i[None, :] <= i[:, None], 0.0, NEG)
    fmask = np.where(i[None, :] <= i[:, None], 0.0, NEG)
    lg = np.log(1.0 - 2.0 ** (-5.0 - np.arange(4)))
    diff = np.arange(SEQ)[None, :] - i[:, None]
    decay = np.stack([np.where(diff >= 0, np.exp(g * np.maximum(diff, 0)), 0.0) for g in lg], axis=1)
    counts = np.zeros((P, 2, SEQ))
    for g, w in enumerate((2, 4, 8, 16)):
        counts[HD * (g % 2):HD * (g % 2) + HD, g // 2] = 1.0 / np.minimum(t + 1, w)
    sink_lhs = np.zeros((1, 192))
    sink_lhs[:, 0:64] = sink_lhs[:, 128:192] = 1.0
    inv = 10000.0 ** (-(d % 32) / 32.0)
    sign = np.where(d < 32, -1.0, 1.0)
    f = lambda a: np.ascontiguousarray(a, dtype=np.float32)
    return {k: f(v) for k, v in dict(rope=rope, mats=mats, bmask=bmask, cmask=cmask, fmask=fmask, decay=decay,
                                     counts=counts, sink_lhs=sink_lhs, inv=inv, sign=sign).items()}


def _features(v):
    return np.ascontiguousarray(v.reshape(-1, P).T)


def _panels(w, chunks, cols):
    L, _, n = w.shape
    return np.ascontiguousarray(
        w.reshape(L, chunks, P, n // cols, cols).transpose(0, 3, 2, 1, 4)).reshape(L, n // cols, P, chunks * cols)


def _layout(a):
    t = _tables()
    dup = lambda v: np.concatenate([v, v], axis=1).T
    c = np.stack([_features(a["c"]), _features(a["c_ctx"])], axis=2).reshape(P, 2 * KC)
    prm = np.concatenate([c, _features(a["c_2"]), _features(a["ada_b"]), _features(a["norm_w"]), _features(a["final_norm_w"]),
                          dup(a["q_norm_a"]), dup(a["k_norm_a"]), _features(a["final_g_2"]),
                          t["inv"][:, None], t["sign"][:, None]], axis=1)
    lyr = []
    for l in range(DEPTH):
        fb = np.zeros((P, 1), a["fox_fb_2"].dtype)
        fb[0:4, 0] = a["fox_fb_2"][l]
        conv_w = a["conv_w_2"][l].reshape(CONV, 2, P).transpose(2, 1, 0).reshape(P, 2 * CONV)
        lyr.append(np.concatenate([_features(a[k][l]) for k in (
            "ada_b_2", "norm_mix_g_2", "norm_ffn_g_2", "pool_scale_2", "ret_gn_g_2", "conv_b_2", "conv_ln_g_2", "conv_ln_b_2")]
            + [conv_w, fb], axis=1))
    w2in = a["w_in_2"]
    at = dict(fq=0, fk=256, fv=512, pu=772, rq=1028, rk=1284, rv=1540, rg=1796, ca=2052, cg=2308)
    order = ("ca", "cg", "rq", "rk", "rv", "rg", "pu", "fq", "fk", "fv")
    in2 = np.concatenate([w2in[:, :, at[k]:at[k] + 256] for k in order], axis=2)
    ffw = w2in[:, :, 768:772].reshape(DEPTH, KC, P, 4).transpose(0, 2, 1, 3).reshape(DEPTH, P, KC * 4)
    poolw = np.zeros((DEPTH, P, 2, P), a["pool_w_2"].dtype)
    for g in range(4):
        r = slice(HD * (g % 2), HD * (g % 2) + HD)
        poolw[:, r, g // 2, r] = a["pool_w_2"][:, g]
    rpb = np.zeros((DEPTH, HEADS, 15, 64), a["rpb_b"].dtype)
    rpb[:, :, :, 16:47] = a["rpb_b"]
    feat = lambda x: x[0].T.reshape(KC, P, -1).transpose(1, 0, 2)
    arrays = dict(
        prm=prm, lyr=np.stack(lyr, axis=1), x=feat(a["x"]), ctx=feat(a["ctx"]), rpb=rpb,
        sinks=a["sink_c"].reshape(1, -1), pos=a["positions_2"].reshape(1, SEQ),
        ada1=_panels(a["ada_w"], KC, PAN), in1=_panels(a["w_in"], KC, PAN), out1=_panels(a["w_out"], MIXC, P),
        ada2=_panels(a["ada_w_2"], KC, PAN), in2=_panels(in2, KC, PAN), out2=_panels(a["w_out_2"], KC, PAN),
        w1=_panels(a["ffn_w1_2"], KC, PAN), w3=_panels(a["ffn_w3_2"], KC, PAN), w2=_panels(a["ffn_w2_2"], FFC, PAN),
        ffw=ffw, poolw=poolw.reshape(DEPTH, P, 2 * P),
        **{k: t[k] for k in ("rope", "mats", "bmask", "cmask", "fmask", "decay", "counts", "sink_lhs")})
    return {k: np.ascontiguousarray(v) for k, v in arrays.items()}


def kernel(**inputs):
    import concourse.bacc as bacc
    from concourse.bass_utils import run_bass_kernel_spmd

    arrays = {f"in_{k}": v for k, v in _layout({k: np.asarray(v) for k, v in inputs.items()}).items()}
    nc = bacc.Bacc("TRN2", target_bir_lowering=False, num_devices=1)
    dram = {k[3:]: nc.dram_tensor(k, v.shape, mybir.dt.from_np(v.dtype), kind="ExternalInput").ap() for k, v in arrays.items()}
    out = nc.dram_tensor("out_features", (P, KC, SEQ), F32, kind="ExternalOutput").ap()
    two_dit_blocks(nc, dram, out)
    got = run_bass_kernel_spmd(nc, [arrays], core_ids=[0]).results[0]["out_features"]
    return np.ascontiguousarray(got.transpose(2, 1, 0).reshape(1, SEQ, DM))
```

```python
from contextlib import ExitStack

import numpy as np

import concourse.bass as bass
from concourse import mybir

F32 = mybir.dt.float32
I32 = mybir.dt.int32
ACT = mybir.ActivationFunctionType
ALU = mybir.AluOpType
AX_X = mybir.AxisListType.X

P = 128
DM = 1024
KC = DM // P
SEQ, CTX = 512, 256
TOK = SEQ + CTX
DEPTH = 2
HD = 64
GRID = 64
ROWS = SEQ // GRID
NBC = 16
BAND_AT = (0, 8, 24, 32)
BAND = 32
NOT_SEEN = 1.0e30
HIGHEST = 3.0e38
EPS = 1e-6
QSCALE = HD ** -0.5
HEADS = 8

PAN = 256
W_IN = 4608
N_IN1 = W_IN // PAN
N_ADA1 = 3 * DM // PAN
N_SS1 = 2 * DM // PAN
N_ADA2 = 6 * DM // PAN
MIXC = 12
RING = 4
FF = 2816
FFC = FF // P
N_FF = FF // PAN
N_IN2 = 10
N_OUT2 = DM // PAN
W2_CUT = [(0, 8), (8, 15), (15, 22)]
PER2 = N_IN2 + N_OUT2 + 2 * N_FF + N_OUT2 * len(W2_CUT)
assert PER2 % RING == 0
CONV = 31
POOLPAD = 16
MAGIC = 1.5 * 2.0 ** 23
PHASES = {"A": (0, 6), "B": (6, 18), "C": (18, 24), "G": (24, W_IN // P)}

PRM = {}
_at = 0
for _name, _n in (("c", 2 * KC), ("c2", KC), ("ada_b", DEPTH * 24), ("norm_w", DEPTH * KC), ("final_w", KC),
                  ("qn", DEPTH), ("kn", DEPTH), ("final_g", KC), ("inv", 1), ("sign", 1)):
    PRM[_name] = (_at, _n)
    _at += _n
N_PRM = _at
LYR = {}
_at = 0
for _name, _n in (("ada_b", 48), ("nmix", KC), ("nffn", KC), ("pool_scale", 2), ("gn", 2), ("conv_b", 2),
                  ("ln_g", 2), ("ln_b", 2), ("conv_w", 2 * CONV), ("fox_b", 1)):
    LYR[_name] = (_at, _n)
    _at += _n
N_LYR = _at


def make_plan(groups, at):
    plan, waiting = [], None
    base = dict(at)
    turns_seen = []

    def turn(kind, count, **more):
        ev = dict(kind=kind, i=len(turns_seen), t=at["t"], n=at[count], **more)
        if len(turns_seen) >= 2:
            ev["before"] = turns_seen[-2]
        turns_seen.append(ev)
        plan.append(ev)
        at["t"] += 1
        at[count] += 1

    def behind(lo, hi):
        u = waiting
        for j in range(lo, hi):
            turn("T", "v", unit=u, steps=u["events"][j], first=j == 0, last=j == len(u["events"]) - 1)
            u["t_last"], u["v_last"] = at["t"] - 1, at["v"] - 1

    def finish():
        plan.append(dict(kind="Y", unit=waiting))
        if waiting.get("closes") is not None:
            v_end.append(waiting["v_last"] + 1)

    v_end = []
    for g, (turns, units) in enumerate(groups):
        for srcs, dst in turns:
            turn("V", "w", src=srcs, dst=dst, need_group=g - 2, v_end=v_end)
        seen = at["w"]
        for u in units:
            u["u"], u["local"], u["turned"] = at["u"], at["u"] - base["u"], seen
            at["u"] += 1
            u["events"], width = [[]], 0
            for step in u["steps"]:
                if width + P * len(step[1]) > 512:
                    u["events"].append([])
                    width = 0
                u["events"][-1].append(step)
                width += P * len(step[1])
            n = len(waiting["events"]) if waiting else 0
            k = len(u["q"])
            for qb in range(k):
                plan.append(dict(kind="S", s=at["s"], local=at["s"] - base["s"], unit=u, qb=qb))
                u["s_last"], u["s_last_local"] = at["s"], at["s"] - base["s"]
                at["s"] += 1
                if waiting:
                    behind(n * qb // k, n * (qb + 1) // k)
            if waiting:
                finish()
            waiting = u
        units[-1]["closes"] = g
    behind(0, len(waiting["events"]))
    finish()
    return plan


def two_dit_blocks(nc, dram, out):
    with ExitStack() as ctx:
        def sb(name, shape, dt=F32, scope=ctx):
            return scope.enter_context(nc.sbuf_tensor(name, shape, dt))

        def sem(name):
            return ctx.enter_context(nc.semaphore(name))

        xl = sb("x_latent", [P, KC, SEQ])
        hl = sb("h_latent", [P, KC, SEQ])
        ring = sb("panel_ring", [P, RING, KC * PAN])
        prm = sb("vectors", [P, N_PRM])
        lyr = sb("layer_vectors", [P, DEPTH, N_LYR])
        mats = sb("matrices", [P, 5, P])
        ident, swap, minus_turn, pairs, ones = (mats[:, i, :] for i in range(5))
        silu_c = sb("silu_c", [P, KC, 2])
        silu_c2 = sb("silu_c2", [P, KC])
        mod1 = sb("mod_first", [P, DEPTH, 24, 2])
        mod2 = sb("mod_second", [P, DEPTH, 48])
        gain1 = sb("gain_first", [P, 2, KC])
        rstd = sb("rstd", [P, TOK])
        probs = sb("probs", [P, 2, 2, TOK])
        squares, std = probs[:, 0, :, :], probs[:, 1, :, :]
        probs_t = sb("probs_turned", [P, 2, 512])
        row_min = sb("row_min", [P, 4])
        row_sum = sb("row_sum", [P, 4])
        weight = sb("row_weight", [P, 4])
        diag = sb("diagonal_weights", [P, 4, P])
        sinks = sb("sinks", [1, DEPTH * HEADS])
        minus_one = sb("minus_one", [1, P])
        qn8 = sb("minus_q_norm_scaled", [P, DEPTH])

        first, second = ExitStack(), ExitStack()
        with first:
            f = lambda *a: sb(*a, scope=first)
            xc = f("x_context", [P, KC, CTX])
            hc = f("h_context", [P, KC, CTX])
            y1 = f("mixed_first", [P, MIXC, TOK])
            slots = f("qkv", [P, 12, TOK])
            vband = f("values_band", [P, 2, 10, P])
            bias = f("bias_rows", [P, 2, ROWS, 48])
            rope_c = f("rope_cos", [P, SEQ])
            rope_s = f("rope_sin", [P, SEQ])
            bmask = f("band_masks", [P, 4, CTX])
            cmask = f("window_mask", [P, 641])
        vseq = slots[:, 9:11, :].rearrange("p a (b c) -> p (a b c)", c=P).rearrange(
            "p (t g c) -> p t g c", t=6, g=2)
        with second:
            f = lambda *a: sb(*a, scope=second)
            mix2 = f("mixed_second", [P, KC, SEQ])
            act2 = f("ffn_hidden", [P, FFC, SEQ])
            u2 = act2[:, 0:20, :]
            vret = f("values_retention", [P, 2, 4, 192])
            vfox = f("values_forgetting", [P, 2, 4, P])
            ret_s = f("decayed_scores", [P, 4, SEQ])
            hpad = f("conv_in", [P, 2, CONV - 1 + SEQ])
            ppad = f("pool_in", [P, 2, POOLPAD + SEQ])
            psums = f("pool_sums", [P, 2, POOLPAD + SEQ])
            fmask = f("causal_mask", [P, P])[:, :]
            decay = f("decay", [P, 4, SEQ])
            counts = f("pool_counts", [P, 2, SEQ])
            rcos = f("ret_cos", [P, SEQ])
            rsin = f("ret_sin", [P, SEQ])
            poolw = f("pool_weights", [P, 2, P])
            ffw = f("forget_weights", [P, KC, 4])
            cur = f("this_layers_vectors", [P, N_LYR])
            mod = f("this_layers_mod", [P, 48])
            gain2 = f("gain_second", [P, 2, KC])
            augq = f("decay_of_queries", [P, SEQ])
            augk = f("decay_of_keys", [P, SEQ])
        conv = u2[:, 0:2, :]
        ret_o = u2[:, 4:6, :]
        pooled = u2[:, 12:14, :]
        angle = u2[:, 16:20, :]
        fz, ft = act2[0:4, 20, :], act2[0:4, 21, :]
        gate_buf = squares
        parts = std[:, :, 0:2 * PAN].rearrange("p k (v n) -> p k v n", v=2)

        ps = ctx.enter_context(nc.psum_tensor("ps", [P, 4096], F32))
        bank = lambda b, a=0, e=512: ps[:, 512 * b + a:512 * b + e]

        vec_in, mats_in, x_in, tables_in, lyr_vec_in = (
            sem(n) for n in ("vec_in", "mats_in", "x_in", "tables_in", "lyr_vec_in"))
        panel_in = [sem(f"panel_in{i}") for i in range(RING)]
        silu_done = sem("silu_done")
        part_ready, mod_ready, mod_taken = sem("part_ready"), sem("mod_ready"), sem("mod_taken")
        x_ready = sem("x_ready")
        sq_ready, sq_summed, std_ready = sem("sq_ready"), sem("sq_summed"), sem("std_ready")
        hm_ready, h_ready = sem("hm_ready"), sem("h_ready")
        proj_ready, proj_taken = sem("proj_ready"), sem("proj_taken")
        qsq_ready, qsum_ready, qstd_ready, qn_done = (
            sem(n) for n in ("qsq_ready", "qsum_ready", "qstd_ready", "qn_done"))
        sw_ready, rope_done, kdup_done = sem("sw_ready"), sem("rope_done"), sem("kdup_done")
        bias_in = [sem("bias_in0"), sem("bias_in1")]
        s_ready, max_ready, exp_done, diag_ready = (sem(n) for n in ("s_ready", "max_ready", "exp_done", "diag_ready"))
        turned, pt_taken, values_taken = sem("turned"), sem("pt_taken"), sem("values_taken")
        pv_steps, y_done = sem("pv_steps"), sem("y_done")
        u_ready = sem("u_ready")
        out_ready = sem("out_ready")
        tables2_in, pos_in, pads_done = sem("tables2_in"), sem("pos_in"), sem("pads_done")
        angle_done, sines_done, ret_trig = sem("angle_done"), sem("sines_done"), sem("ret_trig")
        lyr_in, cur_done = sem("lyr_in"), sem("cur_done")
        conv_done, ln_sum, ln_dev, ln_sq, ln_var, ln_std, ln_norm, conv_mix = (
            sem(n) for n in ("conv_done", "ln_sum", "ln_dev", "ln_sq", "ln_var", "ln_std", "ln_norm", "conv_mix"))
        rv_ready, rv_taken = sem("rv_ready"), sem("rv_taken")
        rs_ready, rs_done, ro_steps, ro_taken = (sem(n) for n in ("rs_ready", "rs_done", "ro_steps", "ro_taken"))
        gn_sum, gn_dev, gn_sq, gn_var, gn_std, ret_mix = (
            sem(n) for n in ("gn_sum", "gn_dev", "gn_sq", "gn_var", "gn_std", "ret_mix"))
        pool_done, pool_proj, pool_mix = sem("pool_done"), sem("pool_proj"), sem("pool_mix")
        ff_ready, ff_log, ff_cum, aug_in = sem("ff_ready"), sem("ff_log"), sem("ff_cum"), sem("aug_in")
        h1_ready, h3_ready, silu_ready, f_ready = (
            sem(n) for n in ("h1_ready", "h3_ready", "silu_ready", "f_ready"))
        w2_used = sem("w2_used")
        result_ready, result_out = sem("result_ready"), sem("result_out")

        def vec(name, i=0, n=1):
            return prm[:, PRM[name][0] + i:PRM[name][0] + i + n]

        def lvec(name, i=0, n=1):
            return cur[:, LYR[name][0] + i:LYR[name][0] + i + n]

        MA, MB, MC = 0, 6, 18
        rows_of = lambda h: slice(HD * (h % 2), HD * (h % 2) + HD)

        def pv_pair(tile, h):
            return tile[:, 0:P] if h % 2 == 0 else tile[:, HD:HD + P]

        def seq_units(mixer, l):
            units = []
            for h in range(HEADS):
                kv, r = h // 4, rows_of(h)
                q, k = slots[r, h // 2, :], slots[r, 6 + kv, :]
                y = y1[r, (0 if mixer == "A" else 8) + h // 2, :]
                sink = [(sinks[:, l * HEADS + h:l * HEADS + h + 1])] if mixer == "C" else []
                for pair in range(2):
                    qbs = [2 * pair, 2 * pair + 1]
                    u = dict(h=h, q=[q[:, P * b:P * b + P] for b in qbs], seg=[], extra=[], w=[], mask=[], steps=[],
                             dst=y[:, 256 * pair:256 * pair + 256])
                    cols = []
                    for b in qbs:
                        if mixer == "A":
                            u["seg"].append([(0, k[:, 0:SEQ]), (SEQ, k[:, SEQ:TOK])])
                            u["w"].append(TOK)
                            u["mask"].append(None)
                            u["extra"].append([])
                            cols.append({t: P * t for t in range(6)})
                            continue
                        at, seg, col = 0, [], {}
                        if b > 0:
                            seg.append((0, k[:, P * (b - 1):P * b]))
                            col[b - 1] = 0
                            at = P
                        seg.append((at, k[:, SEQ:TOK]))
                        col[4], col[5] = at, at + P
                        at += CTX
                        for t in range(b, min(b + 2, 4)):
                            seg.append((at, k[:, P * t:P * t + P]))
                            col[t] = at
                            at += P
                        u["seg"].append(seg)
                        u["extra"].append([(at, minus_one[:, :], sink[0], True)])
                        u["w"].append(at + 1)
                        first_col = 0 if b > 0 else P
                        u["mask"].append(cmask[:, first_col:first_col + at + 1])
                        cols.append(col)
                    for t in [4, 5, 0, 1, 2, 3]:
                        has = [i for i in range(2) if t in cols[i]]
                        if has:
                            u["steps"].append((vseq[:, t, kv, :], [(i, cols[i][t]) for i in has]))
                    units.append(u)
            return units

        def context_units(mixer, l):
            units = []
            for h in range(HEADS):
                r = rows_of(h)
                if mixer == "B":
                    q, k, y0 = slots[r, h // 2, :], slots[r, 4 + h // 2, :], 4
                else:
                    q, k, y0 = slots[r, h // 2, :], slots[r, 6 + h // 4, :], 0 if mixer == "A" else 8
                u = dict(h=h, q=[], seg=[], extra=[], w=[], mask=[], steps=[],
                         dst=y1[r, y0 + h // 2, SEQ:TOK])
                for b in range(2):
                    u["q"].append(q[:, SEQ + P * b:SEQ + P * b + P])
                    u["seg"].append([(0, k[:, SEQ:TOK])])
                    u["mask"].append(None)
                    u["extra"].append([(CTX, minus_one[:, :], sinks[:, l * HEADS + h:l * HEADS + h + 1], True)]
                                      if mixer == "C" else [])
                    u["w"].append(CTX + 1 if mixer == "C" else CTX)
                for t in range(2):
                    lhs = vband[:, h // 2 % 2, t, :] if mixer == "B" else vseq[:, 4 + t, h // 4, :]
                    u["steps"].append((lhs, [(0, P * t), (1, P * t)]))
                units.append(u)
            return units

        def grid(ap):
            return ap.rearrange("p (r c) -> p r c", c=GRID)

        def band_units(h, l):
            r = rows_of(h)
            q, k = slots[r, h // 2, :], slots[r, 4 + h // 2, :]
            y = grid(y1[r, 4 + h // 2, 0:SEQ])
            units = []
            for pair in range(2):
                u = dict(h=h, q=[], seg=[], extra=[], w=[], mask=[], steps=[], bias=(l * HEADS + h) if pair == 0 else None,
                         dst=y[:, :, 32 * pair:32 * pair + 32].rearrange("p r c -> p c r"))
                for i in range(2):
                    b = 2 * pair + i
                    k0 = BAND_AT[b]
                    off = NBC + BAND_AT[b] - NBC * b
                    u["q"].append(q[:, P * b:P * b + P])
                    u["seg"].append([(0, k[:, SEQ:TOK]), (CTX, k[:, ROWS * k0:ROWS * (k0 + BAND)])])
                    u["extra"].append([(CTX, minus_turn, bias[:, h % 2, :, off:off + BAND].rearrange("p k j -> p j k"), False)])
                    u["w"].append(SEQ)
                    v = [1, 2, 2, 3][b]
                    u["mask"].append(bmask[:, 0:v + 1:v, :])
                for t in range(2):
                    u["steps"].append((vband[:, h // 2 % 2, t, :], [(0, P * t), (1, P * t)]))
                for i in range(2):
                    for half in range(2):
                        u["steps"].append((vband[:, h // 2 % 2, 2 + 2 * (2 * pair + i) + half, :], [(i, CTX + P * half)]))
                units.append(u)
            units[-1]["bias_end"] = True
            return units

        def seq_turns():
            out = []
            for t, e in ((0, 4), (4, 6)):
                dst = vseq[:, t:e, :, :].rearrange("p t g (d c) -> p t g d c", c=HD)
                out.append(([slots[:, 5, P * i:P * i + P] for i in range(t, e)], [dst[:, :, :, d, :] for d in range(2)]))
            return out

        def band_turns(p):
            v = slots[:, 8 + p, :]
            src = [v[:, SEQ + P * t:SEQ + P * t + P] for t in range(2)]
            for b in range(4):
                for half in range(2):
                    at0 = ROWS * BAND_AT[b] + P * half
                    src.append(v[:, at0:at0 + P])
            return [(src[t:t + 4], [vband[:, p % 2, t:min(t + 4, 10), :]]) for t in range(0, 10, 4)]

        at = dict(s=0, t=0, v=0, w=0, u=0)
        plans = {}
        for l in range(DEPTH):
            full = l < DEPTH - 1
            for m in "ABC":
                if m == "B":
                    groups = []
                    for p in range(4):
                        units = []
                        for h in (2 * p, 2 * p + 1):
                            units += band_units(h, l)
                        if full:
                            units += [u for u in context_units("B", l) if u["h"] // 2 == p]
                        groups.append((band_turns(p), units))
                else:
                    groups = [(seq_turns(), seq_units(m, l) + (context_units(m, l) if full else []))]
                plans[l, m] = (make_plan(groups, at), at["u"])
        start2 = dict(at)

        def fox_units():
            units = []
            for h in range(4):
                r = rows_of(h)
                q, k = u2[r, 14 + h // 2, :], u2[r, 16 + h // 2, :]
                for pair in range(2):
                    u = dict(h=h, q=[], seg=[], extra=[], w=[], mask=[], steps=[],
                             dst=mix2[r, h // 2, 256 * pair:256 * pair + 256])
                    for b in (2 * pair, 2 * pair + 1):
                        w = P * (b + 1)
                        u["q"].append(q[:, P * b:P * b + P])
                        u["seg"].append([(0, k[:, 0:w])])
                        u["extra"].append([(0, augq[32 * h:32 * h + 2, P * b:P * b + P], augk[32 * h:32 * h + 2, 0:w], False)])
                        u["w"].append(w)
                        u["mask"].append("last tile")
                    for t in range(2 * pair + 2):
                        has = [i for i in range(2) if t <= 2 * pair + i]
                        u["steps"].append((vfox[:, h // 2, t, :], [(i, P * t) for i in has]))
                    units.append(u)
            return units

        def fox_turns():
            return [([u2[:, 18 + p, P * t:P * t + P] for t in range(4)], [vfox[:, p, :, :]]) for p in range(2)]

        fox_plan = make_plan([(fox_turns(), fox_units())], at)
        per = {k: at[k] - start2[k] for k in at}

        class Off:
            def __init__(self, l):
                zero = l is None
                self.s = 0 if zero else l * per["s"]
                self.t = 0 if zero else l * per["t"]
                self.v = 0 if zero else l * per["v"]
                self.w = 0 if zero else l * per["w"]
                self.u = 0 if zero else l * per["u"]

        def scores_at(s, n):
            return ps[:, 2048 + 1024 * (s % 2):2048 + 1024 * (s % 2) + n]

        def turned_at(ev, n):
            return bank(2 + ev["i"] % 2)[:, 0:n]

        def pieces(ev):
            at0, out = 0, []
            for lhs, tiles in ev["steps"]:
                n = P * len(tiles)
                out.append((at0, lhs, P * tiles[0][0], n, tiles))
                at0 += n
            return out, at0

        def attention_pe(pe, plan, o):
            pend = None

            def multiply(ev):
                u = ev["unit"]
                pe.wait_ge(pt_taken, ev["n"] + 1 + o.v)
                if ev["first"]:
                    pe.wait_ge(values_taken, u["turned"] + o.w)
                    if u["local"] >= 2:
                        pe.wait_ge(y_done, u["u"] - 1 + o.u)
                steps, _ = pieces(ev)
                for j, (at0, lhs, col, n, _) in enumerate(steps):
                    ins = nc.tensor.matmul(bank(u["local"] % 2, col, col + n), lhs, probs_t[:, ev["n"] % 2, at0:at0 + n],
                                           start=ev["first"] and j == 0, stop=ev["last"] and j == len(steps) - 1,
                                           skip_group_check=True)
                ins.then_inc(pv_steps, 1)

            for ev in plan:
                u = ev.get("unit")
                if ev["kind"] == "S":
                    qb = ev["qb"]
                    if ev["local"] >= 2:
                        pe.wait_ge(exp_done, ev["s"] - 1 + o.s)
                    if qb == 0 and u.get("bias") is not None:
                        pe.wait_ge(bias_in[u["bias"] % 2], 16 * ROWS * (u["bias"] // 2 + 1))
                    S = scores_at(ev["local"], 1024)
                    for col, rhs in u["seg"][qb]:
                        n = rhs.free_size()
                        assert col // 512 == (col + n - 1) // 512
                        ins = nc.tensor.matmul(S[:, col:col + n], u["q"][qb], rhs, start=True, stop=True, skip_group_check=True)
                    for col, lhs, rhs, alone in u["extra"][qb]:
                        n = rhs.free_size()
                        ins = nc.tensor.matmul(S[:, col:col + n], lhs, rhs, start=alone, stop=True, skip_group_check=True)
                    ins.then_inc(s_ready, 1)
                elif ev["kind"] in "TV":
                    if "before" in ev:
                        b = ev["before"]
                        if b["kind"] == "T":
                            pe.wait_ge(pt_taken, b["n"] + 1 + o.v)
                        else:
                            pe.wait_ge(values_taken, b["n"] + 1 + o.w)
                    if ev["kind"] == "T":
                        if ev["first"]:
                            pe.wait_ge(diag_ready, u["s_last"] + 1 + o.s)
                        for at0, _, _, _, tiles in pieces(ev)[0]:
                            for j, (i, c) in enumerate(tiles):
                                ins = nc.tensor.matmul(turned_at(ev, 512)[:, at0 + P * j:at0 + P * j + P],
                                                       probs[:, u["local"] % 2, i, c:c + P],
                                                       diag[:, (u["s_last_local"] - 1 + i) % 4, :], start=True, stop=True,
                                                       skip_group_check=True)
                    else:
                        for i, x in enumerate(ev["src"]):
                            ins = nc.tensor.transpose(turned_at(ev, 512)[:, P * i:P * i + P], x, ident)
                    ins.then_inc(turned, 1)
                    if pend:
                        multiply(pend)
                    pend = ev if ev["kind"] == "T" else None
                else:
                    if pend:
                        multiply(pend)
                    pend = None

        def attention_dve(dve, plan, o):
            V = nc.vector
            ends = {}
            for ev in plan:
                u = ev.get("unit")
                if ev["kind"] == "S":
                    s, w, mask = ev["local"] % 4, u["w"][ev["qb"]], u["mask"][ev["qb"]]
                    S = scores_at(ev["local"], w)
                    dve.wait_ge(s_ready, ev["s"] + 1 + o.s)
                    if mask == "last tile":
                        V.tensor_tensor(S[:, w - P:w], S[:, w - P:w], fmask, ALU.add)
                        dve.drain()
                        mask = None
                    if mask is None:
                        V.tensor_reduce(row_min[:, s:s + 1], S, AX_X, ALU.min).then_inc(max_ready, 1)
                    else:
                        if len(mask.shape) == 3:
                            S = S.rearrange("p (a n) -> p a n", a=2)
                        V.tensor_tensor_reduce(out=S, in0=S, in1=mask, scale=1.0, scalar=HIGHEST, op0=ALU.add,
                                               op1=ALU.min, accum_out=row_min[:, s:s + 1]).then_inc(max_ready, 1)
                    dve.wait_ge(exp_done, ev["s"] + 1 + o.s)
                    V.reciprocal(weight[:, s:s + 1], row_sum[:, s:s + 1])
                    dve.drain()
                    if u["local"] - 2 in ends:
                        dve.wait_ge(turned, ends[u["local"] - 2] + 1 + o.t)
                    V.tensor_scalar(diag[:, s, :], ident, weight[:, s:s + 1], None, ALU.mult).then_inc(diag_ready, 1)
                elif ev["kind"] == "T":
                    ends[u["local"]] = ev["t"]
                elif ev["kind"] == "V":
                    dve.wait_ge(turned, ev["t"] + 1 + o.t)
                    if ev["need_group"] >= 0:
                        dve.wait_ge(pv_steps, ev["v_end"][ev["need_group"]] + o.v)
                    src = turned_at(ev, P * len(ev["src"])).rearrange("p (t g c) -> p t g c", g=2, c=HD)
                    for d in ev["dst"]:
                        if len(d.shape) == 3:
                            d = d.rearrange("p t (g c) -> p t g c", c=HD)
                        ins = V.tensor_copy(d, src)
                    ins.then_inc(values_taken, 1)
                else:
                    dve.wait_ge(pv_steps, u["v_last"] + 1 + o.v)
                    a, d = bank(u["local"] % 2, 0, 256)[rows_of(u["h"])], u["dst"]
                    if len(d.shape) == 3:
                        a = a.rearrange("p (c r) -> p c r", r=ROWS)
                    V.tensor_copy(d, a).then_inc(y_done, 1)

        def attention_act(act, plan, o):
            ends, held = {}, None

            def exponentials(ev):
                u = ev["unit"]
                s, w = ev["local"] % 4, u["w"][ev["qb"]]
                act.wait_ge(max_ready, ev["s"] + 1 + o.s)
                if ev["qb"] == 0 and u["local"] - 2 in ends:
                    act.wait_ge(turned, ends[u["local"] - 2] + 1 + o.t)
                nc.scalar.activation(probs[:, u["local"] % 2, ev["qb"], 0:w], scores_at(ev["local"], w), ACT.Exp,
                                     bias=row_min[:, s:s + 1], scale=-1.0, accum_out=row_sum[:, s:s + 1]).then_inc(exp_done, 1)

            for ev in plan:
                if ev["kind"] == "S":
                    if held:
                        exponentials(held)
                    held = ev
                elif ev["kind"] == "T":
                    ends[ev["unit"]["local"]] = ev["t"]
                    n = pieces(ev)[1]
                    act.wait_ge(turned, ev["t"] + 1 + o.t)
                    if ev["n"] >= 2:
                        act.wait_ge(pv_steps, ev["n"] - 1 + o.v)
                    nc.scalar.copy(probs_t[:, ev["n"] % 2, 0:n], turned_at(ev, n)).then_inc(pt_taken, 1)
                    if held:
                        exponentials(held)
                    held = None

        ADA1, ADA2, IN1, OUT1 = "ada1", "ada2", "in1", "out1"
        later = ([(ADA1, 0, i) for i in range(N_SS1, N_ADA1)] + [(ADA1, 1, i) for i in range(N_ADA1)]
                 + [(ADA2, l, i) for l in range(DEPTH) for i in range(N_ADA2)])
        spare, free = {}, list(later)
        for l in range(DEPTH):
            for lo, hi in PHASES.values():
                for b in range(lo, hi - 1):
                    spare[l, b] = free.pop(0)
        assert not free
        stream = [(ADA1, 0, i) for i in range(N_SS1)]
        for l in range(DEPTH):
            for i in range(N_IN1):
                stream.append((IN1, l, i))
                stream += [spare[l, b] for b in (2 * i, 2 * i + 1) if (l, b) in spare]
            stream += [(OUT1, l, i) for i in range(KC)]
        number = {p: n for n, p in enumerate(stream)}
        N1 = len(stream)
        ada_seq = [p for p in stream if p[0] in (ADA1, ADA2)]
        ada_no = {p: n for n, p in enumerate(ada_seq)}
        n_mod1 = {l: ada_no[ADA1, l, N_SS1 - 1] + 1 for l in range(DEPTH)}
        n_gate1 = {l: ada_no[ADA1, l, N_ADA1 - 1] + 1 for l in range(DEPTH)}
        per2 = ([("in2", 0, i) for i in range(N_IN2)] + [("out2", 0, i) for i in range(N_OUT2)]
                + [(k, 0, i) for i in range(N_FF) for k in ("w1", "w3")]
                + [("w2", g, j) for g in range(N_OUT2) for j in range(len(W2_CUT))])
        assert len(per2) == PER2

        def slot(n, chunks=KC):
            return ring[:, n % RING, :].rearrange("p (c n) -> p c n", c=chunks)

        def panel_wait(eng, n, l=None):
            eng.wait_ge(panel_in[n % RING], 16 * (n // RING + 1) + (0 if l is None else l * (16 * PER2 // RING)))

        NSEQ = {}
        def blocks_of(l, m):
            lo, hi = PHASES[m]
            last = l == DEPTH - 1
            return [(b, SEQ if last and (m == "G" or b - lo < 4) else TOK) for b in range(lo, hi)]

        for l in range(DEPTH):
            for m in "ABCG":
                for b, _ in blocks_of(l, m):
                    NSEQ[l, b] = len(NSEQ)
        NPROJ1 = len(NSEQ)
        NX1 = DEPTH * KC + KC
        out_tokens = lambda l: TOK if l < DEPTH - 1 else SEQ
        slot_of = lambda b: b if b < 6 else b - 6 if b < 18 else b - 18

        def used(n):
            kind, l, i = stream[n]
            if kind in (ADA1, ADA2):
                k = ada_no[stream[n]]
                return (mod_ready, k + 1) if k < N_SS1 else (part_ready, k - N_SS1 + 1)
            if kind == IN1:
                return proj_ready, NSEQ[l, 2 * i + 1] + 1
            return out_ready, l * KC + i + 1

        def used2(i, l):
            kind, g, j = per2[i]
            if kind == "in2":
                return proj_ready, NPROJ1 + 2 * j + 2 + l * 20
            if kind == "out2":
                return out_ready, DEPTH * KC + 2 * j + 2 + l * 2 * KC
            if kind == "w1":
                return h1_ready, 2 * j + 2 + l * FFC
            if kind == "w3":
                return h3_ready, 2 * j + 2 + l * FFC
            if j < len(W2_CUT) - 1:
                return w2_used, 2 * g + j + 1 + l * 2 * N_OUT2
            return out_ready, DEPTH * KC + KC + 2 * g + 2 + l * 2 * KC

        block = ctx.enter_context(nc.Block())

        @block.sync
        def _(sp):
            sp.dma_start(xl[:, :, :], dram["x"]).then_inc(x_in, 16)
            sp.dma_start(xc[:, :, :], dram["ctx"]).then_inc(x_in, 16)
            sp.dma_start(prm[:, :], dram["prm"]).then_inc(vec_in, 16)
            sp.dma_start(mats[:, :, :], dram["mats"]).then_inc(mats_in, 16)
            for n, (kind, l, i) in enumerate(stream):
                if n >= RING:
                    sp.wait_ge(*used(n - RING))
                src = dram[kind][l, i]
                sp.dma_start(ring[:, n % RING, 0:src.shape[-1]], src).then_inc(panel_in[n % RING], 16)
                if n == N_SS1 + 2:
                    sp.dma_start(rope_c[:, :], dram["rope"][:, 0, :]).then_inc(tables_in, 16)
                    sp.dma_start(rope_s[:, :], dram["rope"][:, 1, :]).then_inc(tables_in, 16)
                    sp.dma_start(bmask[:, :, :], dram["bmask"]).then_inc(tables_in, 16)
                    sp.dma_start(cmask[:, :], dram["cmask"]).then_inc(tables_in, 16)
                    sp.dma_start(sinks[:, :], dram["sinks"]).then_inc(tables_in, 16)
                    sp.dma_start(minus_one[:, :], dram["minus_one"]).then_inc(tables_in, 16)
                    sp.dma_start(lyr[:, :, :], dram["lyr"]).then_inc(lyr_vec_in, 16)
            sp.wait_ge(x_ready, NX1)
            sp.dma_start(angle[:, 0, :].bitcast(I32), dram["pos"].partition_broadcast(P)).then_inc(pos_in, 16)
            for tile, name in ((fmask, "fmask"), (decay[:, :, :], "decay"), (counts[:, :, :], "counts")):
                sp.dma_start(tile, dram[name]).then_inc(tables2_in, 16)
            with sp.Fori(0, DEPTH) as l:
                for i, (kind, g, j) in enumerate(per2):
                    n = N1 + i
                    if i < RING:
                        sp.wait_ge(out_ready, DEPTH * KC + l * 2 * KC)
                    else:
                        sp.wait_ge(*used2(i - RING, l))
                    if kind == "w2":
                        a, e = W2_CUT[j]
                        src = dram[kind][bass.ds(l, 1), g, :, PAN * a:PAN * e]
                    else:
                        src = dram[kind][bass.ds(l, 1), j, :, :]
                    src = src.rearrange("a p n -> (a p) n")
                    sp.dma_start(ring[:, n % RING, 0:src.shape[-1]], src).then_inc(panel_in[n % RING], 16)
                    if i == 0:
                        sp.dma_start(ffw[:, :, :].rearrange("p c n -> p (c n)"),
                                     dram["ffw"][bass.ds(l, 1), :, :].rearrange("a p n -> (a p) n")).then_inc(lyr_in, 16)
                        sp.dma_start(poolw[:, :, :].rearrange("p c n -> p (c n)"),
                                     dram["poolw"][bass.ds(l, 1), :, :].rearrange("a p n -> (a p) n")).then_inc(lyr_in, 16)
            sp.wait_ge(result_ready, KC)
            sp.dma_start(out, hl[:, :, :]).then_inc(result_out, 16)
            sp.wait_ge(result_out, 16)

        @block.gpsimd
        def _(pool):
            s_end = {}
            for l in range(DEPTH):
                for ev in plans[l, "B"][0]:
                    if ev["kind"] == "S" and ev["unit"].get("bias_end"):
                        s_end[l * HEADS + ev["unit"]["h"]] = ev["s"] + 1

            def bias_rows(n):
                if n >= 2:
                    pool.wait_ge(s_ready, s_end[n - 2])
                for r in range(ROWS):
                    src = bass.AP(dram["rpb"].tensor, n * 15 * 64 + 64 * r, [[1, NBC], [64, ROWS], [1, 48]])
                    pool.dma_start(bias[NBC * r:NBC * r + NBC, n % 2, :, :], src).then_inc(bias_in[n % 2], 16)

            for n in range(DEPTH * HEADS):
                bias_rows(n)
            pool.wait_ge(x_ready, NX1)
            pool.memset(hpad[:, :, 0:CONV - 1], 0.0).then_inc(pads_done, 1)
            pool.memset(ppad[:, :, 0:POOLPAD], 0.0).then_inc(pads_done, 1)
            pool.memset(vret[:, :, :, HD:2 * HD], 0.0).then_inc(pads_done, 1)
            pool.memset(augq[:, :], 1.0).then_inc(pads_done, 1)
            pool.memset(augk[:, :], 1.0).then_inc(pads_done, 1)
            pool.wait_ge(pads_done, 5)
            pool.wait_ge(tables2_in, 48)
            with pool.Fori(0, DEPTH) as l:
                pool.wait_ge(proj_taken, NPROJ1 + 14 + l * 20)
                n = POOLPAD + SEQ
                A, B = psums[:, 0, :], psums[:, 1, :]
                halves = {1: (0, 0), 2: (1, 0), 4: (0, 1), 8: (1, 1)}
                for t in range(2):
                    src = ppad[:, t, :]
                    for k, dst in ((1, A), (2, B)) if t == 0 else ((1, A), (2, B), (4, A), (8, B)):
                        lo = 2 * k - 1
                        nc.gpsimd.tensor_tensor(dst[:, lo:n], src[:, lo:n], src[:, lo - k:n - k], ALU.add)
                        pool.drain()
                        half, tile = halves[k]
                        if tile == t:
                            r = slice(HD * half, HD * half + HD)
                            nc.gpsimd.tensor_tensor(pooled[r, t, :], dst[r, POOLPAD:n], counts[r, t, :], ALU.mult)
                        src = dst
                    pool.drain()
                nc.gpsimd.tensor_tensor(pooled, pooled, ppad[:, :, POOLPAD:n], ALU.subtract).then_inc(pool_done, 1)

        @block.scalar
        def _(act):
            A_ = nc.scalar.activation

            def take_mod(p):
                kind, l, i = p
                k = ada_no[p]
                act.wait_ge(mod_ready, k + 1)
                dst = mod1[:, l, 2 * i:2 * i + 2, :].rearrange("p a b -> p (a b)") if kind == ADA1 else mod2[:, l, 2 * i:2 * i + 2]
                n = 4 if kind == ADA1 else 2
                nc.scalar.copy(dst, bank(4 + k % 2, 0, n)).then_inc(mod_taken, 1)

            def norm(k, parts, x_count, kb=None, shift=None, meanwhile=()):
                for c in range(KC):
                    if x_count is None:
                        act.wait_ge(x_in, 32)
                    else:
                        act.wait_ge(x_ready, x_count + c + 1)
                    if isinstance(k, int) and 8 * k + c >= 2 or not isinstance(k, int):
                        act.wait_ge(sq_summed, 8 * k + c - 1)
                    for j, (x, _, lo, n) in enumerate(parts):
                        ins = A_(squares[:, c % 2, lo:lo + n], x[:, c, :], ACT.Square)
                    ins.then_inc(sq_ready, 1)
                act.wait_ge(sq_summed, 8 * k + KC)
                for j, (_, _, lo, n) in enumerate(parts):
                    ins = A_(std[:, 0, lo:lo + n], bank(6 + j, 0, n), ACT.Sqrt, bias=EPS, scale=1.0 / DM)
                ins.then_inc(std_ready, 1)
                for p in meanwhile:
                    take_mod(p)
                if shift is None:
                    return
                for c in range(KC):
                    act.wait_ge(hm_ready, 8 * kb + c + 1)
                    for j, (_, h, lo, n) in enumerate(parts):
                        ins = A_(h[:, c, :], h[:, c, :], ACT.Identity, bias=shift(c, j))
                    ins.then_inc(h_ready, 1)

            both = [(xl, hl, 0, SEQ), (xc, hc, SEQ, CTX)]
            act.wait_ge(vec_in, 16)
            A_(silu_c[:, :, :].rearrange("p a b -> p (a b)"), vec("c", 0, 2 * KC), ACT.Silu).then_inc(silu_done, 1)
            A_(silu_c2[:, :], vec("c2", 0, KC), ACT.Silu).then_inc(silu_done, 1)
            def projected(l, m):
                for b, n in blocks_of(l, m):
                    k = NSEQ[l, b]
                    act.wait_ge(proj_ready, k + 1)
                    if m == "G":
                        dst, f, scale = gate_buf[:, k % 2, :], ACT.Silu, 1.0
                        g = l * MIXC + b - 24
                        if g >= 2:
                            act.wait_ge(u_ready, g - 1)
                    else:
                        dst, f = slots[:, slot_of(b), :], ACT.Copy
                        scale = -QSCALE if m in "BC" and b - {"B": 6, "C": 18}[m] < 4 else 1.0
                    to, src = dst[:, 0:SEQ], bank(k % 2)
                    if m == "B":
                        to, src = to.rearrange("p (c r) -> p r c", r=ROWS), src.rearrange("p (r c) -> p r c", c=GRID)
                    ins = A_(to, src, f, scale=scale)
                    if n == TOK:
                        ins = A_(dst[:, SEQ:TOK], bank(2 + k % 2, 0, CTX), f, scale=scale)
                    ins.then_inc(proj_taken, 1)
                    if (l, b - 1) in spare:
                        take_mod(spare[l, b - 1])

            def qk_norm(l):
                width = lambda j: TOK if l < DEPTH - 1 or j == 4 else SEQ

                def square(j):
                    q = 5 * l + j
                    act.wait_ge(proj_taken, NSEQ[l, j] + 1)
                    if q >= 2:
                        act.wait_ge(qsum_ready, q - 1)
                    A_(squares[:, j % 2, 0:width(j)], slots[:, j, 0:width(j)], ACT.Square).then_inc(qsq_ready, 1)

                def root(j):
                    q = 5 * l + j
                    act.wait_ge(qsum_ready, q + 1)
                    if q >= 2:
                        act.wait_ge(qn_done, q - 1)
                    b = 4 + 2 * (j % 2)
                    ins = A_(std[:, j % 2, 0:SEQ], bank(b), ACT.Sqrt, bias=EPS, scale=1.0 / HD)
                    if width(j) == TOK:
                        ins = A_(std[:, j % 2, SEQ:TOK], bank(b + 1, 0, CTX), ACT.Sqrt, bias=EPS, scale=1.0 / HD)
                    ins.then_inc(qstd_ready, 1)

                square(0)
                for j in range(1, 5):
                    square(j)
                    root(j - 1)
                root(4)

            zero = Off(None)
            for l in range(DEPTH):
                norm(l, both, None if l == 0 else KC * (l - 1), l, lambda c, j: mod1[:, l, c, j:j + 1],
                     stream[:N_SS1] if l == 0 else ())
                for m in "ABC":
                    projected(l, m)
                    if m == "A":
                        qk_norm(l)
                    attention_act(act, plans[l, m][0], zero)
                projected(l, "G")
            latent = [(xl, hl, 0, SEQ)]
            norm(2, latent, KC * (DEPTH - 1))

            act.wait_ge(angle_done, 1)
            A_(rsin[:, :], angle[:, 0, :], ACT.Sin).then_inc(sines_done, 1)
            A_(rcos[:, :], angle[:, 0, :], ACT.Sin, scale=0.5).then_inc(sines_done, 1)
            act.wait_ge(pads_done, 5)
            with act.Fori(0, DEPTH) as l:
                o = Off(l)
                norm(3 + l * 2, latent, NX1 - KC + l * 2 * KC, 2 + l * 2, lambda c, j: mod[:, c:c + 1])
                act.wait_ge(ff_ready, 1 + l)
                A_(fz, bank(3)[0:4], ACT.Identity, bias=lvec("fox_b")[0:4])
                act.drain()
                A_(ft, fz, ACT.Abs)
                act.drain()
                A_(ft, ft, ACT.Exp, scale=-1.0)
                act.drain()
                A_(ft, ft, ACT.Ln, bias=1.0).then_inc(ff_log, 1)
                for m in range(20):
                    act.wait_ge(proj_ready, NPROJ1 + m + 1 + l * 20)
                    src, dst, f, scale = bank(m % 2), u2[:, m, :], ACT.Copy, 1.0
                    if m in (2, 3):
                        f = ACT.Sigmoid
                    elif m in (6, 7):
                        scale = QSCALE
                    elif m in (14, 15):
                        scale = -QSCALE
                    elif m in (10, 11):
                        f = ACT.Silu
                    elif m in (12, 13):
                        dst = ppad[:, m - 12, POOLPAD:]
                    A_(dst, src, f, scale=scale).then_inc(proj_taken, 1)
                act.wait_ge(ff_cum, 1 + l)
                for h in range(4):
                    act.dma_start(augq[32 * h:32 * h + 1, :], ft[h:h + 1, :]).then_inc(aug_in, 16)
                    act.dma_start(augk[32 * h + 1:32 * h + 2, :], fz[h:h + 1, :]).then_inc(aug_in, 16)
                for g in range(2):
                    act.wait_ge(rv_ready, g + 1 + l * 2)
                    for h in range(2):
                        ins = nc.scalar.copy(vret[:, g, :, P * h:P * h + HD],
                                             bank(2 + g).rearrange("p (t c) -> p t c", c=P)[:, :, HD * h:HD * h + HD])
                    ins.then_inc(rv_taken, 1)
                for g in range(2):
                    act.wait_ge(ro_steps, 8 * (g + 1) + l * 16)
                    nc.scalar.copy(ret_o[:, g, :], bank(g)).then_inc(ro_taken, 1)
                act.wait_ge(ln_dev, 2 + l * 2)
                for t in range(2):
                    A_(squares[:, t, 0:SEQ], conv[:, t, :], ACT.Square).then_inc(ln_sq, 1)
                act.wait_ge(ln_var, 1 + l)
                A_(std[:, 0, 0:SEQ], bank(7), ACT.Sqrt, bias=EPS, scale=1.0 / 256).then_inc(ln_std, 1)
                for t in range(2):
                    act.wait_ge(ln_norm, t + 1 + l * 2)
                    A_(mix2[:, 6 + t, :], conv[:, t, :], ACT.Silu, bias=lvec("ln_b", t), scale=lvec("ln_g", t)).then_inc(conv_mix, 1)
                for g in range(2):
                    act.wait_ge(gn_dev, g + 1 + l * 2)
                    A_(squares[:, g, 0:SEQ], ret_o[:, g, :], ACT.Square).then_inc(gn_sq, 1)
                for g in range(2):
                    act.wait_ge(gn_var, g + 1 + l * 2)
                    A_(std[:, g, 0:SEQ], bank(2 + g), ACT.Sqrt, bias=EPS, scale=1.0 / HD).then_inc(gn_std, 1)
                for t in range(2):
                    act.wait_ge(pool_proj, t + 1 + l * 2)
                    A_(mix2[:, 2 + t, :], bank(4 + t), ACT.Identity, scale=lvec("pool_scale", t)).then_inc(pool_mix, 1)
                attention_act(act, fox_plan, o)
                norm(4 + l * 2, latent, NX1 + l * 2 * KC, 3 + l * 2, lambda c, j: mod[:, 24 + c:25 + c])
                for b in range(FFC):
                    act.wait_ge(h1_ready, b + 1 + l * FFC)
                    if b >= 2:
                        act.wait_ge(f_ready, b - 1 + l * FFC)
                    A_(squares[:, b % 2, 0:SEQ], bank(4 * (b // 2 % 2) + b % 2), ACT.Silu).then_inc(silu_ready, 1)
            norm(3 + 2 * DEPTH, latent, NX1 + 2 * KC * DEPTH - KC)

        @block.vector
        def _(dve):
            V = nc.vector

            def norm(k, parts, gain, place=None, signal=None):
                dve.drain()
                dve.wait_ge(std_ready, k + 1)
                n = sum(p[3] for p in parts)
                V.reciprocal(rstd[:, 0:n], std[:, 0, 0:n])
                dve.drain()
                for c in range(KC):
                    for j, (x, h, lo, n) in enumerate(parts):
                        ins = V.scalar_tensor_tensor(out=(place or h)[:, c, :], in0=x[:, c, :], scalar=gain(c, j),
                                                     in1=rstd[:, lo:lo + n], op0=ALU.mult, op1=ALU.mult)
                    ins.then_inc(signal or hm_ready, 1)

            both = [(xl, hl, 0, SEQ), (xc, hc, SEQ, CTX)]
            latent = both[:1]
            dve.wait_ge(vec_in, 16)
            V.tensor_scalar(qn8[:, :], vec("qn", 0, DEPTH), -QSCALE, None, ALU.mult)
            swaps = 0

            def rope(slot_ap, r, cos, sin):
                tmp = probs_t[:, 0, :]
                dve.drain()
                dve.wait_ge(sw_ready, r + 1)
                V.tensor_tensor(tmp, bank(r_bank), sin, ALU.mult)
                V.tensor_tensor(slot_ap, slot_ap, cos, ALU.mult)
                dve.drain()
                V.tensor_tensor(slot_ap, slot_ap, tmp, ALU.add).then_inc(rope_done, 1)

            def qk_norm(l, j):
                q = 5 * l + j
                n = TOK if l < DEPTH - 1 or j == 4 else SEQ
                dve.drain()
                dve.wait_ge(qstd_ready, q + 1)
                V.reciprocal(rstd[:, 0:n], std[:, j % 2, 0:n])
                dve.drain()
                w = vec("kn", l) if j == 4 else qn8[:, l:l + 1]
                V.scalar_tensor_tensor(out=slots[:, j, 0:n], in0=slots[:, j, 0:n], scalar=w, in1=rstd[:, 0:n],
                                       op0=ALU.mult, op1=ALU.mult).then_inc(qn_done, 1)

            def double_keys():
                dve.drain()
                for kv in range(2):
                    for half in range(2):
                        ins = V.tensor_copy(slots[HD * half:HD * half + HD, 6 + kv, :], slots[HD * kv:HD * kv + HD, 4, :])
                ins.then_inc(kdup_done, 1)

            def mod_parts(p):
                k = ada_no[p]
                panel_wait(dve, number[p])
                if k >= N_SS1 + 2:
                    dve.wait_ge(mod_ready, k - 1)
                w = slot(number[p])
                for c in range(KC):
                    for i in range(2 if p[0] == ADA1 else 1):
                        v = silu_c[:, c, i:i + 1] if p[0] == ADA1 else silu_c2[:, c:c + 1]
                        if c == 0:
                            ins = V.tensor_scalar(parts[:, k % 2, i, :], w[:, c, :], v, None, ALU.mult)
                        else:
                            ins = V.scalar_tensor_tensor(out=parts[:, k % 2, i, :], in0=w[:, c, :], scalar=v,
                                                         in1=parts[:, k % 2, i, :], op0=ALU.mult, op1=ALU.add)
                    if c < KC - 1:
                        dve.drain()
                ins.then_inc(part_ready, 1)

            zero = Off(None)
            for l in range(DEPTH):
                dve.wait_ge(mod_taken, n_mod1[l])
                for i in range(2):
                    V.tensor_tensor(mod1[:, l, 0:2 * KC, i], mod1[:, l, 0:2 * KC, i], vec("ada_b", 24 * l, 2 * KC), ALU.add)
                dve.drain()
                for i in range(2):
                    V.scalar_tensor_tensor(out=gain1[:, i, :], in0=mod1[:, l, KC:2 * KC, i], scalar=1.0,
                                           in1=vec("norm_w", KC * l, KC), op0=ALU.add, op1=ALU.mult)
                dve.drain()
                norm(l, both, lambda c, j: gain1[:, j, c:c + 1])
                for m in "ABC":
                    for b, _ in blocks_of(l, m):
                        if (l, b) in spare:
                            mod_parts(spare[l, b])
                    if l == 0 and m == "A":
                        dve.wait_ge(tables_in, 96)
                    if m == "A":
                        qk_norm(l, 0)
                        for j in range(5):
                            if j < 4:
                                qk_norm(l, j + 1)
                            r_bank = j % 2
                            dve.drain()
                            rope(slots[:, j, 0:SEQ], 10 * l + j, rope_c[:, :], rope_s[:, :])
                        double_keys()
                    elif m == "C":
                        for j in range(5):
                            r_bank = j % 2
                            rope(slots[:, j, 0:SEQ], 10 * l + 5 + j, rope_c[:, :], rope_s[:, :])
                        double_keys()
                    attention_dve(dve, plans[l, m][0], zero)
                for b, n in blocks_of(l, "G"):
                    k = NSEQ[l, b]
                    if (l, b) in spare:
                        mod_parts(spare[l, b])
                    dve.wait_ge(proj_taken, k + 1)
                    V.tensor_tensor(y1[:, b - 24, 0:n], y1[:, b - 24, 0:n], gate_buf[:, k % 2, 0:n], ALU.mult).then_inc(u_ready, 1)
                dve.wait_ge(mod_taken, n_gate1[l])
                for i in range(2):
                    V.tensor_tensor(mod1[:, l, 2 * KC:, i], mod1[:, l, 2 * KC:, i], vec("ada_b", 24 * l + 2 * KC, KC), ALU.add)
                dve.drain()
                for o in range(KC):
                    dve.wait_ge(out_ready, KC * l + o + 1)
                    for j, (x, _, lo, n) in enumerate(both if l < DEPTH - 1 else latent):
                        ins = V.scalar_tensor_tensor(out=x[:, o, :], in0=bank(4 - 2 * j + o % 2, 0, n),
                                                     scalar=mod1[:, l, 2 * KC + o, j:j + 1], in1=x[:, o, :],
                                                     op0=ALU.mult, op1=ALU.add)
                    ins.then_inc(x_ready, 1)
            dve.drain()
            norm(2, latent, lambda c, j: vec("final_w", c), place=xl, signal=x_ready)

            dve.wait_ge(pos_in, 16)
            V.tensor_copy(angle[:, 1, :], angle[:, 0, :].bitcast(I32))
            dve.drain()
            V.tensor_scalar(angle[:, 1, :], angle[:, 1, :], vec("inv"), None, ALU.mult)
            dve.drain()
            V.tensor_scalar(angle[:, 2, :], angle[:, 1, :], 1.0 / (2 * np.pi), MAGIC, ALU.mult, ALU.add)
            dve.drain()
            V.tensor_scalar(angle[:, 2, :], angle[:, 2, :], MAGIC, None, ALU.subtract)
            dve.drain()
            for part in TWO_PI:
                V.scalar_tensor_tensor(out=angle[:, 1, :], in0=angle[:, 2, :], scalar=-part, in1=angle[:, 1, :],
                                       op0=ALU.mult, op1=ALU.add)
                dve.drain()
            V.tensor_scalar(angle[:, 0, :], angle[:, 1, :], 3.1415925, -3.1415925, ALU.min, ALU.max).then_inc(angle_done, 1)
            dve.wait_ge(sines_done, 2)
            V.tensor_scalar(rsin[:, :], rsin[:, :], vec("sign"), None, ALU.mult)
            V.tensor_tensor(rcos[:, :], rcos[:, :], rcos[:, :], ALU.mult)
            dve.drain()
            V.tensor_scalar(rcos[:, :], rcos[:, :], -2.0, 1.0, ALU.mult, ALU.add)
            dve.wait_ge(lyr_vec_in, 16)
            dve.wait_ge(pads_done, 5)
            dve.wait_ge(tables2_in, 48)
            dve.wait_ge(mod_taken, len(ada_seq))
            with dve.Fori(0, DEPTH) as l:
                o = Off(l)
                dve.drain()
                V.tensor_copy(cur[:, :], lyr[:, bass.ds(l, 1), :].rearrange("p a b -> p (a b)"))
                dve.drain()
                V.tensor_tensor(mod[:, :], mod2[:, bass.ds(l, 1), :].rearrange("p a b -> p (a b)"), lvec("ada_b", 0, 48), ALU.add)
                dve.drain()
                for i, name in enumerate(("nmix", "nffn")):
                    V.scalar_tensor_tensor(out=gain2[:, i, :], in0=mod[:, 24 * i + KC:24 * i + 2 * KC], scalar=1.0,
                                           in1=lvec(name, 0, KC), op0=ALU.add, op1=ALU.mult)
                dve.drain()
                norm(3 + l * 2, latent, lambda c, j: gain2[:, 0, c:c + 1])
                dve.wait_ge(ff_log, 1 + l)
                V.scalar_tensor_tensor(out=ft, in0=fz, scalar=0.0, in1=ft, op0=ALU.min, op1=ALU.subtract)
                dve.drain()
                V.tensor_tensor_scan(fz, ft, ft, 0.0, ALU.add, ALU.bypass)
                dve.drain()
                V.tensor_scalar(ft, fz, -1.0, None, ALU.mult).then_inc(ff_cum, 1)
                dve.wait_ge(proj_taken, NPROJ1 + 4 + l * 20)
                for t in range(2):
                    V.tensor_tensor(hpad[:, t, CONV - 1:], u2[:, t, :], u2[:, 2 + t, :], ALU.mult)
                dve.drain()
                for j in range(CONV):
                    for t in range(2):
                        w, src = lvec("conv_w", CONV * t + j), hpad[:, t, j:j + SEQ]
                        if j == 0:
                            ins = V.tensor_scalar(conv[:, t, :], src, w, lvec("conv_b", t), ALU.mult, ALU.add)
                        else:
                            ins = V.scalar_tensor_tensor(out=conv[:, t, :], in0=src, scalar=w, in1=conv[:, t, :],
                                                         op0=ALU.mult, op1=ALU.add)
                    if j < CONV - 1:
                        dve.drain()
                ins.then_inc(conv_done, 1)
                for j in range(4):
                    r_bank = j % 2
                    rope(u2[:, 4 + j, :], 10 * DEPTH + j + l * 4, rcos[:, :], rsin[:, :])
                for i in range(16):
                    n = SEQ - P * (i % 4)
                    dve.wait_ge(rs_ready, i + 1 + l * 16)
                    if i >= 4:
                        dve.wait_ge(ro_steps, i - 3 + l * 16)
                    V.tensor_tensor(ret_s[:, i % 4, 0:n], bank(4 + i % 4, 0, n), decay[:, i // 4, 0:n], ALU.mult).then_inc(rs_done, 1)
                dve.wait_ge(ln_sum, 1 + l)
                for t in range(2):
                    V.scalar_tensor_tensor(out=conv[:, t, :], in0=bank(6), scalar=-1.0 / 256, in1=conv[:, t, :],
                                           op0=ALU.mult, op1=ALU.add).then_inc(ln_dev, 1)
                for g in range(2):
                    dve.wait_ge(gn_sum, g + 1 + l * 2)
                    V.scalar_tensor_tensor(out=ret_o[:, g, :], in0=bank(2 + g), scalar=-1.0 / HD, in1=ret_o[:, g, :],
                                           op0=ALU.mult, op1=ALU.add).then_inc(gn_dev, 1)
                dve.wait_ge(ln_std, 1 + l)
                V.reciprocal(rstd[:, 0:SEQ], std[:, 0, 0:SEQ])
                dve.drain()
                for t in range(2):
                    V.tensor_tensor(conv[:, t, :], conv[:, t, :], rstd[:, 0:SEQ], ALU.mult).then_inc(ln_norm, 1)
                for g in range(2):
                    dve.wait_ge(gn_std, g + 1 + l * 2)
                    V.reciprocal(rstd[:, 0:SEQ], std[:, g, 0:SEQ])
                    dve.drain()
                    V.scalar_tensor_tensor(out=ret_o[:, g, :], in0=ret_o[:, g, :], scalar=lvec("gn", g), in1=rstd[:, 0:SEQ],
                                           op0=ALU.mult, op1=ALU.mult)
                    dve.drain()
                    V.tensor_tensor(mix2[:, 4 + g, :], ret_o[:, g, :], u2[:, 10 + g, :], ALU.mult).then_inc(ret_mix, 1)
                attention_dve(dve, fox_plan, o)
                for i in range(KC):
                    dve.wait_ge(out_ready, DEPTH * KC + i + 1 + l * 2 * KC)
                    V.scalar_tensor_tensor(out=xl[:, i, :], in0=bank(i % 2), scalar=mod[:, 16 + i:17 + i], in1=xl[:, i, :],
                                           op0=ALU.mult, op1=ALU.add).then_inc(x_ready, 1)
                dve.drain()
                norm(4 + l * 2, latent, lambda c, j: gain2[:, 1, c:c + 1])
                for b in range(FFC):
                    dve.wait_ge(silu_ready, b + 1 + l * FFC)
                    dve.wait_ge(h3_ready, b + 1 + l * FFC)
                    V.tensor_tensor(act2[:, b, :], squares[:, b % 2, 0:SEQ], bank(4 * (b // 2 % 2) + 2 + b % 2), ALU.mult).then_inc(f_ready, 1)
                for i in range(KC):
                    dve.wait_ge(out_ready, DEPTH * KC + KC + i + 1 + l * 2 * KC)
                    V.scalar_tensor_tensor(out=xl[:, i, :], in0=bank(i % 4), scalar=mod[:, 40 + i:41 + i], in1=xl[:, i, :],
                                           op0=ALU.mult, op1=ALU.add).then_inc(x_ready, 1)
            dve.drain()
            norm(3 + 2 * DEPTH, latent, lambda c, j: vec("final_g", c), signal=result_ready)

        @block.tensor
        def _(pe):
            mm = nc.tensor.matmul

            def make_mod(p):
                n, k = number[p], ada_no[p]
                panel_wait(pe, n)
                if k >= 2:
                    pe.wait_ge(mod_taken, k - 1)
                for b in range(2):
                    for c in range(KC):
                        ins = mm(bank(4 + k % 2, 2 * b, 2 * b + 2), slot(n)[:, c, P * b:P * b + P], silu_c[:, c, :], start=c == 0, stop=c == KC - 1)
                ins.then_inc(mod_ready, 1)

            def norm(k, parts):
                for c in range(KC):
                    pe.wait_ge(sq_ready, 8 * k + c + 1)
                    for j, (_, _, lo, n) in enumerate(parts):
                        ins = mm(bank(6 + j, 0, n), ones, squares[:, c % 2, lo:lo + n], start=c == 0, stop=c == KC - 1)
                    ins.then_inc(sq_summed, 1)

            def sum_mod(p):
                k = ada_no[p]
                pe.wait_ge(part_ready, k - N_SS1 + 1)
                pe.wait_ge(mod_taken, k - 1)
                nv = 2 if p[0] == ADA1 else 1
                for b in range(2):
                    for i in range(nv):
                        ins = mm(bank(4 + k % 2, nv * b + i, nv * b + i + 1), parts[:, k % 2, i, P * b:P * b + P], ones[:, 0:1],
                                 start=True, stop=True)
                ins.then_inc(mod_ready, 1)

            both = [(xl, hl, 0, SEQ), (xc, hc, SEQ, CTX)]
            latent = both[:1]
            pe.wait_ge(mats_in, 16)
            norm(0, both)
            pe.wait_ge(silu_done, 2)
            for p in stream[:N_SS1]:
                make_mod(p)

            def project(l, m):
                for b, n in blocks_of(l, m):
                    k, pn = NSEQ[l, b], number[IN1, l, b // 2]
                    if b % 2 == 0:
                        panel_wait(pe, pn)
                    if k >= 2:
                        pe.wait_ge(proj_taken, k - 1)
                    for c in range(KC):
                        if b == 0:
                            pe.wait_ge(h_ready, KC * l + c + 1)
                        w = slot(pn)[:, c, P * (b % 2):P * (b % 2) + P]
                        ins = mm(bank(k % 2), w, hl[:, c, :], start=c == 0, stop=c == KC - 1)
                    if n == TOK:
                        for c in range(KC):
                            w = slot(pn)[:, c, P * (b % 2):P * (b % 2) + P]
                            ins = mm(bank(2 + k % 2, 0, CTX), w, hc[:, c, :], start=c == 0, stop=c == KC - 1)
                    ins.then_inc(proj_ready, 1)
                    if (l, b - 1) in spare:
                        sum_mod(spare[l, b - 1])
                pe.wait_ge(proj_taken, k + 1)
                pe.wait_ge(mod_taken, ada_no[spare[l, b - 1]] + 1)

            def head_sums(l, j):
                q = 5 * l + j
                pe.wait_ge(qsq_ready, q + 1)
                if q >= 2:
                    pe.wait_ge(qstd_ready, q - 1)
                b = 4 + 2 * (j % 2)
                ins = mm(bank(b), pairs, squares[:, j % 2, 0:SEQ], start=True, stop=True)
                if l < DEPTH - 1 or j == 4:
                    ins = mm(bank(b + 1, 0, CTX), pairs, squares[:, j % 2, SEQ:TOK], start=True, stop=True)
                ins.then_inc(qsum_ready, 1)

            def swap_halves(src, r, j):
                if not isinstance(r, int) or r >= 2:
                    pe.wait_ge(rope_done, r - 1)
                mm(bank(j % 2), swap, src, start=True, stop=True).then_inc(sw_ready, 1)

            zero = Off(None)
            for l in range(DEPTH):
                if l > 0:
                    norm(l, both)
                for m in "ABC":
                    project(l, m)
                    if m == "A":
                        head_sums(l, 0)
                        for j in range(5):
                            if j < 4:
                                head_sums(l, j + 1)
                            pe.wait_ge(qn_done, 5 * l + j + 1)
                            swap_halves(slots[:, j, 0:SEQ], 10 * l + j, j)
                    elif m == "C":
                        for j in range(5):
                            swap_halves(slots[:, j, 0:SEQ], 10 * l + 5 + j, j)
                    if m != "B":
                        pe.wait_ge(kdup_done, 2 * l + (1 if m == "A" else 2))
                    attention_pe(pe, plans[l, m][0], zero)
                    pe.wait_ge(y_done, plans[l, m][1])
                project(l, "G")
                for o in range(KC):
                    pn = number[OUT1, l, o]
                    panel_wait(pe, pn)
                    k = KC * l + o
                    if o >= 2:
                        pe.wait_ge(x_ready, k - 1)
                    for j, (_, _, lo, n) in enumerate(both if l < DEPTH - 1 else latent):
                        for c in range(MIXC):
                            if o == 0:
                                pe.wait_ge(u_ready, MIXC * l + c + 1)
                            ins = mm(bank(4 - 2 * j + o % 2, 0, n), slot(pn, 16)[:, c, :], y1[:, c, lo:lo + n],
                                     start=c == 0, stop=c == MIXC - 1)
                    ins.then_inc(out_ready, 1)
            norm(2, latent)

            pe.wait_ge(tables2_in, 48)
            pe.wait_ge(pads_done, 5)
            with pe.Fori(0, DEPTH) as l:
                o = Off(l)
                hbase = DEPTH * KC + l * 2 * KC
                norm(3 + l * 2, latent)
                pe.wait_ge(lyr_in, 32 + l * 32)
                for c in range(KC):
                    pe.wait_ge(h_ready, hbase + c + 1)
                    ins = mm(bank(3)[0:4], ffw[:, c, :], hl[:, c, :], start=c == 0, stop=c == KC - 1)
                ins.then_inc(ff_ready, 1)
                for m in range(20):
                    n = N1 + m // 2
                    if m % 2 == 0:
                        panel_wait(pe, n, l)
                    pe.wait_ge(proj_taken, NPROJ1 + m - 1 + l * 20)
                    for c in range(KC):
                        ins = mm(bank(m % 2), slot(n)[:, c, P * (m % 2):P * (m % 2) + P], hl[:, c, :], start=c == 0, stop=c == KC - 1)
                    ins.then_inc(proj_ready, 1)
                pe.wait_ge(proj_taken, NPROJ1 + 20 + l * 20)
                for j in range(4):
                    swap_halves(u2[:, 4 + j, :], 10 * DEPTH + j + l * 4, j)
                pe.wait_ge(ff_log, 1 + l)
                for g in range(2):
                    for t in range(4):
                        ins = nc.tensor.transpose(bank(2 + g, P * t, P * t + P), u2[:, 8 + g, P * t:P * t + P], ident)
                    ins.then_inc(rv_ready, 1)
                pe.wait_ge(rope_done, 10 * DEPTH + 4 + l * 4)
                pe.wait_ge(rv_taken, 2 + l * 2)

                def decayed(i):
                    g, h, t = i // 8, i // 4, i % 4
                    n = SEQ - P * t
                    pe.wait_ge(rs_done, i + 1 + l * 16)
                    mm(bank(g, P * t, 512), pv_pair(vret[:, g, t, :], h), ret_s[:, i % 4, 0:n], start=i % 8 == 0, stop=i % 8 == 7,
                       skip_group_check=True).then_inc(ro_steps, 1)

                for i in range(16):
                    g, h, t = i // 8, i // 4, i % 4
                    r, n = rows_of(h), SEQ - P * t
                    if i >= 4:
                        pe.wait_ge(rs_done, i - 3 + l * 16)
                    mm(bank(4 + i % 4, 0, n), u2[r, 6 + g, P * t:P * t + P], u2[r, 4 + g, P * t:SEQ], start=True, stop=True).then_inc(rs_ready, 1)
                    if i >= 2:
                        decayed(i - 2)
                decayed(14)
                decayed(15)
                pe.wait_ge(conv_done, 1 + l)
                for t in range(2):
                    ins = mm(bank(6), ones, conv[:, t, :], start=t == 0, stop=t == 1)
                ins.then_inc(ln_sum, 1)
                for g in range(2):
                    pe.wait_ge(ro_taken, g + 1 + l * 2)
                    mm(bank(2 + g), pairs, ret_o[:, g, :], start=True, stop=True).then_inc(gn_sum, 1)
                for t in range(2):
                    pe.wait_ge(ln_sq, t + 1 + l * 2)
                    ins = mm(bank(7), ones, squares[:, t, 0:SEQ], start=t == 0, stop=t == 1)
                ins.then_inc(ln_var, 1)
                for g in range(2):
                    pe.wait_ge(gn_sq, g + 1 + l * 2)
                    mm(bank(2 + g), pairs, squares[:, g, 0:SEQ], start=True, stop=True).then_inc(gn_var, 1)
                pe.wait_ge(pool_done, 1 + l)
                for t in range(2):
                    mm(bank(4 + t), poolw[:, t, :], pooled[:, t, :], start=True, stop=True).then_inc(pool_proj, 1)
                pe.wait_ge(pool_mix, 2 + l * 2)
                pe.wait_ge(ret_mix, 2 + l * 2)
                pe.wait_ge(conv_mix, 2 + l * 2)
                pe.wait_ge(aug_in, 128 + l * 128)
                attention_pe(pe, fox_plan, o)
                pe.wait_ge(y_done, at["u"] + o.u)
                for i in range(KC):
                    n = N1 + N_IN2 + i // 2
                    if i % 2 == 0:
                        panel_wait(pe, n, l)
                    if i >= 2:
                        pe.wait_ge(x_ready, NX1 + i - 1 + l * 2 * KC)
                    for c in range(KC):
                        ins = mm(bank(i % 2), slot(n)[:, c, P * (i % 2):P * (i % 2) + P], mix2[:, c, :], start=c == 0, stop=c == KC - 1)
                    ins.then_inc(out_ready, 1)
                norm(4 + l * 2, latent)
                for i in range(N_FF):
                    for w, ready in ((0, h1_ready), (1, h3_ready)):
                        n = N1 + N_IN2 + N_OUT2 + 2 * i + w
                        panel_wait(pe, n, l)
                        if i >= 2 and w == 0:
                            pe.wait_ge(f_ready, 2 * i - 2 + l * FFC)
                        for b in range(2):
                            for c in range(KC):
                                if i == 0 and w == 0 and b == 0:
                                    pe.wait_ge(h_ready, hbase + KC + c + 1)
                                ins = mm(bank(4 * (i % 2) + 2 * w + b), slot(n)[:, c, P * b:P * b + P], hl[:, c, :],
                                         start=c == 0, stop=c == KC - 1)
                            ins.then_inc(ready, 1)
                pe.wait_ge(f_ready, FFC + l * FFC)
                for g in range(N_OUT2):
                    if g >= 2:
                        pe.wait_ge(x_ready, NX1 + KC + 2 * g - 2 + l * 2 * KC)
                    for j, (a, e) in enumerate(W2_CUT):
                        n = N1 + N_IN2 + N_OUT2 + 2 * N_FF + len(W2_CUT) * g + j
                        panel_wait(pe, n, l)
                        for b in range(2):
                            for c in range(a, e):
                                ins = mm(bank(2 * (g % 2) + b), slot(n)[:, c - a, P * b:P * b + P], act2[:, c, :],
                                         start=c == 0, stop=c == FFC - 1)
                            if j == len(W2_CUT) - 1:
                                ins.then_inc(out_ready, 1)
                        if j < len(W2_CUT) - 1:
                            ins.then_inc(w2_used, 1)
            norm(3 + 2 * DEPTH, latent)


_hi = float(np.float32(np.round(2 * np.pi * 128) / 128))
_mid = float(np.float32(np.round((2 * np.pi - _hi) * 2.0 ** 19) / 2.0 ** 19))
TWO_PI = (_hi, _mid, float(np.float32(2 * np.pi - _hi - _mid)))


def _tables():
    t = np.arange(SEQ)
    d = np.arange(P) % HD
    freq = 10000.0 ** (-np.arange(16) / 16.0)
    ang = np.concatenate([(t // GRID)[:, None] * freq, (t % GRID)[:, None] * freq], axis=1).T
    rope = np.stack([np.cos(ang)[d % 32], np.where(d < 32, -1.0, 1.0)[:, None] * np.sin(ang)[d % 32]], axis=1)
    i = np.arange(P)
    mats = np.stack([np.eye(P), i[:, None] == (i ^ 32)[None, :], -1.0 * (i[:, None] == (ROWS - 1 - i % ROWS)[None, :] * NBC + (NBC - 1 - i // ROWS)[None, :]),
                     i[:, None] // HD == i[None, :] // HD, np.ones((P, P))], axis=1)
    bmask = np.zeros((P, 4, CTX))
    cl, j = np.arange(P) // ROWS, np.arange(BAND)
    for v, lo in enumerate((np.maximum(cl - 8, 0), cl, np.minimum(cl + 8, 16))):
        seen = (j[None, :] >= lo[:, None]) & (j[None, :] < lo[:, None] + NBC)
        bmask[:, v + 1, :] = np.repeat(np.where(seen, 0.0, NOT_SEEN), ROWS, axis=1)
    cmask = np.zeros((P, 641))
    cmask[:, 0:P] = np.where(i[None, :] >= i[:, None], 0.0, NOT_SEEN)
    cmask[:, 512:640] = np.where(i[None, :] <= i[:, None], 0.0, NOT_SEEN)
    fmask = np.where(i[None, :] <= i[:, None], 0.0, NOT_SEEN)
    lg = np.log(1.0 - 2.0 ** (-5.0 - np.arange(4)))
    diff = np.arange(SEQ)[None, :] - i[:, None]
    decay = np.stack([np.where(diff >= 0, np.exp(g * np.maximum(diff, 0)), 0.0) for g in lg], axis=1)
    counts = np.zeros((P, 2, SEQ))
    for g, w in enumerate((2, 4, 8, 16)):
        counts[HD * (g % 2):HD * (g % 2) + HD, g // 2] = 1.0 / np.minimum(t + 1, w)
    minus_one = np.full((1, P), -1.0)
    inv = 10000.0 ** (-(d % 32) / 32.0)
    sign = np.where(d < 32, -1.0, 1.0)
    f = lambda a: np.ascontiguousarray(a, dtype=np.float32)
    return {k: f(v) for k, v in dict(rope=rope, mats=mats, bmask=bmask, cmask=cmask, fmask=fmask, decay=decay,
                                     counts=counts, minus_one=minus_one, inv=inv, sign=sign).items()}


def _features(v):
    return np.ascontiguousarray(v.reshape(-1, P).T)


def _panels(w, chunks, cols):
    L, _, n = w.shape
    return np.ascontiguousarray(
        w.reshape(L, chunks, P, n // cols, cols).transpose(0, 3, 2, 1, 4)).reshape(L, n // cols, P, chunks * cols)


def _layout(a):
    t = _tables()
    dup = lambda v: np.concatenate([v, v], axis=1).T
    c = np.stack([_features(a["c"]), _features(a["c_ctx"])], axis=2).reshape(P, 2 * KC)
    prm = np.concatenate([c, _features(a["c_2"]), _features(a["ada_b"]), _features(a["norm_w"]), _features(a["final_norm_w"]),
                          dup(a["q_norm_a"]), dup(a["k_norm_a"]), _features(a["final_g_2"]),
                          t["inv"][:, None], t["sign"][:, None]], axis=1)
    lyr = []
    for l in range(DEPTH):
        fb = np.zeros((P, 1), a["fox_fb_2"].dtype)
        fb[0:4, 0] = a["fox_fb_2"][l]
        conv_w = a["conv_w_2"][l].reshape(CONV, 2, P).transpose(2, 1, 0).reshape(P, 2 * CONV)
        lyr.append(np.concatenate([_features(a[k][l]) for k in (
            "ada_b_2", "norm_mix_g_2", "norm_ffn_g_2", "pool_scale_2", "ret_gn_g_2", "conv_b_2", "conv_ln_g_2", "conv_ln_b_2")]
            + [conv_w, fb], axis=1))
    w2in = a["w_in_2"]
    at = dict(fq=0, fk=256, fv=512, pu=772, rq=1028, rk=1284, rv=1540, rg=1796, ca=2052, cg=2308)
    order = ("ca", "cg", "rq", "rk", "rv", "rg", "pu", "fq", "fk", "fv")
    in2 = np.concatenate([w2in[:, :, at[k]:at[k] + 256] for k in order], axis=2)
    ffw = w2in[:, :, 768:772].reshape(DEPTH, KC, P, 4).transpose(0, 2, 1, 3).reshape(DEPTH, P, KC * 4)
    poolw = np.zeros((DEPTH, P, 2, P), a["pool_w_2"].dtype)
    for g in range(4):
        r = slice(HD * (g % 2), HD * (g % 2) + HD)
        poolw[:, r, g // 2, r] = a["pool_w_2"][:, g]
    rpb = np.zeros((DEPTH, HEADS, 15, 64), a["rpb_b"].dtype)
    rpb[:, :, :, 16:47] = a["rpb_b"]
    feat = lambda x: x[0].T.reshape(KC, P, -1).transpose(1, 0, 2)
    arrays = dict(
        prm=prm, lyr=np.stack(lyr, axis=1), x=feat(a["x"]), ctx=feat(a["ctx"]), rpb=rpb,
        sinks=a["sink_c"].reshape(1, -1), pos=a["positions_2"].reshape(1, SEQ),
        ada1=_panels(a["ada_w"], KC, PAN), in1=_panels(a["w_in"], KC, PAN), out1=_panels(a["w_out"], MIXC, P),
        ada2=_panels(a["ada_w_2"], KC, PAN), in2=_panels(in2, KC, PAN), out2=_panels(a["w_out_2"], KC, PAN),
        w1=_panels(a["ffn_w1_2"], KC, PAN), w3=_panels(a["ffn_w3_2"], KC, PAN), w2=_panels(a["ffn_w2_2"], FFC, PAN),
        ffw=ffw, poolw=poolw.reshape(DEPTH, P, 2 * P),
        **{k: t[k] for k in ("rope", "mats", "bmask", "cmask", "fmask", "decay", "counts", "minus_one")})
    return {k: np.ascontiguousarray(v) for k, v in arrays.items()}


def kernel(**inputs):
    import concourse.bacc as bacc
    from concourse.bass_utils import run_bass_kernel_spmd

    arrays = {f"in_{k}": v for k, v in _layout({k: np.asarray(v) for k, v in inputs.items()}).items()}
    nc = bacc.Bacc("TRN2", target_bir_lowering=False, num_devices=1)
    dram = {k[3:]: nc.dram_tensor(k, v.shape, mybir.dt.from_np(v.dtype), kind="ExternalInput").ap() for k, v in arrays.items()}
    out = nc.dram_tensor("out_features", (P, KC, SEQ), F32, kind="ExternalOutput").ap()
    two_dit_blocks(nc, dram, out)
    got = run_bass_kernel_spmd(nc, [arrays], core_ids=[0]).results[0]["out_features"]
    return np.ascontiguousarray(got.transpose(2, 1, 0).reshape(1, SEQ, DM))
```

```python
from contextlib import ExitStack

import numpy as np

import concourse.bass as bass
from concourse import mybir

F32 = mybir.dt.float32
F32R = mybir.dt.float32r
I32 = mybir.dt.int32
ACT = mybir.ActivationFunctionType
ALU = mybir.AluOpType
AX_X = mybir.AxisListType.X

P = 128
DM = 1024
KC = DM // P
SEQ, CTX = 512, 256
TOK = SEQ + CTX
DEPTH = 2
HD = 64
GRID = 64
ROWS = SEQ // GRID
NBC = 16
BAND_AT = (0, 8, 24, 32)
BAND = 32
NOT_SEEN = 1.0e30
HIGHEST = 3.0e38
EPS = 1e-6
QSCALE = HD ** -0.5
HEADS = 8

PAN = 256
W_IN = 4608
N_IN1 = W_IN // P
N_ADA1 = 3 * DM // PAN
N_SS1 = 2 * DM // PAN
N_ADA2 = 6 * DM // PAN
MIXC = 12
STAGE, WIDE = 4, 2
RAW1, SPLIT1 = 3, 2
FF = 2816
FFC = FF // P
HALF = FFC // 2
RAW, SPLIT = 5, 3
W2_CUT = [(0, 6), (6, HALF)]
N_IN2 = 21
PANELS2 = ([("in2", 0, i) for i in range(N_IN2)] + [("out2", 0, i) for i in range(KC)]
           + [p for f in range(2) for p in
              [(k, f, i) for i in range(HALF) for k in ("w1", "w3")]
              + [("w2", f, (o, j)) for o in range(KC) for j in range(len(W2_CUT))]])
PER2 = len(PANELS2)
assert PER2 % RAW == 0 and PER2 % SPLIT == 0
FFN_AT, FFN_PER = N_IN2 + KC, 2 * HALF + KC * len(W2_CUT)
OUTS2 = 3 * KC
CONV = 31
POOLPAD = 16
MAGIC = 1.5 * 2.0 ** 23
KEYS_FIRST = (4, 0, 1, 2, 3)
PHASES = {"A": (0, 6), "B": (6, 18), "C": (18, 24), "G": (24, N_IN1)}

PRM = {}
_at = 0
for _name, _n in (("c", 2 * KC), ("c2", KC), ("ada_b", DEPTH * 24), ("norm_w", DEPTH * KC), ("final_w", KC),
                  ("qn", DEPTH), ("kn", DEPTH), ("final_g", KC), ("inv", 1), ("sign", 1)):
    PRM[_name] = (_at, _n)
    _at += _n
N_PRM = _at
LYR = {}
_at = 0
for _name, _n in (("ada_b", 48), ("nmix", KC), ("nffn", KC), ("pool_scale", 2), ("gn", 2), ("conv_b", 2),
                  ("ln_g", 2), ("ln_b", 2), ("conv_w", 2 * CONV), ("fox_b", 1)):
    LYR[_name] = (_at, _n)
    _at += _n
N_LYR = _at


def make_plan(groups, at):
    plan, waiting = [], None
    base = dict(at)
    turns_seen = []

    def turn(kind, count, **more):
        ev = dict(kind=kind, i=len(turns_seen), t=at["t"], n=at[count], **more)
        if len(turns_seen) >= 2:
            ev["before"] = turns_seen[-2]
        turns_seen.append(ev)
        plan.append(ev)
        at["t"] += 1
        at[count] += 1

    def behind(lo, hi):
        u = waiting
        for j in range(lo, hi):
            turn("T", "v", unit=u, steps=u["events"][j], first=j == 0, last=j == len(u["events"]) - 1)
            u["t_last"], u["v_last"] = at["t"] - 1, at["v"] - 1

    def finish():
        plan.append(dict(kind="Y", unit=waiting))
        if waiting.get("closes") is not None:
            v_end.append(waiting["v_last"] + 1)

    v_end = []

    def values(g, some):
        for srcs, dst in some:
            turn("V", "w", src=srcs, dst=dst, need_group=g - 2, v_end=v_end)

    values(0, groups[0][0])
    for g, (_, units) in enumerate(groups):
        seen = at["w"]
        coming = list(groups[g + 1][0]) if g + 1 < len(groups) else []
        for i, u in enumerate(units):
            u["u"], u["local"], u["turned"] = at["u"], at["u"] - base["u"], seen
            at["u"] += 1
            u["events"], width = [[]], 0
            for step in u["steps"]:
                if width + P * len(step[1]) > 512:
                    u["events"].append([])
                    width = 0
                u["events"][-1].append(step)
                width += P * len(step[1])
            n = len(waiting["events"]) if waiting else 0
            k = len(u["q"])
            for qb in range(k):
                plan.append(dict(kind="S", s=at["s"], local=at["s"] - base["s"], unit=u, qb=qb))
                u["s_last"], u["s_last_local"] = at["s"], at["s"] - base["s"]
                at["s"] += 1
                if waiting:
                    behind(n * qb // k, n * (qb + 1) // k)
            if waiting:
                finish()
            waiting = u
            if i > 0:
                values(g + 1, coming[0:1])
                coming = coming[1:]
        values(g + 1, coming)
        units[-1]["closes"] = g
    behind(0, len(waiting["events"]))
    finish()
    return plan


def two_dit_blocks(nc, dram, kept, out):
    with ExitStack() as ctx:
        def sb(name, shape, dt=F32, scope=ctx):
            return scope.enter_context(nc.sbuf_tensor(name, shape, dt))

        def sem(name):
            return ctx.enter_context(nc.semaphore(name))

        prm = sb("vectors", [P, N_PRM])
        lyr = sb("layer_vectors", [P, DEPTH, N_LYR])
        mats = sb("matrices", [P, 5, P])
        ident, swap, minus_turn, pairs, ones = (mats[:, i, :] for i in range(5))
        head_of = sb("head_of", [P, 5, 10])
        of_head = sb("of_head", [10, 5, P])
        rot_c, rot_s = sb("rope_cos", [P, SEQ]), sb("rope_sin", [P, SEQ])
        silu_c = sb("silu_c", [P, KC, 2])
        silu_c2 = sb("silu_c2", [P, KC])
        scrap = sb("scrap", [P, 1])
        mod1 = sb("mod_first", [P, DEPTH, 24, 2])
        mod2 = sb("mod_second", [P, DEPTH, 48])
        gain1 = sb("gain_first", [P, 2, KC])
        rstd = sb("rstd", [P, TOK])
        probs = sb("probs", [P, 2, 2, TOK])
        squares, std = probs[:, 0, :, :], probs[:, 1, :, :]
        probs_t = sb("probs_turned", [P, 2, 512])
        row_min = sb("row_min", [P, 4])
        row_sum = sb("row_sum", [P, 4])
        weight = sb("row_weight", [P, 4])
        diag = sb("diagonal_weights", [P, 4, P])
        sinks = sb("minus_sinks", [P, DEPTH * HEADS])
        qn8 = sb("minus_q_norm_scaled", [P, DEPTH])

        first, second = ExitStack(), ExitStack()
        with first:
            f = lambda *a: sb(*a, scope=first)
            slots = f("qkv", [P, 12, TOK])
            wide = f("modulation_panels", [P, WIDE, KC * PAN])
            raw1 = f("panels_first", [P, RAW1, KC * P])
            split1 = f("split_panels_first", [P, SPLIT1, 2, KC * P], F32R)
            bias = f("bias_rows", [P, 2, ROWS, 48])
            bmask = f("band_masks", [P, 4, CTX])
            cmask = f("window_mask", [P, 641])
            projecting, updating = ExitStack(), ExitStack()
            with projecting:
                hs1 = sb("h_split_first", [P, 2, KC, TOK], F32R, projecting)
                y1 = sb("mixed_first", [P, MIXC, TOK], F32, projecting)
            with updating:
                u_hi = sb("gated_rounded", [P, MIXC, TOK], F32R, updating)
                sb("gap", [P, 2 * KC - MIXC, TOK], F32, updating)
                u_lo = sb("gated_rest", [P, MIXC, TOK], F32R, updating)
        x1 = slots[:, 0:KC, :]
        stage = y1[:, :, :].rearrange("p a b -> p (a b)")[:, 0:STAGE * KC * PAN].rearrange("p (s n) -> p s n", s=STAGE)
        vband = y1[:, 8:12, :].rearrange("p a b -> p (a b)")[:, 0:20 * P].rearrange(
            "p (s t c) -> p s t c", s=2, t=10)
        vseq = slots[:, 9:11, :].rearrange("p a (b c) -> p (a b c)", c=P).rearrange(
            "p (t g c) -> p t g c", t=6, g=2)
        with second:
            f = lambda *a: sb(*a, scope=second)
            hs = f("h_split", [P, 2, KC, SEQ], F32R)
            decay = f("decay", [P, 4, SEQ])
            xl = f("x_latent", [P, KC, SEQ])
            raw = f("panels", [P, RAW, KC * P])
            split = f("split_panels", [P, SPLIT, 2, KC * P], F32R)
            counts = f("pool_counts", [P, 2, SEQ])
            fmask = f("causal_mask", [P, P])[:, :]
            poolw = f("pool_weights", [P, 2, P])
            cur = f("this_layers_vectors", [P, N_LYR])
            mod = f("this_layers_mod", [P, 48])
            gain2 = f("gain_second", [P, 2, KC])
            mixing, feeding = ExitStack(), ExitStack()
            with mixing:
                f = lambda *a: sb(*a, scope=mixing)
                u2 = f("projected", [P, 20, SEQ])
                vfox = f("values_forgetting", [P, 2, 4, P])
                vret = f("values_retention", [P, 2, 4, 192])
                hpad = f("conv_in", [P, 2, CONV - 1 + SEQ])
                ppad = f("pool_in", [P, 2, POOLPAD + SEQ])
                psums = f("pool_sums", [P, 2, POOLPAD + SEQ])
                augq = f("decay_of_queries", [P, SEQ])
                augk = f("decay_of_keys", [P, SEQ])
            with feeding:
                acts = sb("ffn_hidden_split", [P, 2, HALF, SEQ], F32R, scope=feeding)
        split = split[:, :, :, :].rearrange("p s k (c n) -> p s k c n", c=KC)
        split1 = split1[:, :, :, :].rearrange("p s k (c n) -> p s k c n", c=KC)
        hm1 = probs[:, :, :, :].rearrange("p a b n -> p (a b) n")
        spare_probs = probs[:, :, :, :].rearrange("p a b n -> p (a b n)")[:, 0:4 * SEQ].rearrange("p (a n) -> p a n", a=4)
        hm2 = spare_probs
        ret_s = spare_probs
        conv = u2[:, 0:2, :]
        ret_o = u2[:, 4:6, :]
        pooled = u2[:, 12:14, :]
        ln_root, gn_root = hpad[:, 0, CONV - 1:], psums[:, :, POOLPAD:]
        angle = [probs_t[:, 0, :], probs_t[:, 1, :], diag[:, :, :].rearrange("p a b -> p (a b)")]
        fz, ft = (vfox[0:4, i, :, :].rearrange("p t c -> p (t c)") for i in range(2))
        gate_buf = squares

        ps = ctx.enter_context(nc.psum_tensor("ps", [P, 4096], F32))
        bank = lambda b, a=0, e=512: ps[:, 512 * b + a:512 * b + e]

        vec_in, mats_in, x_in, tables_in, lyr_vec_in = (
            sem(n) for n in ("vec_in", "mats_in", "x_in", "tables_in", "lyr_vec_in"))
        stage_in = [sem(f"stage_in{i}") for i in range(STAGE)]
        wide_in = [sem(f"wide_in{i}") for i in range(WIDE)]
        raw1_in = [sem(f"raw1_in{i}") for i in range(RAW1)]
        rounded1, rest1_done, x_kept, x_back = (sem(n) for n in ("rounded1", "rest1_done", "x_kept", "x_back"))
        silu_done = sem("silu_done")
        part_ready, mod_ready, mod_taken = sem("part_ready"), sem("mod_ready"), sem("mod_taken")
        x_ready = sem("x_ready")
        sq_ready, sq_summed, std_ready = sem("sq_ready"), sem("sq_summed"), sem("std_ready")
        hm_ready, h_ready = sem("hm_ready"), sem("h_ready")
        proj_ready, proj_taken = sem("proj_ready"), sem("proj_taken")
        qn_scaled, qsq_ready, qsum_ready, qstd_ready, qrec_ready, qn_sums, qn_done = (
            sem(n) for n in ("qn_scaled", "qsq_ready", "qsum_ready", "qstd_ready", "qrec_ready", "qn_sums", "qn_done"))
        sw_ready, rope_done, kdup_done = sem("sw_ready"), sem("rope_done"), sem("kdup_done")
        bias_in = [sem("bias_in0"), sem("bias_in1")]
        s_ready, max_ready, exp_done, diag_ready = (sem(n) for n in ("s_ready", "max_ready", "exp_done", "diag_ready"))
        turned, pt_taken, values_taken = sem("turned"), sem("pt_taken"), sem("values_taken")
        pv_steps, y_done = sem("pv_steps"), sem("y_done")
        u_ready = sem("u_ready")
        out_half, out_ready = sem("out_half"), sem("out_ready")
        u_rounded, u_split = sem("u_rounded"), sem("u_split")
        tables2_in, pos_in, pads_done = sem("tables2_in"), sem("pos_in"), sem("pads_done")
        angle_done, sines_done, ret_trig = sem("angle_done"), sem("sines_done"), sem("ret_trig")
        lyr_in, cur_done = sem("lyr_in"), sem("cur_done")
        conv_done, ln_sum, ln_dev, ln_sq, ln_var, ln_std, ln_norm, conv_mix = (
            sem(n) for n in ("conv_done", "ln_sum", "ln_dev", "ln_sq", "ln_var", "ln_std", "ln_norm", "conv_mix"))
        rv_ready, rv_taken = sem("rv_ready"), sem("rv_taken")
        rs_ready, rs_done, ro_steps, ro_taken = (sem(n) for n in ("rs_ready", "rs_done", "ro_steps", "ro_taken"))
        gn_sum, gn_dev, gn_sq, gn_var, gn_std, ret_mix = (
            sem(n) for n in ("gn_sum", "gn_dev", "gn_sq", "gn_var", "gn_std", "ret_mix"))
        pool_done, pool_proj, pool_mix = sem("pool_done"), sem("pool_proj"), sem("pool_mix")
        ff_log, ff_cum, aug_in = sem("ff_log"), sem("ff_cum"), sem("aug_in")
        raw_in = [sem(f"raw_in{i}") for i in range(RAW)]
        rounded, first_rest, rest_done = sem("rounded"), sem("first_rest"), sem("rest_done")
        hh_ready, conv_hi, pool_hi = sem("hh_ready"), sem("conv_hi"), sem("pool_hi")
        h1_ready, h3_ready, silu_ready, f_ready = (
            sem(n) for n in ("h1_ready", "h3_ready", "silu_ready", "f_ready"))
        w2_used = sem("w2_used")
        result_ready, result_out = sem("result_ready"), sem("result_out")

        def vec(name, i=0, n=1):
            return prm[:, PRM[name][0] + i:PRM[name][0] + i + n]

        def lvec(name, i=0, n=1):
            return cur[:, LYR[name][0] + i:LYR[name][0] + i + n]

        MA, MB, MC = 0, 6, 18
        rows_of = lambda h: slice(HD * (h % 2), HD * (h % 2) + HD)

        def pv_pair(tile, h):
            return tile[:, 0:P] if h % 2 == 0 else tile[:, HD:HD + P]

        def seq_units(mixer, l):
            units = []
            for h in range(HEADS):
                kv, r = h // 4, rows_of(h)
                q, k = slots[r, h // 2, :], slots[r, 6 + kv, :]
                y = y1[r, (0 if mixer == "A" else 8) + h // 2, :]
                for pair in range(2):
                    qbs = [2 * pair, 2 * pair + 1]
                    u = dict(h=h, q=[q[:, P * b:P * b + P] for b in qbs], seg=[], extra=[], w=[], mask=[], steps=[],
                             dst=y[:, 256 * pair:256 * pair + 256])
                    cols = []
                    for b in qbs:
                        if mixer == "A":
                            u["seg"].append([(0, k[:, 0:SEQ]), (SEQ, k[:, SEQ:TOK])])
                            u["w"].append(TOK)
                            u["mask"].append(None)
                            u["extra"].append([])
                            cols.append({t: P * t for t in range(6)})
                            continue
                        at, seg, col = 0, [], {}
                        if b > 0:
                            seg.append((0, k[:, P * (b - 1):P * b]))
                            col[b - 1] = 0
                            at = P
                        seg.append((at, k[:, SEQ:TOK]))
                        col[4], col[5] = at, at + P
                        at += CTX
                        for t in range(b, min(b + 2, 4)):
                            seg.append((at, k[:, P * t:P * t + P]))
                            col[t] = at
                            at += P
                        u["seg"].append(seg)
                        u["extra"].append([])
                        u["sink"] = l * HEADS + h
                        u["w"].append(at + 1)
                        first_col = 0 if b > 0 else P
                        u["mask"].append(cmask[:, first_col:first_col + at + 1])
                        cols.append(col)
                    for t in [4, 5, 0, 1, 2, 3]:
                        has = [i for i in range(2) if t in cols[i]]
                        if has:
                            u["steps"].append((vseq[:, t, kv, :], [(i, cols[i][t]) for i in has]))
                    units.append(u)
            return units

        def context_units(mixer, l):
            units = []
            for h in range(HEADS):
                r = rows_of(h)
                if mixer == "B":
                    q, k, y0 = slots[r, h // 2, :], slots[r, 4 + h // 2, :], 4
                else:
                    q, k, y0 = slots[r, h // 2, :], slots[r, 6 + h // 4, :], 0 if mixer == "A" else 8
                u = dict(h=h, q=[], seg=[], extra=[], w=[], mask=[], steps=[],
                         dst=y1[r, y0 + h // 2, SEQ:TOK])
                for b in range(2):
                    u["q"].append(q[:, SEQ + P * b:SEQ + P * b + P])
                    u["seg"].append([(0, k[:, SEQ:TOK])])
                    u["mask"].append(None)
                    u["extra"].append([])
                    if mixer == "C":
                        u["sink"] = l * HEADS + h
                    u["w"].append(CTX + 1 if mixer == "C" else CTX)
                for t in range(2):
                    lhs = vband[:, h // 2 % 2, t, :] if mixer == "B" else vseq[:, 4 + t, h // 4, :]
                    u["steps"].append((lhs, [(0, P * t), (1, P * t)]))
                units.append(u)
            return units

        def grid(ap):
            return ap.rearrange("p (r c) -> p r c", c=GRID)

        def band_units(h, l):
            r = rows_of(h)
            q, k = slots[r, h // 2, :], slots[r, 4 + h // 2, :]
            y = grid(y1[r, 4 + h // 2, 0:SEQ])
            units = []
            for pair in range(2):
                u = dict(h=h, q=[], seg=[], extra=[], w=[], mask=[], steps=[], bias=(l * HEADS + h) if pair == 0 else None,
                         dst=y[:, :, 32 * pair:32 * pair + 32].rearrange("p r c -> p c r"))
                for i in range(2):
                    b = 2 * pair + i
                    k0 = BAND_AT[b]
                    off = NBC + BAND_AT[b] - NBC * b
                    u["q"].append(q[:, P * b:P * b + P])
                    u["seg"].append([(0, k[:, SEQ:TOK]), (CTX, k[:, ROWS * k0:ROWS * (k0 + BAND)])])
                    u["extra"].append([(CTX, minus_turn, bias[:, h % 2, :, off:off + BAND].rearrange("p k j -> p j k"))])
                    u["w"].append(SEQ)
                    v = [1, 2, 2, 3][b]
                    u["mask"].append(bmask[:, 0:v + 1:v, :])
                for t in range(2):
                    u["steps"].append((vband[:, h // 2 % 2, t, :], [(0, P * t), (1, P * t)]))
                for i in range(2):
                    for half in range(2):
                        u["steps"].append((vband[:, h // 2 % 2, 2 + 2 * (2 * pair + i) + half, :], [(i, CTX + P * half)]))
                units.append(u)
            units[-1]["bias_end"] = True
            return units

        def seq_turns():
            out = []
            for t, e in ((0, 4), (4, 6)):
                dst = vseq[:, t:e, :, :].rearrange("p t g (d c) -> p t g d c", c=HD)
                out.append(([slots[:, 5, P * i:P * i + P] for i in range(t, e)], [dst[:, :, :, d, :] for d in range(2)]))
            return out

        def band_turns(p):
            v = slots[:, 8 + p, :]
            src = [v[:, SEQ + P * t:SEQ + P * t + P] for t in range(2)]
            for b in range(4):
                for half in range(2):
                    at0 = ROWS * BAND_AT[b] + P * half
                    src.append(v[:, at0:at0 + P])
            return [(src[t:t + 4], [vband[:, p % 2, t:min(t + 4, 10), :]]) for t in range(0, 10, 4)]

        at = dict(s=0, t=0, v=0, w=0, u=0)
        plans = {}
        for l in range(DEPTH):
            full = l < DEPTH - 1
            for m in "ABC":
                if m == "B":
                    groups = []
                    for p in range(4):
                        units = []
                        for h in (2 * p, 2 * p + 1):
                            units += band_units(h, l)
                        if full:
                            units += [u for u in context_units("B", l) if u["h"] // 2 == p]
                        groups.append((band_turns(p), units))
                else:
                    groups = [(seq_turns(), seq_units(m, l) + (context_units(m, l) if full else []))]
                plans[l, m] = (make_plan(groups, at), at["u"])
        start2 = dict(at)

        def fox_units():
            units = []
            for h in range(4):
                r = rows_of(h)
                q, k = u2[r, 14 + h // 2, :], u2[r, 16 + h // 2, :]
                for pair in range(2):
                    u = dict(h=h, q=[], seg=[], extra=[], w=[], mask=[], steps=[],
                             dst=hs[r, 0, h // 2, 256 * pair:256 * pair + 256],
                             rest=hs[r, 1, h // 2, 256 * pair:256 * pair + 256])
                    for b in (2 * pair, 2 * pair + 1):
                        w = P * (b + 1)
                        u["q"].append(q[:, P * b:P * b + P])
                        u["seg"].append([(0, k[:, 0:w])])
                        u["extra"].append([(0, augq[32 * h:32 * h + 2, P * b:P * b + P], augk[32 * h:32 * h + 2, 0:w])])
                        u["w"].append(w)
                        u["mask"].append("last tile")
                    for t in range(2 * pair + 2):
                        has = [i for i in range(2) if t <= 2 * pair + i]
                        u["steps"].append((vfox[:, h // 2, t, :], [(i, P * t) for i in has]))
                    units.append(u)
            return units

        def fox_turns():
            return [([u2[:, 18 + p, P * t:P * t + P] for t in range(4)], [vfox[:, p, :, :]]) for p in range(2)]

        fox_plan = make_plan([(fox_turns(), fox_units())], at)
        per = {k: at[k] - start2[k] for k in at}

        class Off:
            def __init__(self, l):
                zero = l is None
                self.s = 0 if zero else l * per["s"]
                self.t = 0 if zero else l * per["t"]
                self.v = 0 if zero else l * per["v"]
                self.w = 0 if zero else l * per["w"]
                self.u = 0 if zero else l * per["u"]

        def scores_at(s, n):
            return ps[:, 2048 + 1024 * (s % 2):2048 + 1024 * (s % 2) + n]

        def turned_at(ev, n):
            return bank(2 + ev["i"] % 2)[:, 0:n]

        def pieces(ev):
            at0, out = 0, []
            for lhs, tiles in ev["steps"]:
                n = P * len(tiles)
                out.append((at0, lhs, P * tiles[0][0], n, tiles))
                at0 += n
            return out, at0

        def attention_pe(pe, plan, o):
            pend = None

            def multiply(ev):
                u = ev["unit"]
                pe.wait_ge(pt_taken, ev["n"] + 1 + o.v)
                if ev["first"]:
                    pe.wait_ge(values_taken, u["turned"] + o.w)
                    if u["local"] >= 2:
                        pe.wait_ge(y_done, u["u"] - 1 + o.u)
                steps, _ = pieces(ev)
                for j, (at0, lhs, col, n, _) in enumerate(steps):
                    ins = nc.tensor.matmul(bank(u["local"] % 2, col, col + n), lhs, probs_t[:, ev["n"] % 2, at0:at0 + n],
                                           start=ev["first"] and j == 0, stop=ev["last"] and j == len(steps) - 1,
                                           skip_group_check=True)
                ins.then_inc(pv_steps, 1)

            for ev in plan:
                u = ev.get("unit")
                if ev["kind"] == "S":
                    qb = ev["qb"]
                    if ev["local"] >= 2:
                        pe.wait_ge(exp_done, ev["s"] - 1 + o.s)
                    if qb == 0 and u.get("bias") is not None:
                        pe.wait_ge(bias_in[u["bias"] % 2], 16 * ROWS * (u["bias"] // 2 + 1))
                    S = scores_at(ev["local"], 1024)
                    for col, rhs in u["seg"][qb]:
                        n = rhs.free_size()
                        assert col // 512 == (col + n - 1) // 512
                        ins = nc.tensor.matmul(S[:, col:col + n], u["q"][qb], rhs, start=True, stop=True, skip_group_check=True)
                    for col, lhs, rhs in u["extra"][qb]:
                        n = rhs.free_size()
                        ins = nc.tensor.matmul(S[:, col:col + n], lhs, rhs, start=False, stop=True, skip_group_check=True)
                    ins.then_inc(s_ready, 1)
                elif ev["kind"] in "TV":
                    if "before" in ev:
                        b = ev["before"]
                        if b["kind"] == "T":
                            pe.wait_ge(pt_taken, b["n"] + 1 + o.v)
                        else:
                            pe.wait_ge(values_taken, b["n"] + 1 + o.w)
                    if ev["kind"] == "T":
                        if ev["first"]:
                            pe.wait_ge(diag_ready, u["s_last"] + 1 + o.s)
                        for at0, _, _, _, tiles in pieces(ev)[0]:
                            for j, (i, c) in enumerate(tiles):
                                ins = nc.tensor.matmul(turned_at(ev, 512)[:, at0 + P * j:at0 + P * j + P],
                                                       probs[:, u["local"] % 2, i, c:c + P],
                                                       diag[:, (u["s_last_local"] - 1 + i) % 4, :], start=True, stop=True,
                                                       skip_group_check=True)
                    else:
                        for i, x in enumerate(ev["src"]):
                            ins = nc.tensor.transpose(turned_at(ev, 512)[:, P * i:P * i + P], x, ident)
                    ins.then_inc(turned, 1)
                    if pend:
                        multiply(pend)
                    pend = ev if ev["kind"] == "T" else None
                else:
                    if pend:
                        multiply(pend)
                    pend = None

        def attention_dve(dve, plan, o, between=()):
            V = nc.vector
            ends, between = {}, list(between)
            for ev in plan:
                u = ev.get("unit")
                if ev["kind"] == "S":
                    s, w, mask = ev["local"] % 4, u["w"][ev["qb"]], u["mask"][ev["qb"]]
                    S = scores_at(ev["local"], w)
                    dve.wait_ge(s_ready, ev["s"] + 1 + o.s)
                    if "sink" in u:
                        V.tensor_copy(S[:, w - 1:w], sinks[:, u["sink"]:u["sink"] + 1])
                        dve.drain()
                    if mask == "last tile":
                        V.tensor_tensor(S[:, w - P:w], S[:, w - P:w], fmask, ALU.add)
                        dve.drain()
                        mask = None
                    if mask is None:
                        V.tensor_reduce(row_min[:, s:s + 1], S, AX_X, ALU.min).then_inc(max_ready, 1)
                    else:
                        if len(mask.shape) == 3:
                            S = S.rearrange("p (a n) -> p a n", a=2)
                        V.tensor_tensor_reduce(out=S, in0=S, in1=mask, scale=1.0, scalar=HIGHEST, op0=ALU.add,
                                               op1=ALU.min, accum_out=row_min[:, s:s + 1]).then_inc(max_ready, 1)
                    if between:
                        dve.drain()
                        between.pop(0)()
                    dve.wait_ge(exp_done, ev["s"] + 1 + o.s)
                    V.reciprocal(weight[:, s:s + 1], row_sum[:, s:s + 1])
                    dve.drain()
                    if u["local"] - 2 in ends:
                        dve.wait_ge(turned, ends[u["local"] - 2] + 1 + o.t)
                    V.tensor_scalar(diag[:, s, :], ident, weight[:, s:s + 1], None, ALU.mult).then_inc(diag_ready, 1)
                elif ev["kind"] == "T":
                    ends[u["local"]] = ev["t"]
                elif ev["kind"] == "V":
                    dve.wait_ge(turned, ev["t"] + 1 + o.t)
                    if ev["need_group"] >= 0:
                        dve.wait_ge(pv_steps, ev["v_end"][ev["need_group"]] + o.v)
                    src = turned_at(ev, P * len(ev["src"])).rearrange("p (t g c) -> p t g c", g=2, c=HD)
                    for d in ev["dst"]:
                        if len(d.shape) == 3:
                            d = d.rearrange("p t (g c) -> p t g c", c=HD)
                        ins = V.tensor_copy(d, src)
                    ins.then_inc(values_taken, 1)
                else:
                    dve.wait_ge(pv_steps, u["v_last"] + 1 + o.v)
                    a, d = bank(u["local"] % 2, 0, 256)[rows_of(u["h"])], u["dst"]
                    if len(d.shape) == 3:
                        a = a.rearrange("p (c r) -> p c r", r=ROWS)
                    ins = V.tensor_copy(d, a)
                    if "rest" in u:
                        dve.drain()
                        ins = V.tensor_tensor(u["rest"], a, d.bitcast(F32), ALU.subtract)
                    ins.then_inc(y_done, 1)

        def attention_act(act, plan, o, between=()):
            ends, held, between = {}, None, list(between)

            def exponentials(ev):
                u = ev["unit"]
                s, w = ev["local"] % 4, u["w"][ev["qb"]]
                act.wait_ge(max_ready, ev["s"] + 1 + o.s)
                if ev["qb"] == 0 and u["local"] - 2 in ends:
                    act.wait_ge(turned, ends[u["local"] - 2] + 1 + o.t)
                nc.scalar.activation(probs[:, u["local"] % 2, ev["qb"], 0:w], scores_at(ev["local"], w), ACT.Exp,
                                     bias=row_min[:, s:s + 1], scale=-1.0, accum_out=row_sum[:, s:s + 1]).then_inc(exp_done, 1)
                if between:
                    between.pop(0)()

            for ev in plan:
                if ev["kind"] == "S":
                    if held:
                        exponentials(held)
                    held = ev
                elif ev["kind"] == "T":
                    ends[ev["unit"]["local"]] = ev["t"]
                    n = pieces(ev)[1]
                    act.wait_ge(turned, ev["t"] + 1 + o.t)
                    if ev["n"] >= 2:
                        act.wait_ge(pv_steps, ev["n"] - 1 + o.v)
                    nc.scalar.copy(probs_t[:, ev["n"] % 2, 0:n], turned_at(ev, n)).then_inc(pt_taken, 1)
                    if held:
                        exponentials(held)
                    held = None

        ADA1, ADA2, IN1, OUT1 = "ada1", "ada2", "in1", "out1"
        later = ([(ADA1, 0, i) for i in range(N_SS1, N_ADA1)] + [(ADA1, 1, i) for i in range(N_ADA1)]
                 + [(ADA2, l, i) for l in range(DEPTH) for i in range(N_ADA2)])
        spare, free = {}, list(later)
        for l in range(DEPTH):
            for lo, hi in PHASES.values():
                for b in range(lo, hi - 1):
                    spare[l, b] = free.pop(0)
        assert not free
        first_mod = [(ADA1, 0, i) for i in range(N_SS1)]
        stream = []
        for l in range(DEPTH):
            for b in range(N_IN1):
                stream += [(IN1, l, b)] + ([spare[l, b]] if (l, b) in spare else [])
            stream += [(OUT1, l, i) for i in range(2 * KC)]
        main_seq = [p for p in stream if p[0] in (IN1, OUT1)]
        main_no = {p: n for n, p in enumerate(main_seq)}
        N_MAIN = len(main_seq)
        wide_seq = [p for p in stream if p not in main_no]
        ANGLES_AT = IN1, DEPTH - 1, PHASES["G"][0] + 3
        wide_no = {p: n for n, p in enumerate(wide_seq)}
        ada_seq = first_mod + wide_seq
        ada_no = {p: n for n, p in enumerate(ada_seq)}
        n_mod1 = {l: ada_no[ADA1, l, N_SS1 - 1] + 1 for l in range(DEPTH)}
        n_gate1 = {l: ada_no[ADA1, l, N_ADA1 - 1] + 1 for l in range(DEPTH)}

        def wide_slot(p):
            return wide[:, wide_no[p] % WIDE, :].rearrange("p (c n) -> p c n", c=KC)

        def wide_wait(eng, p):
            eng.wait_ge(wide_in[wide_no[p] % WIDE], 16 * (wide_no[p] // WIDE + 1))

        NSEQ = {(l, b): l * N_IN1 + b for l in range(DEPTH) for b in range(N_IN1)}
        def blocks_of(l, m):
            lo, hi = PHASES[m]
            last = l == DEPTH - 1
            return [(b, SEQ if last and (m == "G" or b - lo < 4) else TOK) for b in range(lo, hi)]

        NPROJ1 = len(NSEQ)
        NX1 = DEPTH * KC + KC
        out_tokens = lambda l: TOK if l < DEPTH - 1 else SEQ
        slot_of = lambda b: b if b < 6 else b - 6 if b < 18 else b - 18

        def parts_made(k):
            return part_ready, k // 2 + 1 if k < N_SS1 else k - N_SS1 + N_SS1 // 2 + 1

        def products(k):
            at = slots[:, 8 + k // 2, 0:2 * PAN] if k < N_SS1 else std[:, k % 2, 0:2 * PAN]
            return at.rearrange("p (v n) -> p v n", v=2)

        def stage_wait(eng, k):
            eng.wait_ge(stage_in[k % STAGE], 16 * (k // STAGE + 1))

        def main_used(n):
            kind, l, i = main_seq[n]
            if kind == IN1:
                return proj_ready, NSEQ[l, i] + 1
            return (out_half if i % 2 == 0 else out_ready), l * KC + i // 2 + 1

        def main_size(n):
            return P * (KC if main_seq[n][0] == IN1 else MIXC // 2)

        def flat1(n, k):
            return split1[:, n % SPLIT1, k, :, :].rearrange("p c n -> p (c n)")[:, 0:main_size(n)]

        def used2(n, l):
            kind, f, j = PANELS2[n]
            if kind == "in2":
                return proj_ready, NPROJ1 + j + 1 + l * N_IN2
            if kind == "out2":
                return out_ready, DEPTH * KC + j + 1 + l * OUTS2
            if kind in ("w1", "w3"):
                return h1_ready if kind == "w1" else h3_ready, HALF * f + j + 1 + l * FFC
            o, part = j
            if part < len(W2_CUT) - 1:
                return w2_used, KC * f + o + 1 + l * 2 * KC
            return out_ready, DEPTH * KC + KC * (f + 1) + o + 1 + l * OUTS2

        def rest_signal(n, l):
            return (first_rest, n + 1 + l * 2) if n < 2 else (rest_done, n - 1 + l * (PER2 - 2))

        def panel_size(n):
            kind, _, j = PANELS2[n]
            return P * (W2_CUT[j[1]][1] - W2_CUT[j[1]][0] if kind == "w2" else KC)

        def flat(n, k):
            return split[:, n % SPLIT, k, :, :].rearrange("p c n -> p (c n)")[:, 0:panel_size(n)]

        block = ctx.enter_context(nc.Block())

        @block.sync
        def _(sp):
            sp.dma_start(x1[:, :, 0:SEQ], dram["x"]).then_inc(x_in, 16)
            sp.dma_start(x1[:, :, SEQ:TOK], dram["ctx"]).then_inc(x_in, 16)
            sp.dma_start(prm[:, :], dram["prm"]).then_inc(vec_in, 16)
            sp.dma_start(mats[:, :, :], dram["mats"]).then_inc(mats_in, 16)
            for i, (kind, l, j) in enumerate(first_mod):
                if i >= STAGE:
                    sp.wait_ge(mod_ready, i - STAGE + 1)
                sp.dma_start(stage[:, i % STAGE, :], dram[kind][l, j]).then_inc(stage_in[i % STAGE], 16)
            for i, p in enumerate(stream):
                kind, l, j = p
                if p in main_no:
                    n = main_no[p]
                    if n >= RAW1:
                        sp.wait_ge(rest1_done, n - RAW1 + 1)
                    sp.dma_start(raw1[:, n % RAW1, 0:main_size(n)], dram[kind][l, j]).then_inc(raw1_in[n % RAW1], 16)
                else:
                    n = wide_no[p]
                    if n >= WIDE:
                        sp.wait_ge(*parts_made(ada_no[wide_seq[n - WIDE]]))
                    sp.dma_start(wide[:, n % WIDE, :], dram[kind][l, j]).then_inc(wide_in[n % WIDE], 16)
                if p == ANGLES_AT:
                    sp.wait_ge(y_done, plans[DEPTH - 1, "C"][1])
                    sp.dma_start(angle[0].bitcast(I32), dram["pos"].partition_broadcast(P)).then_inc(pos_in, 16)
                if i == 2:
                    sp.dma_start(rot_c[:, :], dram["rope"][:, 0, :]).then_inc(tables_in, 16)
                    sp.dma_start(rot_s[:, :], dram["rope"][:, 1, :]).then_inc(tables_in, 16)
                    sp.dma_start(bmask[:, :, :], dram["bmask"]).then_inc(tables_in, 16)
                    sp.dma_start(cmask[:, :], dram["cmask"]).then_inc(tables_in, 16)
                    sp.dma_start(sinks[:, :], dram["sinks"].partition_broadcast(P)).then_inc(tables_in, 16)
                    sp.dma_start(head_of[:, :, :], dram["head_of"]).then_inc(tables_in, 16)
                    sp.dma_start(of_head[:, :, :], dram["of_head"]).then_inc(tables_in, 16)
                    sp.dma_start(lyr[:, :, :], dram["lyr"]).then_inc(lyr_vec_in, 16)
            sp.wait_ge(x_ready, NX1)
            for tile, name in ((fmask, "fmask"), (decay[:, :, :], "decay"), (counts[:, :, :], "counts")):
                sp.dma_start(tile, dram[name]).then_inc(tables2_in, 16)
            with sp.Fori(0, DEPTH) as l:
                for n, (kind, f, j) in enumerate(PANELS2):
                    if n == 0:
                        sp.wait_ge(x_ready, NX1 + l * OUTS2)
                    elif n >= RAW:
                        sp.wait_ge(*rest_signal(n - RAW, l))
                    if kind == "w2":
                        a, e = W2_CUT[j[1]]
                        src = dram[kind][bass.ds(l, 1), f, j[0], :, P * a:P * e]
                    else:
                        src = dram[kind][bass.ds(l, 1), HALF * f + j, :, :]
                    sp.dma_start(raw[:, n % RAW, 0:panel_size(n)], src.rearrange("a p n -> (a p) n")).then_inc(raw_in[n % RAW], 16)
                    if n == RAW - 1:
                        sp.dma_start(poolw[:, :, :].rearrange("p c n -> p (c n)"),
                                     dram["poolw"][bass.ds(l, 1), :, :].rearrange("a p n -> (a p) n")).then_inc(lyr_in, 16)
            sp.wait_ge(result_ready, KC)
            sp.dma_start(out, xl[:, :, :]).then_inc(result_out, 16)
            sp.wait_ge(result_out, 16)

        @block.gpsimd
        def _(pool):
            s_end = {}
            for l in range(DEPTH):
                for ev in plans[l, "B"][0]:
                    if ev["kind"] == "S" and ev["unit"].get("bias_end"):
                        s_end[l * HEADS + ev["unit"]["h"]] = ev["s"] + 1

            def bias_rows(n):
                if n >= 2:
                    pool.wait_ge(s_ready, s_end[n - 2])
                for r in range(ROWS):
                    src = bass.AP(dram["rpb"].tensor, n * 15 * 64 + 64 * r, [[1, NBC], [64, ROWS], [1, 48]])
                    pool.dma_start(bias[NBC * r:NBC * r + NBC, n % 2, :, :], src).then_inc(bias_in[n % 2], 16)

            def rest1(n):
                pool.wait_ge(rounded1, n + 1)
                nc.gpsimd.tensor_tensor(flat1(n, 1), raw1[:, n % RAW1, 0:main_size(n)], flat1(n, 0).bitcast(F32),
                                        ALU.subtract).then_inc(rest1_done, 1)

            for n in range(SPLIT1):
                bias_rows(n)
                rest1(n)
            for l in range(DEPTH):
                for m in "ABC":
                    for b, _ in blocks_of(l, m):
                        rest1(main_no[IN1, l, b] + SPLIT1)
                    if m == "B":
                        for h in range(2, HEADS + (2 if l < DEPTH - 1 else 0)):
                            bias_rows(l * HEADS + h)
                pool.wait_ge(y_done, plans[l, "C"][1])
                if l == 0:
                    pool.dma_start(x1[:, :, 0:SEQ], dram["x"]).then_inc(x_back, 16)
                    pool.dma_start(x1[:, :, SEQ:TOK], dram["ctx"]).then_inc(x_back, 16)
                else:
                    pool.wait_ge(x_kept, 16 * l)
                    pool.dma_start(x1[:, :, 0:SEQ], kept).then_inc(x_back, 16)
                for p in [(IN1, l, b) for b, _ in blocks_of(l, "G")] + [(OUT1, l, i) for i in range(2 * KC)]:
                    if main_no[p] + SPLIT1 < N_MAIN:
                        rest1(main_no[p] + SPLIT1)
                if l < DEPTH - 1:
                    pool.wait_ge(x_ready, KC * (l + 1))
                    pool.dma_start(kept, x1[:, :, 0:SEQ]).then_inc(x_kept, 16)
            pool.wait_ge(x_ready, NX1)
            pool.memset(hpad[:, :, 0:CONV - 1], 0.0).then_inc(pads_done, 1)
            pool.memset(ppad[:, :, 0:POOLPAD], 0.0).then_inc(pads_done, 1)
            pool.memset(vret[:, :, :, HD:2 * HD], 0.0).then_inc(pads_done, 1)
            pool.memset(augq[:, :], 1.0).then_inc(pads_done, 1)
            pool.memset(augk[:, :], 1.0).then_inc(pads_done, 1)
            pool.wait_ge(pads_done, 5)
            pool.wait_ge(tables2_in, 48)
            with pool.Fori(0, DEPTH) as l:
                for i in range(2):
                    pool.wait_ge(rounded, i + 1 + l * PER2)
                    nc.gpsimd.tensor_tensor(flat(i, 1), raw[:, i % RAW, 0:panel_size(i)], flat(i, 0).bitcast(F32),
                                            ALU.subtract).then_inc(first_rest, 1)
                pool.wait_ge(proj_taken, NPROJ1 + 15 + l * N_IN2)
                n = POOLPAD + SEQ
                A, B = psums[:, 0, :], psums[:, 1, :]
                halves = {1: (0, 0), 2: (1, 0), 4: (0, 1), 8: (1, 1)}
                for t in range(2):
                    src = ppad[:, t, :]
                    for k, dst in ((1, A), (2, B)) if t == 0 else ((1, A), (2, B), (4, A), (8, B)):
                        lo = 2 * k - 1
                        nc.gpsimd.tensor_tensor(dst[:, lo:n], src[:, lo:n], src[:, lo - k:n - k], ALU.add)
                        pool.drain()
                        half, tile = halves[k]
                        if tile == t:
                            r = slice(HD * half, HD * half + HD)
                            nc.gpsimd.tensor_tensor(pooled[r, t, :], dst[r, POOLPAD:n], counts[r, t, :], ALU.mult)
                        src = dst
                    pool.drain()
                nc.gpsimd.tensor_tensor(pooled, pooled, ppad[:, :, POOLPAD:n], ALU.subtract).then_inc(pool_done, 1)

        @block.scalar
        def _(act):
            A_ = nc.scalar.activation

            def load_table(f):
                A_(scrap[:, :], ones[:, 0:1], f)
                act.drain()


            def take_mod(p):
                kind, l, i = p
                k = ada_no[p]
                act.wait_ge(mod_ready, k + 1)
                dst = mod1[:, l, 2 * i:2 * i + 2, :].rearrange("p a b -> p (a b)") if kind == ADA1 else mod2[:, l, 2 * i:2 * i + 2]
                n = 4 if kind == ADA1 else 2
                nc.scalar.copy(dst, bank(4, 0, n)).then_inc(mod_taken, 1)

            def square1(k, c, n):
                if k == 0:
                    act.wait_ge(x_in, 32)
                else:
                    act.wait_ge(x_ready, KC * (k - 1) + c + 1)
                if KC * k + c >= 2:
                    act.wait_ge(sq_summed, KC * k + c - 1)
                A_(squares[:, c % 2, 0:n], x1[:, c, 0:n], ACT.Square).then_inc(sq_ready, 1)

            def root1(k, parts):
                act.wait_ge(sq_summed, 8 * k + KC)
                for j, (lo, n) in enumerate(parts):
                    ins = A_(std[:, 0, lo:lo + n], bank(6 + j, 0, n), ACT.Sqrt, bias=EPS, scale=1.0 / DM)
                ins.then_inc(std_ready, 1)

            def round_panel1(n):
                act.wait_ge(raw1_in[n % RAW1], 16 * (n // RAW1 + 1))
                if n >= SPLIT1:
                    act.wait_ge(*main_used(n - SPLIT1))
                A_(flat1(n, 0), raw1[:, n % RAW1, 0:main_size(n)], ACT.Copy).then_inc(rounded1, 1)

            both = [(0, SEQ), (SEQ, CTX)]
            act.wait_ge(vec_in, 16)
            A_(silu_c[:, :, :].rearrange("p a b -> p (a b)"), vec("c", 0, 2 * KC), ACT.Silu).then_inc(silu_done, 1)
            A_(silu_c2[:, :], vec("c2", 0, KC), ACT.Silu).then_inc(silu_done, 1)
            def projected(l, m):
                for b, n in blocks_of(l, m):
                    k = NSEQ[l, b]
                    act.wait_ge(proj_ready, k + 1)
                    if m == "A" and b == 5:
                        act.wait_ge(qsum_ready, 5 * l + 5)
                        A_(rstd[0:10, 0:SEQ], bank(7)[0:10], ACT.Sqrt, bias=EPS, scale=1.0 / HD)
                        A_(rstd[0:10, SEQ:TOK], bank(5, 0, CTX)[0:10], ACT.Sqrt, bias=EPS, scale=1.0 / HD).then_inc(qstd_ready, 1)
                    if b == 0 and l > 0:
                        act.wait_ge(x_kept, 16 * l)
                    if m == "G":
                        dst, f, scale = gate_buf[:, k % 2, :], ACT.Silu, 1.0
                        g = l * MIXC + b - 24
                        if g >= 2:
                            act.wait_ge(u_ready, g - 1)
                    else:
                        dst, f = slots[:, slot_of(b), :], ACT.Copy
                        scale = -QSCALE if m in "BC" and b - {"B": 6, "C": 18}[m] < 4 else 1.0
                    if m == "A" and b < 5:
                        if 5 * l + b >= 2:
                            act.wait_ge(qsum_ready, 5 * l + b - 1)
                        ins = A_(squares[:, b % 2, 0:SEQ], bank(k % 2), ACT.Square)
                        if n == TOK:
                            ins = A_(squares[:, b % 2, SEQ:TOK], bank(2 + k % 2, 0, CTX), ACT.Square)
                        ins.then_inc(qsq_ready, 1)
                        f, scale = ACT.Identity, vec("kn", l) if b == 4 else qn8[:, l:l + 1]
                    to, src = dst[:, 0:SEQ], bank(k % 2)
                    if m == "B":
                        to, src = to.rearrange("p (c r) -> p r c", r=ROWS), src.rearrange("p (r c) -> p r c", c=GRID)
                    ins = A_(to, src, f, scale=scale)
                    if n == TOK:
                        ins = A_(dst[:, SEQ:TOK], bank(2 + k % 2, 0, CTX), f, scale=scale)
                    ins.then_inc(proj_taken, 1)
                    if (l, b - 1) in spare:
                        take_mod(spare[l, b - 1])
                    round_panel1(main_no[IN1, l, b] + SPLIT1)
                    if (IN1, l, b) == ANGLES_AT:
                        act.wait_ge(angle_done, 1)
                        A_(rot_s[:, :], angle[0], ACT.Sin).then_inc(sines_done, 1)
                        A_(rot_c[:, :], angle[0], ACT.Sin, scale=0.5).then_inc(sines_done, 1)

            def double_keys(l, m):
                if m == "A":
                    act.wait_ge(qn_done, 5 * l + 1)
                else:
                    act.wait_ge(rope_done, 10 * l + 10)
                for kv in range(2):
                    for half in range(2):
                        ins = nc.scalar.copy(slots[HD * half:HD * half + HD, 6 + kv, :], slots[HD * kv:HD * kv + HD, 4, :])
                ins.then_inc(kdup_done, 1)

            zero = Off(None)
            act.wait_ge(mats_in, 16)
            act.wait_ge(qn_scaled, 1)
            for l in range(DEPTH):
                if l == 0:
                    for c in range(KC):
                        square1(0, c, TOK)
                root1(l, both)
                if l == 0:
                    for p in first_mod:
                        take_mod(p)
                    for n in range(SPLIT1):
                        round_panel1(n)
                for c in range(KC):
                    act.wait_ge(hm_ready, KC * l + c + 1)
                    for j, (lo, n) in enumerate(both):
                        ins = A_(hs1[:, 0, c, lo:lo + n], hm1[:, c % 4, lo:lo + n], ACT.Identity, bias=mod1[:, l, c, j:j + 1])
                    ins.then_inc(hh_ready, 1)
                for m in "ABC":
                    projected(l, m)
                    load_table(ACT.Exp)
                    if m != "B":
                        double_keys(l, m)
                    attention_act(act, plans[l, m][0], zero)
                projected(l, "G")
                n = out_tokens(l)
                for c in range(MIXC):
                    act.wait_ge(u_ready, MIXC * l + c + 1)
                    A_(u_hi[:, c, 0:n], y1[:, c, 0:n], ACT.Copy).then_inc(u_rounded, 1)
                load_table(ACT.Sqrt)
                for i in range(2 * KC):
                    if main_no[OUT1, l, i] + SPLIT1 < N_MAIN:
                        round_panel1(main_no[OUT1, l, i] + SPLIT1)
                    if i % 2 == 1:
                        square1(l + 1, i // 2, n)
            root1(DEPTH, both[:1])

            def round_panel(n, l):
                act.wait_ge(raw_in[n % RAW], 16 * (n // RAW + 1) + l * (16 * PER2 // RAW))
                if n >= SPLIT:
                    act.wait_ge(*used2(n - SPLIT, l))
                A_(flat(n, 0), raw[:, n % RAW, 0:panel_size(n)], ACT.Copy).then_inc(rounded, 1)

            def square(k, c, x_count):
                act.wait_ge(x_ready, x_count + c + 1)
                act.wait_ge(sq_summed, 8 * k + c - 1)
                A_(squares[:, c % 2, 0:SEQ], xl[:, c, :], ACT.Square).then_inc(sq_ready, 1)

            def root(k):
                act.wait_ge(sq_summed, 8 * k + KC)
                A_(std[:, 0, 0:SEQ], bank(6), ACT.Sqrt, bias=EPS, scale=1.0 / DM).then_inc(std_ready, 1)

            def shifted(k, shift):
                for c in range(KC):
                    act.wait_ge(hm_ready, KC * (k - 1) + c + 1)
                    A_(hs[:, 0, c, :], hm2[:, c % 4, :], ACT.Identity, bias=shift(c)).then_inc(hh_ready, 1)

            for c in range(KC):
                square(3, c, NX1 - KC)
            act.wait_ge(pads_done, 5)
            with act.Fori(0, DEPTH) as l:
                o = Off(l)
                root(3 + l * 2)
                for n in range(SPLIT):
                    round_panel(n, l)
                shifted(3 + l * 2, lambda c: mod[:, c:c + 1])
                for m in range(N_IN2):
                    act.wait_ge(proj_ready, NPROJ1 + m + 1 + l * N_IN2)
                    b = m - 1
                    if m == 0:
                        A_(fz, bank(0)[0:4], ACT.Identity, bias=lvec("fox_b")[0:4]).then_inc(proj_taken, 1)
                    else:
                        src, dst, f, scale = bank(m % 2), u2[:, b, :], ACT.Copy, 1.0
                        if b in (2, 3):
                            f = ACT.Sigmoid
                        elif b in (6, 7):
                            scale = QSCALE
                        elif b in (14, 15):
                            scale = -QSCALE
                        elif b in (10, 11):
                            f = ACT.Silu
                        elif b in (12, 13):
                            dst = ppad[:, b - 12, POOLPAD:]
                        A_(dst, src, f, scale=scale).then_inc(proj_taken, 1)
                    round_panel(m + SPLIT, l)
                    if m == 0:
                        act.drain()
                        A_(ft, fz, ACT.Abs)
                        act.drain()
                        A_(ft, ft, ACT.Exp, scale=-1.0)
                        act.drain()
                        A_(ft, ft, ACT.Ln, bias=1.0).then_inc(ff_log, 1)
                for t in range(2):
                    act.wait_ge(pool_proj, t + 1 + l * 2)
                    A_(hs[:, 0, 2 + t, :], bank(4 + t), ACT.Identity, scale=lvec("pool_scale", t)).then_inc(pool_hi, 1)
                act.wait_ge(ff_cum, 1 + l)
                for h in range(4):
                    act.dma_start(augq[32 * h:32 * h + 1, :], ft[h:h + 1, :]).then_inc(aug_in, 16)
                    act.dma_start(augk[32 * h + 1:32 * h + 2, :], fz[h:h + 1, :]).then_inc(aug_in, 16)
                for g in range(2):
                    act.wait_ge(rv_ready, g + 1 + l * 2)
                    for h in range(2):
                        ins = nc.scalar.copy(vret[:, g, :, P * h:P * h + HD],
                                             bank(2 + g).rearrange("p (t c) -> p t c", c=P)[:, :, HD * h:HD * h + HD])
                    ins.then_inc(rv_taken, 1)
                for g in range(2):
                    act.wait_ge(ro_steps, 8 * (g + 1) + l * 16)
                    nc.scalar.copy(ret_o[:, g, :], bank(g)).then_inc(ro_taken, 1)
                act.wait_ge(ln_dev, 2 + l * 2)
                for t in range(2):
                    A_(squares[:, t, 0:SEQ], conv[:, t, :], ACT.Square).then_inc(ln_sq, 1)
                act.wait_ge(ln_var, 1 + l)
                A_(ln_root, bank(7), ACT.Sqrt, bias=EPS, scale=1.0 / 256).then_inc(ln_std, 1)
                for g in range(2):
                    act.wait_ge(gn_dev, g + 1 + l * 2)
                    A_(squares[:, g, 0:SEQ], ret_o[:, g, :], ACT.Square).then_inc(gn_sq, 1)
                for g in range(2):
                    act.wait_ge(gn_var, g + 1 + l * 2)
                    A_(gn_root[:, g, :], bank(2 + g), ACT.Sqrt, bias=EPS, scale=1.0 / HD).then_inc(gn_std, 1)

                def conv_out(t):
                    act.wait_ge(ln_norm, t + 1 + l * 2)
                    A_(conv[:, t, :], conv[:, t, :], ACT.Silu, bias=lvec("ln_b", t), scale=lvec("ln_g", t))
                    act.drain()
                    A_(hs[:, 0, 6 + t, :], conv[:, t, :], ACT.Copy).then_inc(conv_hi, 1)

                nothing = lambda: None
                attention_act(act, fox_plan, o, [nothing] * 4 + [lambda: conv_out(0), nothing, lambda: conv_out(1)])
                load_table(ACT.Sqrt)
                for c in range(KC):
                    square(4 + l * 2, c, NX1 + l * OUTS2)
                    round_panel(N_IN2 + c + SPLIT, l)
                root(4 + l * 2)
                load_table(ACT.Silu)
                shifted(4 + l * 2, lambda c: mod[:, 24 + c:25 + c])
                for f in range(2):
                    n = FFN_AT + f * FFN_PER
                    for b in range(HALF):
                        k = HALF * f + b
                        act.wait_ge(h1_ready, k + 1 + l * FFC)
                        if k >= 2:
                            act.wait_ge(f_ready, k - 1 + l * FFC)
                        A_(squares[:, k % 2, 0:SEQ], bank(4 + k % 2), ACT.Silu).then_inc(silu_ready, 1)
                        round_panel(n + 2 * b + SPLIT, l)
                        round_panel(n + 2 * b + 1 + SPLIT, l)
                    if f == 1:
                        load_table(ACT.Sqrt)
                    for c in range(KC):
                        for j in range(len(W2_CUT)):
                            i = n + 2 * HALF + len(W2_CUT) * c + j + SPLIT
                            if i < PER2:
                                round_panel(i, l)
                        if f == 1:
                            square(5 + l * 2, c, NX1 + 2 * KC + l * OUTS2)
            root(3 + 2 * DEPTH)

        @block.vector
        def _(dve):
            V = nc.vector

            def norm(k, src, gain, place, signal):
                dve.drain()
                dve.wait_ge(std_ready, k + 1)
                V.reciprocal(rstd[:, 0:SEQ], std[:, 0, 0:SEQ])
                dve.drain()
                for c in range(KC):
                    V.scalar_tensor_tensor(out=place[:, c, :], in0=src[:, c, 0:SEQ], scalar=gain(c),
                                           in1=rstd[:, 0:SEQ], op0=ALU.mult, op1=ALU.mult).then_inc(signal, 1)

            both = [(0, SEQ), (SEQ, CTX)]
            dve.wait_ge(vec_in, 16)
            V.tensor_scalar(qn8[:, :], vec("qn", 0, DEPTH), -QSCALE, None, ALU.mult).then_inc(qn_scaled, 1)
            def rope(slot_ap, r, cos, sin, at0):
                tmp = probs_t[:, 0, :]
                dve.drain()
                dve.wait_ge(sw_ready, r + 1)
                V.tensor_tensor(tmp, bank(at0), sin, ALU.mult)
                V.tensor_tensor(slot_ap, slot_ap, cos, ALU.mult)
                dve.drain()
                V.tensor_tensor(slot_ap, slot_ap, tmp, ALU.add).then_inc(rope_done, 1)

            def qk_norm(l, i, j):
                dve.wait_ge(qn_sums, 5 * l + i + 1)
                b = 4 + 2 * (i % 2)
                ins = V.tensor_tensor(slots[:, j, 0:SEQ], slots[:, j, 0:SEQ], bank(b), ALU.mult)
                if l < DEPTH - 1 or j == 4:
                    ins = V.tensor_tensor(slots[:, j, SEQ:TOK], slots[:, j, SEQ:TOK], bank(b + 1, 0, CTX), ALU.mult)
                ins.then_inc(qn_done, 1)

            def angles():
                dve.wait_ge(pos_in, 16)
                V.tensor_copy(angle[1], angle[0].bitcast(I32))
                dve.drain()
                V.tensor_scalar(angle[1], angle[1], vec("inv"), None, ALU.mult)
                dve.drain()
                V.tensor_scalar(angle[2], angle[1], 1.0 / (2 * np.pi), MAGIC, ALU.mult, ALU.add)
                dve.drain()
                V.tensor_scalar(angle[2], angle[2], MAGIC, None, ALU.subtract)
                dve.drain()
                for part in TWO_PI:
                    V.scalar_tensor_tensor(out=angle[1], in0=angle[2], scalar=-part, in1=angle[1], op0=ALU.mult, op1=ALU.add)
                    dve.drain()
                V.tensor_scalar(angle[0], angle[1], 3.1415925, -3.1415925, ALU.min, ALU.max).then_inc(angle_done, 1)

            def rotary_tables():
                dve.wait_ge(sines_done, 2)
                V.tensor_scalar(rot_s[:, :], rot_s[:, :], vec("sign"), None, ALU.mult)
                V.tensor_tensor(rot_c[:, :], rot_c[:, :], rot_c[:, :], ALU.mult)
                dve.drain()
                V.tensor_scalar(rot_c[:, :], rot_c[:, :], -2.0, 1.0, ALU.mult, ALU.add)

            def mod_parts(p):
                k = ada_no[p]
                if k < N_SS1:
                    stage_wait(dve, k)
                    w = stage[:, k % STAGE, :].rearrange("p (c n) -> p c n", c=KC)
                else:
                    wide_wait(dve, p)
                    w = wide_slot(p)
                if k >= N_SS1 + 2:
                    dve.wait_ge(mod_ready, k - 1)
                to = products(k)
                for c in range(KC):
                    for i in range(2 if p[0] == ADA1 else 1):
                        v = silu_c[:, c, i:i + 1] if p[0] == ADA1 else silu_c2[:, c:c + 1]
                        if c == 0:
                            ins = V.tensor_scalar(to[:, i, :], w[:, c, :], v, None, ALU.mult)
                        else:
                            ins = V.scalar_tensor_tensor(out=to[:, i, :], in0=w[:, c, :], scalar=v,
                                                         in1=to[:, i, :], op0=ALU.mult, op1=ALU.add)
                    if c < KC - 1:
                        dve.drain()
                ins.then_inc(part_ready, 1)

            def over_roots(l):
                dve.wait_ge(std_ready, l + 1)
                V.reciprocal(rstd[:, :], std[:, 0, :])

            dve.wait_ge(silu_done, 2)
            for i, p in enumerate(first_mod[1::2]):
                if i == 2:
                    over_roots(0)
                mod_parts(p)
            zero = Off(None)
            for l in range(DEPTH):
                dve.wait_ge(mod_taken, n_mod1[l])
                for i in range(2):
                    V.tensor_tensor(mod1[:, l, 0:2 * KC, i], mod1[:, l, 0:2 * KC, i], vec("ada_b", 24 * l, 2 * KC), ALU.add)
                dve.drain()
                for i in range(2):
                    V.scalar_tensor_tensor(out=gain1[:, i, :], in0=mod1[:, l, KC:2 * KC, i], scalar=1.0,
                                           in1=vec("norm_w", KC * l, KC), op0=ALU.add, op1=ALU.mult)
                dve.drain()
                if l > 0:
                    over_roots(l)
                dve.drain()
                for c in range(KC + 1):
                    if c < KC:
                        for j, (lo, n) in enumerate(both):
                            ins = V.scalar_tensor_tensor(out=hm1[:, c % 4, lo:lo + n], in0=x1[:, c, lo:lo + n], scalar=gain1[:, j, c:c + 1],
                                                         in1=rstd[:, lo:lo + n], op0=ALU.mult, op1=ALU.mult)
                        ins.then_inc(hm_ready, 1)
                    if c > 0:
                        dve.wait_ge(hh_ready, KC * l + c)
                        for j, (lo, n) in enumerate(both):
                            ins = V.scalar_tensor_tensor(out=hs1[:, 1, c - 1, lo:lo + n], in0=hm1[:, (c - 1) % 4, lo:lo + n],
                                                         scalar=mod1[:, l, c - 1, j:j + 1],
                                                         in1=hs1[:, 0, c - 1, lo:lo + n].bitcast(F32), op0=ALU.add, op1=ALU.subtract)
                        ins.then_inc(h_ready, 1)
                dve.drain()
                for m in "ABC":
                    if l == 0 and m == "A":
                        dve.wait_ge(tables_in, 112)
                        V.tensor_scalar(sinks[:, :], sinks[:, :], -1.0, None, ALU.mult)
                    first = PHASES[m][0]
                    for b, _ in blocks_of(l, m):
                        if (l, b) in spare:
                            mod_parts(spare[l, b])
                        if m != "B" and b > first:
                            rope(slots[:, b - first - 1, 0:SEQ], 10 * l + (0 if m == "A" else 5) + b - first - 1, rot_c[:, :], rot_s[:, :], 6)
                    if m == "A":
                        dve.wait_ge(qstd_ready, l + 1)
                        V.reciprocal(rstd[0:10, :], rstd[0:10, :]).then_inc(qrec_ready, 1)
                        for i, j in enumerate(KEYS_FIRST):
                            qk_norm(l, i, j)
                    attention_dve(dve, plans[l, m][0], zero)
                for b, n in blocks_of(l, "G"):
                    k = NSEQ[l, b]
                    if (IN1, l, b) == ANGLES_AT:
                        angles()
                    if (l, b) in spare:
                        mod_parts(spare[l, b])
                    dve.wait_ge(proj_taken, k + 1)
                    V.tensor_tensor(y1[:, b - 24, 0:n], y1[:, b - 24, 0:n], gate_buf[:, k % 2, 0:n], ALU.mult).then_inc(u_ready, 1)
                if l == DEPTH - 1:
                    rotary_tables()
                dve.wait_ge(mod_taken, n_gate1[l])
                for i in range(2):
                    V.tensor_tensor(mod1[:, l, 2 * KC:, i], mod1[:, l, 2 * KC:, i], vec("ada_b", 24 * l + 2 * KC, KC), ALU.add)
                dve.drain()
                n = out_tokens(l)
                for c in range(MIXC):
                    dve.wait_ge(u_rounded, MIXC * l + c + 1)
                    V.tensor_tensor(u_lo[:, c, 0:n], y1[:, c, 0:n], u_hi[:, c, 0:n].bitcast(F32), ALU.subtract).then_inc(u_split, 1)
                dve.wait_ge(x_back, 32 + 16 * l)
                for o in range(KC):
                    dve.wait_ge(out_ready, KC * l + o + 1)
                    for j, (lo, n) in enumerate(both if l < DEPTH - 1 else both[:1]):
                        ins = V.scalar_tensor_tensor(out=x1[:, o, lo:lo + n], in0=bank(4 - 2 * j + o % 2, 0, n),
                                                     scalar=mod1[:, l, 2 * KC + o, j:j + 1], in1=x1[:, o, lo:lo + n],
                                                     op0=ALU.mult, op1=ALU.add)
                    ins.then_inc(x_ready, 1)
            dve.drain()
            norm(DEPTH, x1, lambda c: vec("final_w", c), xl, x_ready)

            dve.wait_ge(lyr_vec_in, 16)
            dve.wait_ge(pads_done, 5)
            dve.wait_ge(tables2_in, 48)
            dve.wait_ge(mod_taken, len(ada_seq))
            def rest(n, l):
                dve.wait_ge(rounded, n + 1 + l * PER2)
                V.tensor_tensor(flat(n, 1), raw[:, n % RAW, 0:panel_size(n)], flat(n, 0).bitcast(F32), ALU.subtract).then_inc(rest_done, 1)

            def norm_split(k, gain, shift, panels):
                dve.drain()
                dve.wait_ge(std_ready, k + 1)
                V.reciprocal(rstd[:, 0:SEQ], std[:, 0, 0:SEQ])
                dve.drain()
                for c in range(KC + 1):
                    if c < KC:
                        V.scalar_tensor_tensor(out=hm2[:, c % 4, :], in0=xl[:, c, :], scalar=gain(c), in1=rstd[:, 0:SEQ],
                                               op0=ALU.mult, op1=ALU.mult).then_inc(hm_ready, 1)
                    if c > 0:
                        dve.wait_ge(hh_ready, KC * (k - 1) + c)
                        V.scalar_tensor_tensor(out=hs[:, 1, c - 1, :], in0=hm2[:, (c - 1) % 4, :], scalar=shift(c - 1),
                                               in1=hs[:, 0, c - 1, :].bitcast(F32), op0=ALU.add, op1=ALU.subtract).then_inc(h_ready, 1)
                for p in panels:
                    rest(*p)

            with dve.Fori(0, DEPTH) as l:
                o = Off(l)
                dve.drain()
                V.tensor_copy(cur[:, :], lyr[:, bass.ds(l, 1), :].rearrange("p a b -> p (a b)"))
                dve.drain()
                V.tensor_tensor(mod[:, :], mod2[:, bass.ds(l, 1), :].rearrange("p a b -> p (a b)"), lvec("ada_b", 0, 48), ALU.add)
                dve.drain()
                for i, name in enumerate(("nmix", "nffn")):
                    V.scalar_tensor_tensor(out=gain2[:, i, :], in0=mod[:, 24 * i + KC:24 * i + 2 * KC], scalar=1.0,
                                           in1=lvec(name, 0, KC), op0=ALU.add, op1=ALU.mult)
                dve.drain()
                norm_split(3 + l * 2, lambda c: gain2[:, 0, c:c + 1], lambda c: mod[:, c:c + 1], [(n, l) for n in range(2, SPLIT)])

                def tap(j):
                    for t in range(2):
                        w, src = lvec("conv_w", CONV * t + j), hpad[:, t, j:j + SEQ]
                        if j == 0:
                            ins = V.tensor_scalar(conv[:, t, :], src, w, lvec("conv_b", t), ALU.mult, ALU.add)
                        else:
                            ins = V.scalar_tensor_tensor(out=conv[:, t, :], in0=src, scalar=w, in1=conv[:, t, :],
                                                         op0=ALU.mult, op1=ALU.add)
                    if j < CONV - 1:
                        dve.drain()
                    else:
                        ins.then_inc(conv_done, 1)

                taps = 0
                for m in range(N_IN2):
                    rest(m + SPLIT, l)
                    if m == 1:
                        dve.wait_ge(ff_log, 1 + l)
                        V.scalar_tensor_tensor(out=ft, in0=fz, scalar=0.0, in1=ft, op0=ALU.min, op1=ALU.subtract)
                        dve.drain()
                        V.tensor_tensor_scan(fz, ft, ft, 0.0, ALU.add, ALU.bypass)
                        dve.drain()
                        V.tensor_scalar(ft, fz, -1.0, None, ALU.mult).then_inc(ff_cum, 1)
                    if m == 4:
                        dve.wait_ge(proj_taken, NPROJ1 + 5 + l * N_IN2)
                        for t in range(2):
                            V.tensor_tensor(hpad[:, t, CONV - 1:], u2[:, t, :], u2[:, 2 + t, :], ALU.mult)
                        dve.drain()
                    if m > 4:
                        to = CONV * (m - 4) // (N_IN2 - 5)
                        for j in range(taps, to):
                            tap(j)
                        taps = to
                for t in range(2):
                    dve.wait_ge(pool_hi, t + 1 + l * 2)
                    V.scalar_tensor_tensor(out=hs[:, 1, 2 + t, :], in0=bank(4 + t), scalar=lvec("pool_scale", t),
                                           in1=hs[:, 0, 2 + t, :].bitcast(F32), op0=ALU.mult, op1=ALU.subtract).then_inc(pool_mix, 1)
                for j in range(4):
                    rope(u2[:, 4 + j, :], 10 * DEPTH + j + l * 4, rot_c[:, :], rot_s[:, :], j % 2)
                for i in range(16):
                    n = SEQ - P * (i % 4)
                    dve.wait_ge(rs_ready, i + 1 + l * 16)
                    if i >= 4:
                        dve.wait_ge(ro_steps, i - 3 + l * 16)
                    V.tensor_tensor(ret_s[:, i % 4, 0:n], bank(4 + i % 4, 0, n), decay[:, i // 4, 0:n], ALU.mult).then_inc(rs_done, 1)
                dve.wait_ge(ln_sum, 1 + l)
                for t in range(2):
                    V.scalar_tensor_tensor(out=conv[:, t, :], in0=bank(6), scalar=-1.0 / 256, in1=conv[:, t, :],
                                           op0=ALU.mult, op1=ALU.add).then_inc(ln_dev, 1)
                for g in range(2):
                    dve.wait_ge(gn_sum, g + 1 + l * 2)
                    V.scalar_tensor_tensor(out=ret_o[:, g, :], in0=bank(2 + g), scalar=-1.0 / HD, in1=ret_o[:, g, :],
                                           op0=ALU.mult, op1=ALU.add).then_inc(gn_dev, 1)
                def over(ready, count, root, half):
                    dve.wait_ge(ready, count)
                    n = SEQ // 2
                    V.reciprocal(root[:, n * half:n * half + n], root[:, n * half:n * half + n])

                def ln_scale():
                    for t in range(2):
                        V.tensor_tensor(conv[:, t, :], conv[:, t, :], ln_root, ALU.mult).then_inc(ln_norm, 1)

                def gn_scale(g):
                    V.scalar_tensor_tensor(out=ret_o[:, g, :], in0=ret_o[:, g, :], scalar=lvec("gn", g), in1=gn_root[:, g, :],
                                           op0=ALU.mult, op1=ALU.mult)

                def gn_gate(g):
                    V.tensor_tensor(ret_o[:, g, :], ret_o[:, g, :], u2[:, 10 + g, :], ALU.mult)

                def gn_round(g):
                    V.tensor_copy(hs[:, 0, 4 + g, :], ret_o[:, g, :])

                def gn_rest(g):
                    V.tensor_tensor(hs[:, 1, 4 + g, :], ret_o[:, g, :], hs[:, 0, 4 + g, :].bitcast(F32), ALU.subtract).then_inc(ret_mix, 1)

                def conv_rest(t):
                    dve.wait_ge(conv_hi, t + 1 + l * 2)
                    V.tensor_tensor(hs[:, 1, 6 + t, :], conv[:, t, :], hs[:, 0, 6 + t, :].bitcast(F32), ALU.subtract).then_inc(conv_mix, 1)

                steps = [lambda: over(ln_std, 1 + l, ln_root, 0), lambda: over(ln_std, 1 + l, ln_root, 1), ln_scale]
                for g in range(2):
                    steps += [lambda g=g: over(gn_std, g + 1 + l * 2, gn_root[:, g, :], 0),
                              lambda g=g: over(gn_std, g + 1 + l * 2, gn_root[:, g, :], 1)]
                steps += [lambda: (gn_scale(0), gn_scale(1)), lambda: (gn_gate(0), gn_gate(1)),
                          lambda: (gn_round(0), gn_round(1)), lambda: (gn_rest(0), gn_rest(1)),
                          lambda: conv_rest(0), lambda: conv_rest(1)]
                attention_dve(dve, fox_plan, o, steps)

                def update(k, i, at0, gate):
                    dve.wait_ge(out_ready, DEPTH * KC + k * KC + i + 1 + l * OUTS2)
                    V.scalar_tensor_tensor(out=xl[:, i, :], in0=bank(at0), scalar=mod[:, gate + i:gate + i + 1], in1=xl[:, i, :],
                                           op0=ALU.mult, op1=ALU.add).then_inc(x_ready, 1)

                for i in range(KC):
                    update(0, i, i % 2, 16)
                    rest(N_IN2 + i + SPLIT, l)
                norm_split(4 + l * 2, lambda c: gain2[:, 1, c:c + 1], lambda c: mod[:, 24 + c:25 + c], [])
                for f in range(2):
                    n = FFN_AT + f * FFN_PER
                    for b in range(HALF):
                        k = HALF * f + b
                        rest(n + 2 * b + SPLIT, l)
                        dve.wait_ge(silu_ready, k + 1 + l * FFC)
                        dve.wait_ge(h3_ready, k + 1 + l * FFC)
                        t = squares[:, k % 2, 0:SEQ]
                        V.tensor_tensor(t, t, bank(6 + k % 2), ALU.mult)
                        dve.drain()
                        V.tensor_copy(acts[:, 0, b, :], t)
                        dve.drain()
                        V.tensor_tensor(acts[:, 1, b, :], t, acts[:, 0, b, :].bitcast(F32), ALU.subtract).then_inc(f_ready, 1)
                        rest(n + 2 * b + 1 + SPLIT, l)
                    for c in range(KC):
                        for j in range(len(W2_CUT)):
                            i = n + 2 * HALF + len(W2_CUT) * c + j + SPLIT
                            if j == len(W2_CUT) - 1:
                                if f == 1 and c == 0:
                                    dve.drain()
                                update(1 + f, c, c % 4, 40)
                            if i < PER2:
                                rest(i, l)
            dve.drain()
            norm(3 + 2 * DEPTH, xl, lambda c: vec("final_g", c), xl, result_ready)

        @block.tensor
        def _(pe):
            mm = nc.tensor.matmul

            def make_mod(p):
                k = ada_no[p]
                stage_wait(pe, k)
                w = stage[:, k % STAGE, :].rearrange("p (c n) -> p c n", c=KC)
                if k >= 1:
                    pe.wait_ge(mod_taken, k)
                for b in range(2):
                    for c in range(KC):
                        ins = mm(bank(4, 2 * b, 2 * b + 2), w[:, c, P * b:P * b + P], silu_c[:, c, :], start=c == 0, stop=c == KC - 1)
                ins.then_inc(mod_ready, 1)

            def sum_squares1(k, c, parts):
                pe.wait_ge(sq_ready, 8 * k + c + 1)
                for j, (lo, n) in enumerate(parts):
                    ins = mm(bank(6 + j, 0, n), ones, squares[:, c % 2, lo:lo + n], start=c == 0, stop=c == KC - 1)
                ins.then_inc(sq_summed, 1)

            def sum_mod(p):
                k = ada_no[p]
                pe.wait_ge(*parts_made(k))
                pe.wait_ge(mod_taken, k)
                nv = 2 if p[0] == ADA1 else 1
                for b in range(2):
                    for i in range(nv):
                        ins = mm(bank(4, nv * b + i, nv * b + i + 1), products(k)[:, i, P * b:P * b + P], ones[:, 0:1],
                                 start=True, stop=True)
                ins.then_inc(mod_ready, 1)

            both = [(0, SEQ), (SEQ, CTX)]
            pe.wait_ge(mats_in, 16)
            for c in range(KC):
                sum_squares1(0, c, both)
            pe.wait_ge(silu_done, 2)
            for i, p in enumerate(first_mod):
                (sum_mod if i % 2 else make_mod)(p)

            def block_chunk(l, b, n, c):
                k, s = NSEQ[l, b], main_no[IN1, l, b] % SPLIT1
                for i, (w, h) in enumerate(((0, 0), (0, 1), (1, 0))):
                    for at0, lo, e in ((bank(k % 2), 0, SEQ), (bank(2 + k % 2, 0, CTX), SEQ, TOK)):
                        if lo < n:
                            ins = mm(at0, split1[:, s, w, c, :], hs1[:, h, c, lo:e], start=c == 0 and i == 0, stop=c == KC - 1 and i == 2)
                if c == KC - 1:
                    ins.then_inc(proj_ready, 1)

            def project(l, m):
                for b, n in blocks_of(l, m):
                    k = NSEQ[l, b]
                    pe.wait_ge(rest1_done, main_no[IN1, l, b] + 1)
                    if k >= 2:
                        pe.wait_ge(proj_taken, k - 1)
                    if b == 0:
                        pe.wait_ge(rest1_done, main_no[IN1, l, 1] + 1)
                        if k >= 1:
                            pe.wait_ge(proj_taken, k)
                        for c in range(KC):
                            pe.wait_ge(h_ready, KC * l + c + 1)
                            block_chunk(l, 0, n, c)
                            block_chunk(l, 1, n, c)
                        sum_mod(spare[l, 0])
                        continue
                    j = b - PHASES[m][0] - 1
                    if b == 1:
                        rotate_before(l, m, 0, k)
                        continue
                    for c in range(KC):
                        if c == KC // 2 and m in "AC" and 0 <= j < 5:
                            rotate_before(l, m, j, k)
                        block_chunk(l, b, n, c)
                    if (l, b - 1) in spare:
                        sum_mod(spare[l, b - 1])
                pe.wait_ge(proj_taken, k + 1)
                pe.wait_ge(mod_taken, ada_no[spare[l, b - 1]] + 1)

            def rotate_before(l, m, j, k):
                pe.wait_ge(proj_taken, k)
                swap_halves(slots[:, j, 0:SEQ], 10 * l + (0 if m == "A" else 5) + j, 6)
                if m == "A":
                    if l == 0 and j == 0:
                        pe.wait_ge(tables_in, 112)
                    head_sums(l, j)

            def head_sums(l, j):
                pe.wait_ge(qsq_ready, 5 * l + j + 1)
                ins = mm(bank(7)[0:10], head_of[:, j, :], squares[:, j % 2, 0:SEQ], start=j == 0, stop=j == 4)
                full = l < DEPTH - 1
                if full or j == 4:
                    ins = mm(bank(5, 0, CTX)[0:10], head_of[:, j, :], squares[:, j % 2, SEQ:TOK], start=not full or j == 0, stop=j == 4)
                ins.then_inc(qsum_ready, 1)

            def spread(l, i, j):
                b = 4 + 2 * (i % 2)
                if i >= 2:
                    pe.wait_ge(qn_done, 5 * l + i - 1)
                ins = mm(bank(b), of_head[:, j, :], rstd[0:10, 0:SEQ], start=True, stop=True)
                if l < DEPTH - 1 or j == 4:
                    ins = mm(bank(b + 1, 0, CTX), of_head[:, j, :], rstd[0:10, SEQ:TOK], start=True, stop=True)
                ins.then_inc(qn_sums, 1)

            def swap_halves(src, r, at0):
                if not isinstance(r, int):
                    pe.wait_ge(rope_done, r - 1)
                elif r >= 1:
                    pe.wait_ge(rope_done, r)
                mm(bank(at0), swap, src, start=True, stop=True).then_inc(sw_ready, 1)

            zero = Off(None)
            for l in range(DEPTH):
                for m in "ABC":
                    project(l, m)
                    if m == "A":
                        pe.wait_ge(rope_done, 10 * l + 5)
                        pe.wait_ge(qrec_ready, l + 1)
                        for i, j in enumerate(KEYS_FIRST):
                            spread(l, i, j)
                        pe.wait_ge(qn_done, 5 * l + 5)
                    if m != "B":
                        pe.wait_ge(rope_done, 10 * l + (5 if m == "A" else 10))
                        pe.wait_ge(kdup_done, 2 * l + (1 if m == "A" else 2))
                    attention_pe(pe, plans[l, m][0], zero)
                    pe.wait_ge(y_done, plans[l, m][1])
                project(l, "G")
                for o in range(KC):
                    k = KC * l + o
                    parts = both if l < DEPTH - 1 else both[:1]
                    if o >= 2:
                        pe.wait_ge(x_ready, k - 1)
                    for part in range(2):
                        n = main_no[OUT1, l, 2 * o + part]
                        pe.wait_ge(rest1_done, n + 1)
                        for c in range(MIXC // 2):
                            uc = MIXC // 2 * part + c
                            if o == 0:
                                pe.wait_ge(u_split, MIXC * l + uc + 1)
                            for i, (w, u) in enumerate(((0, u_hi), (0, u_lo), (1, u_hi))):
                                for j, (lo, e) in enumerate(parts):
                                    ins = mm(bank(4 - 2 * j + o % 2, 0, e), split1[:, n % SPLIT1, w, c, :], u[:, uc, lo:lo + e],
                                             start=uc == 0 and i == 0, stop=uc == MIXC - 1 and i == 2)
                        if part == 0:
                            ins.then_inc(out_half, 1)
                    ins.then_inc(out_ready, 1)
                    if o >= 2:
                        sum_squares1(l + 1, o - 2, parts)
                for c in (KC - 2, KC - 1):
                    sum_squares1(l + 1, c, parts)

            def product(out, n, moving, chunks, first, last):
                base = chunks[0] if PANELS2[n][0] == "w2" else 0
                for i, c in enumerate(chunks):
                    for j, (a, b) in enumerate(((0, 0), (0, 1), (1, 0))):
                        ins = mm(out, split[:, n % SPLIT, a, c - base, :], moving[:, b, c, :], start=first and i == 0 and j == 0,
                                 stop=last and i == len(chunks) - 1 and j == 2)
                return ins

            def split_wait(n, l):
                pe.wait_ge(*rest_signal(n, l))

            def first_products(banks, panels, h_count, signals, l):
                for n in panels:
                    split_wait(n, l)
                for c in range(KC):
                    pe.wait_ge(h_ready, h_count + c + 1)
                    for at0, n, signal in zip(banks, panels, signals):
                        ins = product(at0, n, hs, [c], c == 0, c == KC - 1)
                        if c == KC - 1:
                            ins.then_inc(signal, 1)

            def sum_squares(k, c):
                pe.wait_ge(sq_ready, 8 * k + c + 1)
                mm(bank(6), ones, squares[:, c % 2, 0:SEQ], start=c == 0, stop=c == KC - 1).then_inc(sq_summed, 1)

            for c in range(KC):
                sum_squares(3, c)
            pe.wait_ge(tables2_in, 48)
            pe.wait_ge(pads_done, 5)
            with pe.Fori(0, DEPTH) as l:
                o = Off(l)
                hbase = DEPTH * KC + l * 2 * KC
                pe.wait_ge(proj_taken, NPROJ1 + l * N_IN2)
                first_products((bank(0), bank(1)), (0, 1), hbase, (proj_ready, proj_ready), l)
                for m in range(2, N_IN2):
                    split_wait(m, l)
                    pe.wait_ge(proj_taken, NPROJ1 + m - 1 + l * N_IN2)
                    product(bank(m % 2), m, hs, range(KC), True, True).then_inc(proj_ready, 1)
                pe.wait_ge(proj_taken, NPROJ1 + N_IN2 + l * N_IN2)
                pe.wait_ge(pool_done, 1 + l)
                pe.wait_ge(lyr_in, 16 + l * 16)
                for t in range(2):
                    mm(bank(4 + t), poolw[:, t, :], pooled[:, t, :], start=True, stop=True).then_inc(pool_proj, 1)
                for j in range(4):
                    swap_halves(u2[:, 4 + j, :], 10 * DEPTH + j + l * 4, j % 2)
                for g in range(2):
                    for t in range(4):
                        ins = nc.tensor.transpose(bank(2 + g, P * t, P * t + P), u2[:, 8 + g, P * t:P * t + P], ident)
                    ins.then_inc(rv_ready, 1)
                pe.wait_ge(rope_done, 10 * DEPTH + 4 + l * 4)
                pe.wait_ge(rv_taken, 2 + l * 2)
                pe.wait_ge(pool_mix, 2 + l * 2)

                def decayed(i):
                    g, h, t = i // 8, i // 4, i % 4
                    n = SEQ - P * t
                    pe.wait_ge(rs_done, i + 1 + l * 16)
                    mm(bank(g, P * t, 512), pv_pair(vret[:, g, t, :], h), ret_s[:, i % 4, 0:n], start=i % 8 == 0, stop=i % 8 == 7,
                       skip_group_check=True).then_inc(ro_steps, 1)

                for i in range(16):
                    g, h, t = i // 8, i // 4, i % 4
                    r, n = rows_of(h), SEQ - P * t
                    if i >= 4:
                        pe.wait_ge(rs_done, i - 3 + l * 16)
                    mm(bank(4 + i % 4, 0, n), u2[r, 6 + g, P * t:P * t + P], u2[r, 4 + g, P * t:SEQ], start=True, stop=True).then_inc(rs_ready, 1)
                    if i >= 2:
                        decayed(i - 2)
                decayed(14)
                decayed(15)
                pe.wait_ge(conv_done, 1 + l)
                for t in range(2):
                    ins = mm(bank(6), ones, conv[:, t, :], start=t == 0, stop=t == 1)
                ins.then_inc(ln_sum, 1)
                for g in range(2):
                    pe.wait_ge(ro_taken, g + 1 + l * 2)
                    mm(bank(2 + g), pairs, ret_o[:, g, :], start=True, stop=True).then_inc(gn_sum, 1)
                for t in range(2):
                    pe.wait_ge(ln_sq, t + 1 + l * 2)
                    ins = mm(bank(7), ones, squares[:, t, 0:SEQ], start=t == 0, stop=t == 1)
                ins.then_inc(ln_var, 1)
                for g in range(2):
                    pe.wait_ge(gn_sq, g + 1 + l * 2)
                    mm(bank(2 + g), pairs, squares[:, g, 0:SEQ], start=True, stop=True).then_inc(gn_var, 1)
                pe.wait_ge(ln_std, 1 + l)
                pe.wait_ge(gn_std, 2 + l * 2)
                pe.wait_ge(aug_in, 128 + l * 128)
                attention_pe(pe, fox_plan, o)
                pe.wait_ge(y_done, at["u"] + o.u)
                pe.wait_ge(ret_mix, 2 + l * 2)
                pe.wait_ge(conv_mix, 2 + l * 2)
                for i in range(KC):
                    split_wait(N_IN2 + i, l)
                    if i >= 2:
                        pe.wait_ge(x_ready, NX1 + i - 1 + l * OUTS2)
                    product(bank(i % 2), N_IN2 + i, hs, range(KC), True, True).then_inc(out_ready, 1)
                    if i >= 2:
                        sum_squares(4 + l * 2, i - 2)
                sum_squares(4 + l * 2, KC - 2)
                sum_squares(4 + l * 2, KC - 1)
                for f in range(2):
                    n = FFN_AT + f * FFN_PER
                    if f == 0:
                        first_products((bank(4), bank(6)), (n, n + 1), hbase + KC, (h1_ready, h3_ready), l)
                    for b in range(1 if f == 0 else 0, HALF):
                        k = HALF * f + b
                        for w, ready in ((0, h1_ready), (1, h3_ready)):
                            split_wait(n + 2 * b + w, l)
                            if k >= 2 and w == 0:
                                pe.wait_ge(f_ready, k - 1 + l * FFC)
                            at0 = bank(4 + 2 * w + k % 2)
                            product(at0, n + 2 * b + w, hs, range(KC), True, True).then_inc(ready, 1)
                    for c in range(KC):
                        if c >= 4:
                            pe.wait_ge(x_ready, NX1 + KC * (f + 1) + c - 3 + l * OUTS2)
                        elif c == 0 and f == 1:
                            pe.wait_ge(x_ready, NX1 + 2 * KC + l * OUTS2)
                        for j, (a, e) in enumerate(W2_CUT):
                            i = n + 2 * HALF + len(W2_CUT) * c + j
                            split_wait(i, l)
                            if c == 0:
                                pe.wait_ge(f_ready, HALF * f + e + l * FFC)
                            ins = product(bank(c % 4), i, acts, range(a, e), j == 0, j == len(W2_CUT) - 1)
                            ins.then_inc(w2_used if j < len(W2_CUT) - 1 else out_ready, 1)
                        if f == 1 and c >= 2:
                            sum_squares(5 + l * 2, c - 2)
                sum_squares(5 + l * 2, KC - 2)
                sum_squares(5 + l * 2, KC - 1)


_hi = float(np.float32(np.round(2 * np.pi * 128) / 128))
_mid = float(np.float32(np.round((2 * np.pi - _hi) * 2.0 ** 19) / 2.0 ** 19))
TWO_PI = (_hi, _mid, float(np.float32(2 * np.pi - _hi - _mid)))


def _tables():
    t = np.arange(SEQ)
    d = np.arange(P) % HD
    freq = 10000.0 ** (-np.arange(16) / 16.0)
    ang = np.concatenate([(t // GRID)[:, None] * freq, (t % GRID)[:, None] * freq], axis=1).T
    rope = np.stack([np.cos(ang)[d % 32], np.where(d < 32, -1.0, 1.0)[:, None] * np.sin(ang)[d % 32]], axis=1)
    i = np.arange(P)
    mats = np.stack([np.eye(P), i[:, None] == (i ^ 32)[None, :], -1.0 * (i[:, None] == (ROWS - 1 - i % ROWS)[None, :] * NBC + (NBC - 1 - i // ROWS)[None, :]),
                     i[:, None] // HD == i[None, :] // HD, np.ones((P, P))], axis=1)
    bmask = np.zeros((P, 4, CTX))
    cl, j = np.arange(P) // ROWS, np.arange(BAND)
    for v, lo in enumerate((np.maximum(cl - 8, 0), cl, np.minimum(cl + 8, 16))):
        seen = (j[None, :] >= lo[:, None]) & (j[None, :] < lo[:, None] + NBC)
        bmask[:, v + 1, :] = np.repeat(np.where(seen, 0.0, NOT_SEEN), ROWS, axis=1)
    cmask = np.zeros((P, 641))
    cmask[:, 0:P] = np.where(i[None, :] >= i[:, None], 0.0, NOT_SEEN)
    cmask[:, 512:640] = np.where(i[None, :] <= i[:, None], 0.0, NOT_SEEN)
    fmask = np.where(i[None, :] <= i[:, None], 0.0, NOT_SEEN)
    lg = np.log(1.0 - 2.0 ** (-5.0 - np.arange(4)))
    diff = np.arange(SEQ)[None, :] - i[:, None]
    decay = np.stack([np.where(diff >= 0, np.exp(g * np.maximum(diff, 0)), 0.0) for g in lg], axis=1)
    counts = np.zeros((P, 2, SEQ))
    for g, w in enumerate((2, 4, 8, 16)):
        counts[HD * (g % 2):HD * (g % 2) + HD, g // 2] = 1.0 / np.minimum(t + 1, w)
    of_head = (np.arange(10)[:, None, None] == 2 * np.arange(5)[None, :, None] + (i // HD)[None, None, :]) * 1.0
    inv = 10000.0 ** (-(d % 32) / 32.0)
    sign = np.where(d < 32, -1.0, 1.0)
    f = lambda a: np.ascontiguousarray(a, dtype=np.float32)
    return {k: f(v) for k, v in dict(rope=rope, mats=mats, bmask=bmask, cmask=cmask, fmask=fmask, decay=decay,
                                     counts=counts, of_head=of_head, head_of=of_head.transpose(2, 1, 0), inv=inv, sign=sign).items()}


def _features(v):
    return np.ascontiguousarray(v.reshape(-1, P).T)


def _panels(w, chunks, cols):
    L, _, n = w.shape
    return np.ascontiguousarray(
        w.reshape(L, chunks, P, n // cols, cols).transpose(0, 3, 2, 1, 4)).reshape(L, n // cols, P, chunks * cols)


def _layout(a):
    t = _tables()
    dup = lambda v: np.concatenate([v, v], axis=1).T
    c = np.stack([_features(a["c"]), _features(a["c_ctx"])], axis=2).reshape(P, 2 * KC)
    prm = np.concatenate([c, _features(a["c_2"]), _features(a["ada_b"]), _features(a["norm_w"]), _features(a["final_norm_w"]),
                          dup(a["q_norm_a"]), dup(a["k_norm_a"]), _features(a["final_g_2"]),
                          t["inv"][:, None], t["sign"][:, None]], axis=1)
    lyr = []
    for l in range(DEPTH):
        fb = np.zeros((P, 1), a["fox_fb_2"].dtype)
        fb[0:4, 0] = a["fox_fb_2"][l]
        conv_w = a["conv_w_2"][l].reshape(CONV, 2, P).transpose(2, 1, 0).reshape(P, 2 * CONV)
        lyr.append(np.concatenate([_features(a[k][l]) for k in (
            "ada_b_2", "norm_mix_g_2", "norm_ffn_g_2", "pool_scale_2", "ret_gn_g_2", "conv_b_2", "conv_ln_g_2", "conv_ln_b_2")]
            + [conv_w, fb], axis=1))
    w2in = a["w_in_2"]
    at = dict(fq=0, fk=256, fv=512, pu=772, rq=1028, rk=1284, rv=1540, rg=1796, ca=2052, cg=2308)
    order = ("ca", "cg", "rq", "rk", "rv", "rg", "pu", "fq", "fk", "fv")
    out1 = _panels(a["w_out"], MIXC, P).reshape(DEPTH, KC, P, 2, MIXC // 2 * P).transpose(0, 1, 3, 2, 4).reshape(
        DEPTH, 2 * KC, P, MIXC // 2 * P)
    forget = np.zeros((DEPTH, DM, P), w2in.dtype)
    forget[:, :, 0:4] = w2in[:, :, 768:772]
    in2 = np.concatenate([forget] + [w2in[:, :, at[k]:at[k] + 256] for k in order], axis=2)
    w2 = a["ffn_w2_2"].reshape(DEPTH, 2, HALF * P, DM)
    poolw = np.zeros((DEPTH, P, 2, P), a["pool_w_2"].dtype)
    for g in range(4):
        r = slice(HD * (g % 2), HD * (g % 2) + HD)
        poolw[:, r, g // 2, r] = a["pool_w_2"][:, g]
    rpb = np.zeros((DEPTH, HEADS, 15, 64), a["rpb_b"].dtype)
    rpb[:, :, :, 16:47] = a["rpb_b"]
    feat = lambda x: x[0].T.reshape(KC, P, -1).transpose(1, 0, 2)
    arrays = dict(
        prm=prm, lyr=np.stack(lyr, axis=1), x=feat(a["x"]), ctx=feat(a["ctx"]), rpb=rpb,
        sinks=a["sink_c"].reshape(1, -1), pos=a["positions_2"].reshape(1, SEQ),
        ada1=_panels(a["ada_w"], KC, PAN), in1=_panels(a["w_in"], KC, P), out1=out1,
        ada2=_panels(a["ada_w_2"], KC, PAN), in2=_panels(in2, KC, P), out2=_panels(a["w_out_2"], KC, P),
        w1=_panels(a["ffn_w1_2"], KC, P), w3=_panels(a["ffn_w3_2"], KC, P),
        w2=np.stack([_panels(w2[:, f], HALF, P) for f in range(2)], axis=1),
        poolw=poolw.reshape(DEPTH, P, 2 * P),
        **{k: t[k] for k in ("rope", "mats", "bmask", "cmask", "fmask", "decay", "counts", "head_of", "of_head")})
    return {k: np.ascontiguousarray(v) for k, v in arrays.items()}


def kernel(**inputs):
    import concourse.bacc as bacc
    from concourse.bass_utils import run_bass_kernel_spmd

    arrays = {f"in_{k}": v for k, v in _layout({k: np.asarray(v) for k, v in inputs.items()}).items()}
    nc = bacc.Bacc("TRN2", target_bir_lowering=False, num_devices=1)
    dram = {k[3:]: nc.dram_tensor(k, v.shape, mybir.dt.from_np(v.dtype), kind="ExternalInput").ap() for k, v in arrays.items()}
    out = nc.dram_tensor("out_features", (P, KC, SEQ), F32, kind="ExternalOutput").ap()
    kept = nc.dram_tensor("kept_stream", (P, KC, SEQ), F32).ap()
    two_dit_blocks(nc, dram, kept, out)
    got = run_bass_kernel_spmd(nc, [arrays], core_ids=[0]).results[0]["out_features"]
    return np.ascontiguousarray(got.transpose(2, 1, 0).reshape(1, SEQ, DM))
```
